# Optimizing a Trainium2 kernel written in Bass

```python
import math
import jax
import jax.numpy as jnp
from jax import lax
import numpy as np

D_MODEL = 1024
BATCH = 1
SEQ = 256
DEPTH = 1
DEC_BATCH = 1
DEC_SEQ = 1024
PAST_LEN = 128

GRID_W = 64
ATT_HEADS = 8
ATT_HEAD_DIM = 64
ATT_WIDTH = ATT_HEADS * ATT_HEAD_DIM
WIN_H_MAX = 8
WIN_W = 16
SSD_HEADS = 8
SSD_HEAD_DIM = 64
SSD_WIDTH = SSD_HEADS * SSD_HEAD_DIM
SSD_GROUPS = 2
SSD_STATE = 128
SSD_CONV = 5
SSD_CHUNK = 128
CONV_CH = SSD_WIDTH + 2 * SSD_GROUPS * SSD_STATE
MIX_WIDTH = ATT_WIDTH + SSD_WIDTH
IN_COLS = 3 * ATT_WIDTH + SSD_WIDTH + CONV_CH + SSD_HEADS
PEER_HEADS = 8
PEER_N_KEYS = 128
PEER_N_EXPERTS = PEER_N_KEYS * PEER_N_KEYS
PEER_D_KEY = 128
PEER_TOPK = 16
PEER_BLOCK = 128
EPS = 1e-6

kernel_name = 'hymba_natten_ssd_peer_encoder'

def rms_norm(x, w):
    xf = x.astype(jnp.float32)
    y = xf * lax.rsqrt(jnp.mean(xf * xf, axis=-1, keepdims=True) + EPS)
    return (y * w.astype(jnp.float32)).astype(x.dtype)

def neighbourhood_attention(q, k, v, rpb):
    b, l, h, dh = q.shape
    rows = l // GRID_W
    kh = min(WIN_H_MAX, rows)
    r = jnp.arange(rows)
    row_start = jnp.clip(r - kh // 2, 0, rows - kh)
    key_rows = row_start[:, None] + jnp.arange(kh)[None, :]
    c = jnp.arange(GRID_W)
    col_start = jnp.clip(c - WIN_W // 2, 0, GRID_W - WIN_W)
    col_in = (c[None, :] >= col_start[:, None]) & (c[None, :] < col_start[:, None] + WIN_W)
    qg = q.reshape(b, rows, GRID_W, h, dh)
    kg = k.reshape(b, rows, GRID_W, h, dh)[:, key_rows]
    vg = v.reshape(b, rows, GRID_W, h, dh)[:, key_rows]
    scores = jnp.einsum('brqhd,brjkhd->bhrqjk', qg, kg,
                        preferred_element_type=jnp.float32) * (dh ** -0.5)
    dr = key_rows - r[:, None] + (WIN_H_MAX - 1)
    dc = jnp.clip(c[None, :] - c[:, None], -(WIN_W - 1), WIN_W - 1) + (WIN_W - 1)
    bias = rpb.astype(jnp.float32)[:, dr[:, None, :, None], dc[None, :, None, :]]
    logits = jnp.where(col_in[:, None, :], scores + bias[None], -jnp.inf)
    probs = jax.nn.softmax(logits.reshape(b, h, rows, GRID_W, kh * GRID_W), axis=-1).reshape(logits.shape)
    out = jnp.einsum('bhrqjk,brjkhd->brqhd', probs.astype(v.dtype), vg)
    return out.reshape(b, l, h * dh)

def centred_depthwise_conv(x, w, bias):
    ch = x.shape[-1]
    y = lax.conv_general_dilated(
        x.astype(jnp.float32), w.astype(jnp.float32)[:, None, :],
        window_strides=(1,), padding=[(SSD_CONV // 2, SSD_CONV // 2)],
        dimension_numbers=('NWC', 'WIO', 'NWC'), feature_group_count=ch)
    return y + bias.astype(jnp.float32)

def segsum(x):
    t = x.shape[-1]
    xr = jnp.broadcast_to(x[..., None], x.shape + (t,))
    xr = jnp.where(jnp.tril(jnp.ones((t, t), dtype=bool), -1), xr, 0.0)
    cs = jnp.cumsum(xr, axis=-2)
    return jnp.where(jnp.tril(jnp.ones((t, t), dtype=bool), 0), cs, -jnp.inf)

def ssd_chunked(x, dt, a, bm, cm):
    b, l, h, p = x.shape
    g, n = bm.shape[-2:]
    r = h // g
    nc = l // SSD_CHUNK
    q = SSD_CHUNK
    dtf = dt.astype(jnp.float32)
    xdt = (x.astype(jnp.float32) * dtf[..., None]).reshape(b, nc, q, g, r, p)
    adt = (dtf * a.astype(jnp.float32)).reshape(b, nc, q, g, r).transpose(0, 3, 4, 1, 2)
    bm = bm.astype(jnp.float32).reshape(b, nc, q, g, n)
    cm = cm.astype(jnp.float32).reshape(b, nc, q, g, n)
    a_cs = jnp.cumsum(adt, axis=-1)
    decay_in = jnp.exp(segsum(adt))
    cb = jnp.einsum('bclgn,bcsgn->bgcls', cm, bm)
    y_diag = jnp.einsum('bgcls,bgrcls,bcsgrp->bclgrp', cb, decay_in, xdt)
    decay_st = jnp.exp(a_cs[..., -1:] - a_cs)
    states = jnp.einsum('bcsgn,bgrcs,bcsgrp->bcgrpn', bm, decay_st, xdt)
    states = jnp.concatenate([jnp.zeros_like(states[:, :1]), states], axis=1)
    chunk_tot = jnp.pad(a_cs[..., -1], ((0, 0), (0, 0), (0, 0), (1, 0)))
    decay_ch = jnp.exp(segsum(chunk_tot))
    states = jnp.einsum('bgrzc,bcgrpn->bzgrpn', decay_ch, states)[:, :-1]
    y_off = jnp.einsum('bclgn,bcgrpn,bgrcl->bclgrp', cm, states, jnp.exp(a_cs))
    return (y_diag + y_off).reshape(b, l, h, p)

def ssd_bidirectional(xbc_raw, z, dt_raw, conv_w, conv_b, dt_bias, a_log, d_skip, ssd_norm_w):
    b, l, _ = xbc_raw.shape
    xbc = jax.nn.silu(centred_depthwise_conv(xbc_raw, conv_w, conv_b))
    xs, bm, cm = jnp.split(xbc, [SSD_WIDTH, SSD_WIDTH + SSD_GROUPS * SSD_STATE], axis=-1)
    xs = xs.reshape(b, l, SSD_HEADS, SSD_HEAD_DIM)
    bm = bm.reshape(b, l, SSD_GROUPS, SSD_STATE)
    cm = cm.reshape(b, l, SSD_GROUPS, SSD_STATE)
    dt_raw = dt_raw.astype(jnp.float32)
    y = xs * d_skip.astype(jnp.float32)[:, None]
    dt_f = jax.nn.softplus(dt_raw + dt_bias[0].astype(jnp.float32))
    y = y + ssd_chunked(xs, dt_f, -jnp.exp(a_log[0].astype(jnp.float32)), bm, cm)
    dt_b = jax.nn.softplus(dt_raw[:, ::-1] + dt_bias[1].astype(jnp.float32))
    y = y + ssd_chunked(xs[:, ::-1], dt_b, -jnp.exp(a_log[1].astype(jnp.float32)),
                        bm[:, ::-1], cm[:, ::-1])[:, ::-1]
    y = y.reshape(b, l, SSD_WIDTH) * jax.nn.silu(z.astype(jnp.float32))
    return rms_norm(y, ssd_norm_w)

def parallel_mixer(h, w_in, rpb, conv_w, conv_b, dt_bias, a_log, d_skip, ssd_norm_w, w_out):
    b, l, _ = h.shape
    proj = h @ w_in
    splits = [ATT_WIDTH, 2 * ATT_WIDTH, 3 * ATT_WIDTH,
              3 * ATT_WIDTH + SSD_WIDTH, 3 * ATT_WIDTH + SSD_WIDTH + CONV_CH]
    q, k, v, z, xbc, dt_raw = jnp.split(proj, splits, axis=-1)
    shp = (b, l, ATT_HEADS, ATT_HEAD_DIM)
    att = neighbourhood_attention(q.reshape(shp), k.reshape(shp), v.reshape(shp), rpb)
    ssd = ssd_bidirectional(xbc, z, dt_raw, conv_w, conv_b, dt_bias, a_log, d_skip, ssd_norm_w)
    mixed = jnp.concatenate([att.astype(jnp.float32), ssd.astype(jnp.float32)], axis=-1)
    return mixed @ w_out

def peer_ffn(h, w_query, sub_keys, expert_u, expert_v):
    b, l, d = h.shape
    blocks = h.reshape(-1, PEER_BLOCK, d)

    def retrieve(xb):
        t = xb.shape[0]
        qry = (xb @ w_query).reshape(t, PEER_HEADS, 2, PEER_D_KEY)
        s = jnp.einsum('thzk,hznk->thzn', qry, sub_keys, preferred_element_type=jnp.float32)
        sv, si = lax.top_k(s, PEER_TOPK)
        cand = sv[:, :, 0, :, None] + sv[:, :, 1, None, :]
        cand_idx = si[:, :, 0, :, None] * PEER_N_KEYS + si[:, :, 1, None, :]
        top_s, top_pos = lax.top_k(cand.reshape(t, PEER_HEADS, PEER_TOPK * PEER_TOPK), PEER_TOPK)
        idx = jnp.take_along_axis(cand_idx.reshape(t, PEER_HEADS, PEER_TOPK * PEER_TOPK), top_pos, axis=-1)
        gate = jax.nn.softmax(top_s, axis=-1)
        u = expert_u[idx]
        v = expert_v[idx]
        act = jax.nn.gelu(jnp.einsum('td,thkd->thk', xb, u, preferred_element_type=jnp.float32),
                          approximate=False) * gate
        return jnp.einsum('thk,thkd->td', act.astype(v.dtype), v)

    return lax.map(retrieve, blocks).reshape(b, l, d)

def trunk(x, norm_mix_w, w_in, rpb, conv_w, conv_b, dt_bias, a_log, d_skip, ssd_norm_w, w_out,
          norm_ffn_w, w_query, sub_keys, expert_u, expert_v, norm_final_w):
    for i in range(DEPTH):
        hm = rms_norm(x, norm_mix_w[i])
        x = x + parallel_mixer(hm, w_in[i], rpb[i], conv_w[i], conv_b[i], dt_bias[i], a_log[i],
                               d_skip[i], ssd_norm_w[i], w_out[i])
        hf = rms_norm(x, norm_ffn_w[i])
        x = x + peer_ffn(hf, w_query[i], sub_keys[i], expert_u[i], expert_v[i])
    return rms_norm(x, norm_final_w)

def setup_inputs(seed: int = 0) -> dict:
    key = jax.random.key(seed)
    ks = jax.random.split(key, 20)
    f32 = jnp.float32

    def nrm(k, shape, scale):
        return jax.random.normal(k, shape, f32) * scale

    u = jax.random.uniform(ks[7], (DEPTH, 2, SSD_HEADS), f32)
    dt0 = jnp.exp(u * (math.log(0.1) - math.log(0.001)) + math.log(0.001))
    dt_bias = dt0 + jnp.log(-jnp.expm1(-dt0))
    a_log = jnp.log(jax.random.uniform(ks[8], (DEPTH, 2, SSD_HEADS), f32, 1.0, 16.0))
    return {
        'x_prompt': nrm(ks[0], (BATCH, SEQ, D_MODEL), 1.0),
        'x_sample': nrm(ks[1], (DEC_BATCH, DEC_SEQ, D_MODEL), 1.0),
        'norm_mix_w': 1.0 + nrm(ks[2], (DEPTH, D_MODEL), 0.01),
        'w_in': nrm(ks[3], (DEPTH, D_MODEL, IN_COLS), D_MODEL ** -0.5),
        'rpb': nrm(ks[4], (DEPTH, ATT_HEADS, 2 * WIN_H_MAX - 1, 2 * WIN_W - 1), 0.02),
        'conv_w': nrm(ks[5], (DEPTH, SSD_CONV, CONV_CH), SSD_CONV ** -0.5),
        'conv_b': nrm(ks[6], (DEPTH, CONV_CH), 0.01),
        'dt_bias': dt_bias,
        'a_log': a_log,
        'd_skip': 1.0 + nrm(ks[9], (DEPTH, SSD_HEADS), 0.1),
        'ssd_norm_w': 1.0 + nrm(ks[10], (DEPTH, SSD_WIDTH), 0.01),
        'w_out': nrm(ks[11], (DEPTH, MIX_WIDTH, D_MODEL), MIX_WIDTH ** -0.5),
        'norm_ffn_w': 1.0 + nrm(ks[12], (DEPTH, D_MODEL), 0.01),
        'w_query': nrm(ks[13], (DEPTH, D_MODEL, PEER_HEADS * 2 * PEER_D_KEY), D_MODEL ** -0.5),
        'sub_keys': nrm(ks[14], (DEPTH, PEER_HEADS, 2, PEER_N_KEYS, PEER_D_KEY), PEER_D_KEY ** -0.5),
        'expert_u': nrm(ks[15], (DEPTH, PEER_N_EXPERTS, D_MODEL), D_MODEL ** -0.5),
        'expert_v': nrm(ks[16], (DEPTH, PEER_N_EXPERTS, D_MODEL), PEER_HEADS ** -0.5),
        'norm_final_w': 1.0 + nrm(ks[17], (D_MODEL,), 0.01),
    }

def reference(x_prompt, x_sample, norm_mix_w, w_in, rpb, conv_w, conv_b, dt_bias, a_log, d_skip,
              ssd_norm_w, w_out, norm_ffn_w, w_query, sub_keys, expert_u, expert_v, norm_final_w):
    y_prompt = trunk(x_prompt, norm_mix_w, w_in, rpb, conv_w, conv_b, dt_bias, a_log, d_skip,
                     ssd_norm_w, w_out, norm_ffn_w, w_query, sub_keys, expert_u, expert_v, norm_final_w)
    y_sample = trunk(x_sample, norm_mix_w, w_in, rpb, conv_w, conv_b, dt_bias, a_log, d_skip,
                     ssd_norm_w, w_out, norm_ffn_w, w_query, sub_keys, expert_u, expert_v, norm_final_w)
    return (y_prompt, y_sample)


_drawn_inputs = setup_inputs


def setup_inputs(seed=0):
    import zlib

    import numpy as np

    out = dict(_drawn_inputs(seed))
    spreads = {}
    factors = {'norm_mix_w': 3.383,
     'rpb': 7.078,
     'conv_b': 13.0,
     'ssd_norm_w': 18.76,
     'norm_ffn_w': 18.493,
     'norm_final_w': 190.623,
     'd_skip': 31.294}
    for name, (base, spread) in spreads.items():
        noise = np.random.default_rng([zlib.crc32(name.encode()), seed]).standard_normal(out[name].shape)
        drawn = base * np.exp(spread * noise) if base else spread * noise
        out[name] = jnp.asarray(drawn.astype(out[name].dtype))
    for name, factor in factors.items():
        out[name] = (out[name] * factor).astype(out[name].dtype)
    return out
```

```python
from contextlib import ExitStack

import concourse.bass as bass
from concourse import mybir

ALU = mybir.AluOpType
ACT = mybir.ActivationFunctionType
AX = mybir.AxisListType
F32 = mybir.dt.float32
F32R = mybir.dt.float32r
BF16 = mybir.dt.bfloat16
U32 = mybir.dt.uint32

P = 128
D = 1024
KD = D // P
SEQ_P, SEQ_S = 256, 1024
T = SEQ_P + SEQ_S
NT = T // P
SEGS = [(0, 512), (512, 512), (1024, 256)]
EPS = 1e-6
GRID_W = 64
HEADS = 8
HD = 64
SSD_W = HEADS * HD
NB_IN = 25
BLK_Z, BLK_XBC, BLK_DT = 12, 16, 24
CONV_TAPS = 5
PAD_T = T + 6
CONV_T = T + 2
BIAS_GEN, BIAS_INT = 16 * GRID_W, 9 * GRID_W
TOPK = 16
NKEY = 128
LOWEST = -3.0e38
HALF = T // 2
NTH = HALF // P
TB = 64
PRODUCTS = [(0, 0), (1, 0), (0, 1)]


class Steps:

    def __init__(self, eng, sem):
        self.eng, self.sem, self.base, self.k, self.outer = eng, sem, 0, 0, []

    def enter(self, i, per):
        self.outer.append((self.base, self.k, per))
        self.base, self.k = i * per + self.base + self.k, 0

    def leave(self, n):
        base, k, per = self.outer.pop()
        assert self.k == per, (self.k, per)
        self.base, self.k = base, k + n * per

    def add(self, ins):
        self.k += 1
        ins.then_inc(self.sem, 1)

    def wait(self):
        self.eng.wait_ge(self.sem, self.base + self.k)

    def link(self, ins):
        self.add(ins)
        self.wait()


def scope(nc, ctx):
    sems = []

    def sb(name, shape, dt=F32):
        return ctx.enter_context(nc.sbuf_tensor(name, shape, dt))

    def ps(name, shape, dt=F32):
        return ctx.enter_context(nc.psum_tensor(name, shape, dt))

    def sem(name):
        sems.append(nc.alloc_semaphore(name))
        return sems[-1]

    def clear():
        if sems:
            nc.clear_and_free_semaphores(sems)
            nc.all_engine_barrier()

    ctx.callback(clear)
    return sb, ps, sem


def pair_of(sem, name):
    return [sem(name + "0"), sem(name + "1")]


def rounds(eng, n, step):
    with eng.Fori(0, n // 2) as i:
        for u in range(2):
            step(i, u)
    if n % 2:
        step(n // 2, 0)


def rows_bcast(dram, n, parts=P):
    return bass.AP(tensor=dram.tensor, offset=dram.offset, ap=[[0, parts], [1, n]])


def one(ap, r):
    return ap[bass.ds(r, 1)].rearrange("o p c -> p (o c)")


def norm_inputs(nc, x, w_row, ident, hT):
    with ExitStack() as ctx:
        sb, ps, sem = scope(nc, ctx)
        xall = sb("n1_x", [P, NT, D])
        junk = sb("n1_junk", [P, D])
        wrow = sb("n1_w", [P, D])
        idm = sb("n1_ident", [P, P])
        ssq = sb("n1_ssq", [P, NT])
        rstd = sb("n1_rstd", [P, NT])
        xs = sb("n1_xs", [P, 2, D])
        xT = ps("n1_xT", [P, 2, D])
        consts_in, x_in = sem("n1_consts_in"), [sem(f"n1_x_in{t}") for t in range(NT)]
        squared, var_ready, root_ready = sem("n1_squared"), sem("n1_var"), sem("n1_root")
        dve_steps, scaled, turned = sem("n1_dve"), sem("n1_scaled"), sem("n1_turned")
        hi_done, lo_done = sem("n1_hi"), sem("n1_lo")
        block = ctx.enter_context(nc.Block())

        @block.sync
        def _(sp):
            for t in range(NT):
                sp.dma_start(xall[:, t, :], x[t * P:(t + 1) * P, :]).then_inc(x_in[t], 16)
            sp.dma_start(wrow[:], rows_bcast(w_row, D)).then_inc(consts_in, 16)
            sp.dma_start(idm[:], ident).then_inc(consts_in, 16)

        @block.scalar
        def _(act):
            for t in range(NT):
                act.wait_ge(x_in[t], 16)
                if t:
                    act.wait_ge(squared, t)
                act.activation(junk[:], xall[:, t, :], ACT.Square, accum_out=ssq[:, t:t + 1]).then_inc(squared, 1)
            act.wait_ge(var_ready, 1)
            act.activation(rstd[:], ssq[:], ACT.Sqrt).then_inc(root_ready, 1)
            with act.Fori(0, NT // 2) as i:
                for u in range(2):
                    act.wait_ge(turned, i * 2 + (u + 1))
                    act.activation(hT[0][:, :, bass.ds(i * (2 * P) + u * P, P)],
                                   xT[:, u].rearrange("p (k t) -> p k t", k=KD), ACT.Copy).then_inc(hi_done, 1)

        @block.vector
        def _(dve):
            own = Steps(dve, dve_steps)
            dve.wait_ge(squared, NT)
            dve.tensor_scalar(ssq[:], ssq[:], 1.0 / D, EPS, ALU.mult, ALU.add).then_inc(var_ready, 1)
            dve.wait_ge(root_ready, 1)
            own.link(dve.reciprocal(rstd[:], rstd[:]))
            dve.wait_ge(consts_in, 32)
            with dve.Fori(0, NT // 2) as i:
                for u in range(2):
                    dve.scalar_tensor_tensor(xs[:, u], one_of(xall, i * 2 + u),
                                             rstd[:, bass.ds(i * 2 + u, 1)], wrow[:],
                                             ALU.mult, ALU.mult).then_inc(scaled, 1)
                for u in range(2):
                    dve.wait_ge(hi_done, i * 2 + (u + 1))
                    tok = bass.ds(i * (2 * P) + u * P, P)
                    dve.tensor_tensor(hT[1][:, :, tok], xT[:, u].rearrange("p (k t) -> p k t", k=KD),
                                      hT[0][:, :, tok].bitcast(F32), ALU.subtract).then_inc(lo_done, 1)

        @block.tensor
        def _(pe):
            pe.sem_inc(lo_done, 2)
            pe.wait_ge(consts_in, 32)
            with pe.Fori(0, NT // 2) as i:
                for u in range(2):
                    pe.wait_ge(scaled, i * 2 + (u + 1))
                    pe.wait_ge(lo_done, i * 2 + (u + 1))
                    for k in range(KD):
                        mm = pe.transpose(xT[:, u, k * P:(k + 1) * P], xs[:, u, k * P:(k + 1) * P], idm[:])
                    mm.then_inc(turned, 1)


def one_of(ap, r):
    return ap[:, bass.ds(r, 1), :].rearrange("p o d -> p (o d)")


def split(dve, own, hi, lo, raw):
    own.link(dve.tensor_copy(hi, raw))
    return dve.tensor_tensor(lo, raw, hi.bitcast(F32), ALU.subtract)


def project_in(nc, w_blocks, hT, projT):
    with ExitStack() as ctx:
        sb, ps, sem = scope(nc, ctx)
        wraw = sb("pi_wraw", [P, 2, KD * P])
        w = [sb(f"pi_w_{part}", [P, 2, KD * P], F32R) for part in ("hi", "lo")]
        res = sb("pi_out", [P, 2, T])
        acc = ps("pi_acc", [P, 2, 3 * 512])
        w_in = pair_of(sem, "pi_w_in")
        split_done, dve_steps = sem("pi_split"), sem("pi_dve")
        summed, copied = sem("pi_summed"), sem("pi_copied")
        stored = pair_of(sem, "pi_stored")
        block = ctx.enter_context(nc.Block())

        @block.sync
        def _(sp):
            def load(r, u):
                sp.wait_ge(split_done, r * 2 + (u + 1))
                sp.dma_start(wraw[:, u], one(w_blocks, r * 2 + u)).then_inc(w_in[u], 16)
            rounds(sp, NB_IN, load)

        @block.vector
        def _(dve):
            own = Steps(dve, dve_steps)
            dve.sem_inc(split_done, 2)

            def parts(r, u):
                dve.wait_ge(w_in[u], r * 16 + 16)
                dve.wait_ge(summed, r * 2 + (u + 1))
                split(dve, own, w[0][:, u], w[1][:, u], wraw[:, u]).then_inc(split_done, 1)

            with dve.Fori(0, NB_IN // 2) as i:
                own.enter(i, 2)
                for u in range(2):
                    parts(i, u)
            own.leave(NB_IN // 2)
            parts(NB_IN // 2, 0)

        @block.tensor
        def _(pe):
            pe.sem_inc(summed, 2)

            def block_products(r, u):
                pe.wait_ge(split_done, r * 2 + (u + 3))
                pe.wait_ge(copied, r * 2 + (u + 1))
                for k in range(KD):
                    for n, (a, b) in enumerate(PRODUCTS):
                        for t0, tn in SEGS:
                            mm = pe.matmul(acc[:, u, t0:t0 + tn], w[a][:, u, k * P:(k + 1) * P],
                                           hT[b][:, k, t0:t0 + tn], start=(k + n == 0),
                                           stop=(k == KD - 1 and n == 2))
                mm.then_inc(summed, 1)
            rounds(pe, NB_IN, block_products)

        @block.scalar
        def _(act):
            act.sem_inc(copied, 2)
            act.sem_inc(stored[0], 16)
            act.sem_inc(stored[1], 16)

            def copy_out(r, u):
                act.wait_ge(summed, r * 2 + (u + 3))
                act.wait_ge(stored[u], r * 16 + 16)
                act.activation(res[:, u], acc[:, u, 0:T], ACT.Copy).then_inc(copied, 1)
                act.wait_ge(copied, r * 2 + (u + 3))
                act.dma_start(one(projT, r * 2 + u), res[:, u]).then_inc(stored[u], 16)
            rounds(act, NB_IN, copy_out)
            act.wait_ge(stored[0], 16 * (1 + (NB_IN + 1) // 2))
            act.wait_ge(stored[1], 16 * (1 + NB_IN // 2))


def conv_silu(nc, projT, conv_w, conv_b, xbcT):
    NB = 8
    with ExitStack() as ctx:
        sb, ps, sem = scope(nc, ctx)
        taps = sb("cv_taps", [P, NB * CONV_TAPS])
        bias = sb("cv_bias", [P, NB])
        xp = sb("cv_x", [P, 2, PAD_T])
        y = sb("cv_y", [P, 2, CONV_T])
        z = sb("cv_z", [P, 2, CONV_T])
        consts_in, pads = sem("cv_consts_in"), sem("cv_pads")
        x_in, stored = pair_of(sem, "cv_x_in"), pair_of(sem, "cv_stored")
        summed, squashed, dve_steps = sem("cv_summed"), sem("cv_silu"), sem("cv_dve")
        block = ctx.enter_context(nc.Block())

        @block.sync
        def _(sp):
            sp.dma_start(taps[:], conv_w).then_inc(consts_in, 16)
            sp.dma_start(bias[:], conv_b).then_inc(consts_in, 16)
            sp.wait_ge(pads, 1)
            with sp.Fori(0, NB // 2) as i:
                for u in range(2):
                    sp.wait_ge(summed, i * 2 + (u + 1))
                    src = one(projT, i * 2 + (BLK_XBC + u))
                    sp.dma_start(xp[:, u, 2:2 + SEQ_P], src[:, 0:SEQ_P]).then_inc(x_in[u], 16)
                    sp.dma_start(xp[:, u, 4 + SEQ_P:4 + T], src[:, SEQ_P:T]).then_inc(x_in[u], 16)

        @block.vector
        def _(dve):
            own = Steps(dve, dve_steps)
            dve.sem_inc(summed, 2)
            dve.memset(xp[:], 0.0).then_inc(pads, 1)
            dve.wait_ge(consts_in, 32)
            with dve.Fori(0, NB // 2) as i:
                own.enter(i, 2 * (CONV_TAPS - 1))
                for u in range(2):
                    dve.wait_ge(x_in[u], i * 32 + 32)
                    dve.wait_ge(squashed, i * 2 + (u + 1))
                    tap = [taps[:, bass.ds(i * (2 * CONV_TAPS) + (u * CONV_TAPS + j), 1)] for j in range(CONV_TAPS)]
                    own.link(dve.tensor_scalar(y[:, u], xp[:, u, 0:CONV_T], tap[0], None, ALU.mult))
                    for j in range(1, CONV_TAPS):
                        ins = dve.scalar_tensor_tensor(y[:, u], xp[:, u, j:j + CONV_T], tap[j], y[:, u],
                                                       ALU.mult, ALU.add)
                        if j < CONV_TAPS - 1:
                            own.link(ins)
                        else:
                            ins.then_inc(summed, 1)

        @block.scalar
        def _(act):
            act.sem_inc(squashed, 2)
            act.sem_inc(stored[0], 32)
            act.sem_inc(stored[1], 32)
            act.wait_ge(consts_in, 32)
            with act.Fori(0, NB // 2) as i:
                for u in range(2):
                    act.wait_ge(summed, i * 2 + (u + 3))
                    act.wait_ge(stored[u], i * 32 + 32)
                    act.activation(z[:, u], y[:, u], ACT.Silu, bias=bias[:, bass.ds(i * 2 + u, 1)]
                                   ).then_inc(squashed, 1)
                    act.wait_ge(squashed, i * 2 + (u + 3))
                    dst = one(xbcT, i * 2 + u)
                    act.dma_start(dst[:, 0:SEQ_P], z[:, u, 0:SEQ_P]).then_inc(stored[u], 16)
                    act.dma_start(dst[:, SEQ_P:T], z[:, u, SEQ_P + 2:CONV_T]).then_inc(stored[u], 16)
            for u in range(2):
                act.wait_ge(stored[u], 32 * (1 + NB // 2))


def attention_tiles():
    tiles = [(0, 0, 4 * GRID_W, 7 * GRID_W), (P, 0, 4 * GRID_W, 5 * GRID_W)]
    rows = SEQ_S // GRID_W
    for r in range(0, rows, 2):
        first = min(max(r - 4, 0), rows - 8)
        last = min(max(r + 1 - 4, 0), rows - 8) + 8
        col = BIAS_GEN if last - first == 9 else (first - r + 7) * GRID_W
        tiles.append((SEQ_P + r * GRID_W, SEQ_P + first * GRID_W, (last - first) * GRID_W, col))
    return tiles


def attention(nc, projT, bias_tab, ident, mixT):
    tiles = attention_tiles()
    NTI = len(tiles)
    KMAX = 640
    heads_in = projT.rearrange("b (h p) t -> (b h) p t", h=2)
    heads_out = mixT.rearrange("b (h p) t -> (b h) p t", h=2)
    with ExitStack() as ctx:
        sb, ps, sem = scope(nc, ctx)
        idm = sb("at_ident", [P, P])
        q, k, vT = (sb(f"at_{n}", [HD, 2, T]) for n in ("q", "k", "v"))
        bias = sb("at_bias", [P, 2, BIAS_GEN + BIAS_INT])
        v = sb("at_vtok", [P, 2, NT * HD])
        logits = sb("at_logits", [P, 2, KMAX])
        probs = sb("at_probs", [P, 2, KMAX])
        probsT = sb("at_probsT", [P, 2, KMAX])
        outT = sb("at_outT", [HD, 2, T])
        top = sb("at_max", [P, 2])
        total = sb("at_sum", [P, 2])
        inv = sb("at_inv", [P, 2])
        scores = ps("at_scores", [P, 2, 1024])
        turned = ps("at_turned", [P, 1024])
        oT = ps("at_oT", [P, 2, 512])
        ident_in = sem("at_ident_in")
        head_in, stored = pair_of(sem, "at_head_in"), pair_of(sem, "at_stored")
        head_done = sem("at_head_done")
        v_turned, v_ready = sem("at_v_turned"), sem("at_v_ready")
        scored, biased = sem("at_scored"), sem("at_biased")
        max_ready, exp_ready, normed = sem("at_max_ready"), sem("at_exp"), sem("at_normed")
        p_turned, pT_ready = sem("at_p_turned"), sem("at_pT")
        weighed, o_ready = sem("at_weighed"), sem("at_o")
        dve_steps, passed = sem("at_dve"), sem("at_passed")
        block = ctx.enter_context(nc.Block())

        @block.sync
        def _(sp):
            sp.dma_start(idm[:], ident).then_inc(ident_in, 16)
            with sp.Fori(0, HEADS // 2) as i:
                for u in range(2):
                    sp.wait_ge(head_done, i * 2 + (u + 1))
                    for n, dst in enumerate((q, k, vT)):
                        sp.dma_start(dst[:, u], one(heads_in, i * 2 + (8 * n + u))).then_inc(head_in[u], 16)
                    sp.dma_start(bias[:, u], one(bias_tab, i * 2 + u)).then_inc(head_in[u], 16)

        @block.tensor
        def _(pe):
            pe.sem_inc(head_done, 2)
            pe.wait_ge(ident_in, 16)
            with pe.Fori(0, HEADS // 2) as i:
                for u in range(2):
                    n0 = i * (2 * NTI) + u * NTI
                    pe.wait_ge(head_in[u], i * 64 + 64)
                    pe.wait_ge(pT_ready, n0 + 1)
                    pe.sem_inc(passed, 1)
                    for t in range(NT):
                        mm = pe.transpose(turned[:, t * HD:(t + 1) * HD], vT[:, u, t * P:(t + 1) * P],
                                          idm[0:HD, 0:HD])
                    mm.then_inc(v_turned, 1)

                    def score(n):
                        q0, k0, kn, _ = tiles[n]
                        pe.wait_ge(biased, n0 + (n + 1))
                        for c in range(0, kn, 512):
                            w = min(512, kn - c)
                            mm = pe.matmul(scores[:, n % 2, c:c + w], q[:, u, q0:q0 + P],
                                           k[:, u, k0 + c:k0 + c + w], start=True, stop=True)
                        mm.then_inc(scored, 1)

                    def weigh(n):
                        q0, k0, kn, _ = tiles[n]
                        pe.wait_ge(normed, n0 + (n + 1))
                        if n == 0:
                            pe.wait_ge(v_ready, i * 2 + (u + 1))
                        else:
                            pe.wait_ge(pT_ready, n0 + (n + 1))
                        for c in range(0, kn, P):
                            w = min(P, kn - c)
                            mm = pe.transpose(turned[0:w, c:c + P], probs[:, n % 2, c:c + w], idm[:])
                        mm.then_inc(p_turned, 1)
                        pe.wait_ge(pT_ready, n0 + (n + 2))
                        pe.wait_ge(o_ready, n0 + (n + 1))
                        for c in range(0, kn, P):
                            w = min(P, kn - c)
                            vt = (k0 + c) // P
                            mm = pe.matmul(oT[0:HD, n % 2, 0:P], v[0:w, u, vt * HD:(vt + 1) * HD],
                                           probsT[0:w, n % 2, c:c + P], start=(c == 0), stop=(c + P >= kn))
                        mm.then_inc(weighed, 1)

                    score(0)
                    for n in range(NTI):
                        if n + 1 < NTI:
                            score(n + 1)
                        weigh(n)
                    pe.wait_ge(weighed, n0 + NTI)
                    pe.sem_inc(head_done, 1)

        @block.vector
        def _(dve):
            own = Steps(dve, dve_steps)
            dve.sem_inc(biased, 2)
            dve.sem_inc(o_ready, 2)
            dve.sem_inc(stored[0], 16)
            dve.sem_inc(stored[1], 16)
            with dve.Fori(0, HEADS // 2) as i:
                own.enter(i, 2 * NTI)
                for u in range(2):
                    n0 = i * (2 * NTI) + u * NTI
                    dve.wait_ge(v_turned, i * 2 + (u + 1))
                    dve.wait_ge(head_done, i * 2 + (u + 1))
                    dve.tensor_copy(v[:, u], turned[:, 0:NT * HD]).then_inc(v_ready, 1)

                    def bias_and_max(n):
                        _, _, kn, col = tiles[n]
                        dve.wait_ge(scored, n0 + (n + 1))
                        dve.wait_ge(exp_ready, n0 + (n + 1))
                        dve.scalar_tensor_tensor(logits[:, n % 2, 0:kn], scores[:, n % 2, 0:kn], HD ** -0.5,
                                                 bias[:, u, col:col + kn], ALU.mult, ALU.add).then_inc(biased, 1)
                        dve.wait_ge(biased, n0 + (n + 3))
                        dve.tensor_reduce(top[:, n % 2:n % 2 + 1], logits[:, n % 2, 0:kn], AX.X, ALU.max,
                                          negate=True).then_inc(max_ready, 1)

                    def norm(n):
                        _, _, kn, _ = tiles[n]
                        dve.wait_ge(exp_ready, n0 + (n + 3))
                        own.link(dve.reciprocal(inv[:, n % 2:n % 2 + 1], total[:, n % 2:n % 2 + 1]))
                        dve.tensor_scalar(probs[:, n % 2, 0:kn], probs[:, n % 2, 0:kn], inv[:, n % 2:n % 2 + 1],
                                          None, ALU.mult).then_inc(normed, 1)

                    def take(n):
                        q0 = tiles[n][0]
                        dve.wait_ge(weighed, n0 + (n + 1))
                        if n == 0:
                            dve.wait_ge(stored[u], i * 16 + 16)
                        dve.tensor_copy(outT[:, u, q0:q0 + P], oT[0:HD, n % 2, 0:P]).then_inc(o_ready, 1)

                    bias_and_max(0)
                    for n in range(NTI):
                        if n + 1 < NTI:
                            bias_and_max(n + 1)
                        norm(n)
                        if n:
                            take(n - 1)
                    take(NTI - 1)
            own.leave(HEADS // 2)

        @block.scalar
        def _(act):
            act.sem_inc(exp_ready, 2)
            act.sem_inc(pT_ready, 1)
            with act.Fori(0, HEADS // 2) as i:
                for u in range(2):
                    n0 = i * (2 * NTI) + u * NTI

                    def exp(n):
                        kn = tiles[n][2]
                        act.wait_ge(max_ready, n0 + (n + 1))
                        act.wait_ge(pT_ready, n0 + (n if n else 1))
                        act.activation(probs[:, n % 2, 0:kn], logits[:, n % 2, 0:kn], ACT.Exp,
                                       bias=top[:, n % 2:n % 2 + 1], accum_out=total[:, n % 2:n % 2 + 1]
                                       ).then_inc(exp_ready, 1)

                    def copy_turned(n):
                        kn = tiles[n][2]
                        full = kn // P * P
                        act.wait_ge(p_turned, n0 + (n + 1))
                        act.wait_ge(o_ready, n0 + (n + 1))
                        ins = act.activation(probsT[:, n % 2, 0:full], turned[:, 0:full], ACT.Copy)
                        if kn > full:
                            ins = act.activation(probsT[0:kn - full, n % 2, full:full + P],
                                                 turned[0:kn - full, full:full + P], ACT.Copy)
                        ins.then_inc(pT_ready, 1)

                    exp(0)
                    for n in range(NTI):
                        if n + 1 < NTI:
                            exp(n + 1)
                        copy_turned(n)
                    act.wait_ge(o_ready, n0 + (NTI + 2))
                    act.dma_start(one(heads_out, i * 2 + u), outT[:, u]).then_inc(stored[u], 16)
            for u in range(2):
                act.wait_ge(stored[u], 16 * (1 + HEADS // 2))


C_IDENT, C_LE, C_GT, C_GE, C_LT, C_ONES = range(6)
CHUNKS = [range(0, SEQ_P // P), range(SEQ_P // P, NT)]
HB = HEADS * NT
LOG1P_TERMS = 9


def bc(ap, n):
    return ap.unsqueeze(3).to_broadcast([ap.shape[0], ap.shape[1], ap.shape[2], n])


def ssd(nc, projT, xbcT, dt_bias, a_log, d_row, norm_row, consts, mixT):
    G = HEADS // 2
    with ExitStack() as ctx:
        sb, _, sem = scope(nc, ctx)
        cm = sb("sd_consts", [P, 6, P])
        xtok = sb("sd_x", [P, NT, SSD_W])
        zt = sb("sd_z", [P, NT, SSD_W])
        dt = sb("sd_dt", [P, NT, 2, HEADS])
        adt = sb("sd_adt", [P, NT, 2, HEADS])
        decay = sb("sd_decay", [P, 5, NT, 2, HEADS])
        wst = sb("sd_wst", [P, NT, 2, HEADS])
        entering = [sb(f"sd_ent{d}", [P, NT, SSD_W]) for d in range(2)]
        y = sb("sd_y", [P, NT, SSD_W])
        ssq = sb("sd_ssq", [P, NT])
        nrow = sb("sd_nrow", [P, SSD_W])
        drow = sb("sd_drow", [P, SSD_W])

        with ExitStack() as c0:
            sb, ps, sem = scope(nc, c0)
            dtT = sb("s0_dtT", [HEADS, T])
            bias = sb("s0_bias", [P, 2, HEADS])
            alog = sb("s0_alog", [P, 2, HEADS])
            raw, u, t, t2, s = (sb(f"s0_{n}", [P, NT, 2, HEADS]) for n in ("raw", "u", "t", "t2", "s"))
            dps = ps("s0_dt", [P, NT, HEADS])
            cum = ps("s0_cum", [P, 2, 512])
            loaded, turned, steps = sem("s0_in"), sem("s0_turned"), sem("s0_dve")
            neg_ready, exped, adt_ready, summed, dec_ready, a_exp = (
                sem(f"s0_{n}") for n in ("neg", "exped", "adt", "summed", "dec", "aexp"))
            block = c0.enter_context(nc.Block())

            @block.sync
            def _(sp):
                sp.dma_start(cm[:], consts).then_inc(loaded, 16)
                sp.dma_start(dtT[:], projT[BLK_DT, 0:HEADS, :]).then_inc(loaded, 16)
                sp.dma_start(bias[:].rearrange("p d h -> p (d h)"), rows_bcast(dt_bias, 2 * HEADS)).then_inc(loaded, 16)
                sp.dma_start(alog[:].rearrange("p d h -> p (d h)"), rows_bcast(a_log, 2 * HEADS)).then_inc(loaded, 16)
                sp.dma_start(drow[:], rows_bcast(d_row, SSD_W)).then_inc(loaded, 16)
                sp.dma_start(nrow[:], rows_bcast(norm_row, SSD_W)).then_inc(loaded, 16)

            @block.tensor
            def _(pe):
                pe.wait_ge(loaded, 96)
                for c in range(NT):
                    mm = pe.transpose(dps[:, c], dtT[:, c * P:(c + 1) * P], cm[0:HEADS, C_IDENT, 0:HEADS])
                mm.then_inc(turned, 1)
                pe.wait_ge(adt_ready, 1)
                flat = adt[:].rearrange("p c d h -> p (c d h)")
                n = 2 * HB
                for m, mask in enumerate((C_LE, C_GT, C_GE, C_LT, C_ONES)):
                    mm = pe.matmul(cum[:, m // 3, (m % 3) * n:(m % 3 + 1) * n], cm[:, mask], flat, start=True, stop=True)
                mm.then_inc(summed, 1)

            @block.vector
            def _(dve):
                own = Steps(dve, steps)
                dve.wait_ge(turned, 1)
                for d in range(2):
                    ins = dve.tensor_tensor(raw[:, :, d], dps[:], bias[:, d].unsqueeze(1).to_broadcast([P, NT, HEADS]),
                                            ALU.add)
                    own.add(ins)
                own.wait()
                own.link(dve.tensor_scalar(t[:], raw[:], -1.0, None, ALU.mult))
                dve.tensor_tensor(u[:], raw[:], t[:], ALU.min).then_inc(neg_ready, 1)
                dve.wait_ge(exped, 1)
                own.link(dve.tensor_scalar(t[:], u[:], 2.0, None, ALU.add))
                own.link(dve.reciprocal(t2[:], t[:]))
                own.link(dve.tensor_tensor(t[:], u[:], t2[:], ALU.mult))
                own.link(dve.tensor_tensor(t2[:], t[:], t[:], ALU.mult))
                own.link(dve.tensor_scalar(s[:], t2[:], 1.0 / (2 * LOG1P_TERMS + 1), None, ALU.mult))
                for m in range(LOG1P_TERMS - 1, 0, -1):
                    own.link(dve.scalar_tensor_tensor(s[:], s[:], 1.0 / (2 * m + 1), t2[:], ALU.add, ALU.mult))
                own.link(dve.scalar_tensor_tensor(s[:], s[:], 1.0, t[:], ALU.add, ALU.mult))
                own.link(dve.tensor_scalar(raw[:], raw[:], 0.0, None, ALU.max))
                own.link(dve.scalar_tensor_tensor(dt[:], s[:], 2.0, raw[:], ALU.mult, ALU.add))
                dve.wait_ge(a_exp, 1)
                dve.scalar_tensor_tensor(adt[:].rearrange("p c d h -> p c (d h)"), dt[:].rearrange("p c d h -> p c (d h)"),
                                         -1.0, alog[:].rearrange("p d h -> p (d h)").unsqueeze(1).to_broadcast([P, NT, 2 * HEADS]),
                                         ALU.mult, ALU.mult).then_inc(adt_ready, 1)
                dve.wait_ge(dec_ready, 1)
                for d in range(2):
                    own.add(dve.tensor_tensor(wst[:, :, d], dt[:, :, d], decay[:, 1 + 2 * d, :, d], ALU.mult))
                own.wait()

            @block.scalar
            def _(act):
                act.wait_ge(loaded, 96)
                act.activation(alog[:], alog[:], ACT.Exp).then_inc(a_exp, 1)
                act.wait_ge(neg_ready, 1)
                act.activation(u[:], u[:], ACT.Exp).then_inc(exped, 1)
                act.wait_ge(summed, 1)
                flat = decay[:].rearrange("p m c d h -> p (m c d h)")
                act.activation(flat[:, 0:6 * HB], cum[:, 0, 0:6 * HB], ACT.Exp)
                act.activation(flat[:, 6 * HB:10 * HB], cum[:, 1, 0:4 * HB], ACT.Exp).then_inc(dec_ready, 1)

        with ExitStack() as c1:
            sb, ps, sem = scope(nc, c1)
            xb = sb("s1_xb", [P, 2, 6, P])
            zT = sb("s1_zT", [P, 2, 4, P])
            btok = sb("s1_b", [P, 2, 2 * P])
            xw = sb("s1_xw", [P, 2, 2, SSD_W])
            x_ps, z_ps, b_ps = ps("s1_xps", [P, SSD_W]), ps("s1_zps", [P, SSD_W]), ps("s1_bps", [P, 512])
            st_ps = ps("s1_st", [P, 2, SSD_W])
            loaded = pair_of(sem, "s1_in")
            read_in, turned, x_ready, xw_ready, b_ready, z_ready, st_done, st_out = (
                sem(f"s1_{n}") for n in ("read", "turned", "x", "xw", "b", "z", "st", "stout"))
            block = c1.enter_context(nc.Block())

            @block.sync
            def _(sp):
                with sp.Fori(0, NT // 2) as i:
                    for u in range(2):
                        tok = bass.ds(i * (2 * P) + u * P, P)
                        sp.wait_ge(turned, i * 2 + (u + 1))
                        sp.dma_start(xb[:, u], xbcT[0:6, :, tok].rearrange("b p t -> p b t")).then_inc(loaded[u], 16)
                        sp.dma_start(zT[:, u], projT[BLK_Z:BLK_Z + 4, :, tok].rearrange("b p t -> p b t")
                                     ).then_inc(loaded[u], 16)

            @block.tensor
            def _(pe):
                pe.sem_inc(turned, 2)
                with pe.Fori(0, NT // 2) as i:
                    for u in range(2):
                        pe.wait_ge(loaded[u], i * 32 + 32)
                        pe.wait_ge(x_ready, i * 2 + (u + 1))
                        pe.wait_ge(b_ready, i * 2 + (u + 1))
                        pe.wait_ge(z_ready, i * 2 + (u + 1))
                        for b in range(4):
                            pe.transpose(x_ps[:, b * P:(b + 1) * P], xb[:, u, b], cm[:, C_IDENT])
                            pe.transpose(z_ps[:, b * P:(b + 1) * P], zT[:, u, b], cm[:, C_IDENT])
                        for b in range(2):
                            mm = pe.transpose(b_ps[:, b * P:(b + 1) * P], xb[:, u, 4 + b], cm[:, C_IDENT])
                        mm.then_inc(turned, 1)
                        pe.wait_ge(b_ready, i * 2 + (u + 2))
                        pe.wait_ge(xw_ready, i * 2 + (u + 1))
                        pe.wait_ge(st_out, i * 2 + (u + 1))
                        for d in range(2):
                            for g in range(2):
                                mm = pe.matmul(st_ps[:, d, g * 256:(g + 1) * 256], btok[:, u, g * P:(g + 1) * P],
                                               xw[:, u, d, g * 256:(g + 1) * 256], start=True, stop=True)
                        mm.then_inc(st_done, 1)

            @block.vector
            def _(dve):
                dve.sem_inc(x_ready, 1)
                with dve.Fori(0, NT // 2) as i:
                    for u in range(2):
                        c = i * 2 + u
                        dve.wait_ge(turned, i * 2 + (u + 3))
                        dve.tensor_copy(one_of(xtok, c), x_ps[:]).then_inc(x_ready, 1)
                        dve.wait_ge(x_ready, i * 2 + (u + 2))
                        dve.wait_ge(st_done, i * 2 + (u + 1))
                        for d in range(2):
                            ins = dve.tensor_tensor(
                                xw[:, u, d].rearrange("p (h c) -> p h c", h=HEADS),
                                one_of(xtok, c).rearrange("p (h c) -> p h c", h=HEADS),
                                wst[:, bass.ds(c, 1), d, :].rearrange("p o h -> p (o h)").unsqueeze(2).to_broadcast(
                                    [P, HEADS, HD]), ALU.mult)
                        ins.then_inc(xw_ready, 1)

            @block.scalar
            def _(act):
                act.sem_inc(b_ready, 1)
                act.sem_inc(z_ready, 1)
                act.sem_inc(st_out, 1)
                act.sem_inc(st_done, 2)
                with act.Fori(0, NT // 2) as i:
                    for u in range(2):
                        c = i * 2 + u
                        act.wait_ge(turned, i * 2 + (u + 3))
                        act.wait_ge(st_done, i * 2 + (u + 1))
                        act.activation(btok[:, u], b_ps[:, 0:2 * P], ACT.Copy).then_inc(b_ready, 1)
                        act.activation(one_of(zt, c), z_ps[:], ACT.Silu).then_inc(z_ready, 1)
                        act.wait_ge(st_done, i * 2 + (u + 3))
                        act.activation(one_of(entering[0], c), st_ps[:, 0], ACT.Copy)
                        act.activation(one_of(entering[1], c), st_ps[:, 1], ACT.Copy).then_inc(st_out, 1)

        with ExitStack() as c2:
            sb, ps, sem = scope(nc, c2)
            carry = sb("s2_carry", [P, 2, 2, SSD_W])
            steps = [sem("s2_fwd"), sem("s2_bwd")]
            block = c2.enter_context(nc.Block())

            def recur(eng, d):
                own = Steps(eng, steps[d])
                for seq in CHUNKS:
                    order = list(seq) if d == 0 else list(seq)[::-1]
                    own.link(eng.memset(carry[:, d, 0], 0.0))
                    for n, c in enumerate(order):
                        cur, nxt = carry[:, d, n % 2], carry[:, d, 1 - n % 2]
                        own.link(eng.tensor_tensor(
                            nxt.rearrange("p (h c) -> p h c", h=HEADS), cur.rearrange("p (h c) -> p h c", h=HEADS),
                            decay[:, 4, c, d, :].unsqueeze(2).to_broadcast([P, HEADS, HD]), ALU.mult))
                        own.link(eng.tensor_tensor(nxt, nxt, entering[d][:, c, :], ALU.add))
                        own.link(eng.tensor_copy(entering[d][:, c, :], cur))

            @block.vector
            def _(dve):
                recur(dve, 0)

            @block.gpsimd
            def _(pool):
                recur(pool, 1)

        with ExitStack() as c3:
            sb, ps, sem = scope(nc, c3)
            bcT = sb("s3_bcT", [P, 2, 4, P])
            seg = sb("s3_seg", [P, 2, HEADS, P])
            xdt = sb("s3_xdt", [P, 2, 2, SSD_W])
            m = sb("s3_m", [P, 2, 2, G, P])
            cb = sb("s3_cb", [P, 2, 2, P])
            tmp = sb("s3_tmp", [P, SSD_W])
            acc = sb("s3_acc", [P, SSD_W])
            seg_ps = ps("s3_seg_ps", [P, 2 * HEADS * P])
            cb_ps, y_ps, off_ps = ps("s3_cb_ps", [P, 512]), ps("s3_y_ps", [P, SSD_W]), ps("s3_off_ps", [P, 2, SSD_W])
            loaded = pair_of(sem, "s3_in")
            seg_ready, seg_done, cb_done, decayed, m_ready, y_done, gated = (
                sem(f"s3_{n}") for n in ("seg", "segdone", "cbdone", "decayed", "m", "y", "gated"))
            steps, passed = sem("s3_dve"), sem("s3_passed")
            block = c3.enter_context(nc.Block())

            @block.sync
            def _(sp):
                with sp.Fori(0, NT // 2) as i:
                    for u in range(2):
                        sp.wait_ge(y_done, i * 2 + (u + 1))
                        sp.dma_start(bcT[:, u], xbcT[4:8, :, bass.ds(i * (2 * P) + u * P, P)].rearrange("b p t -> p b t")
                                     ).then_inc(loaded[u], 16)

            @block.vector
            def _(dve):
                own = Steps(dve, steps)
                dve.sem_inc(gated, 1)
                with dve.Fori(0, NT // 2) as i:
                    own.enter(i, 2 * 10)
                    for u in range(2):
                        c = i * 2 + u
                        row = lambda ap, d: ap[:, bass.ds(c, 1), d, :].rearrange("p o h -> p (o h)")
                        dve.wait_ge(seg_done, i * 2 + (u + 1))
                        for d, mask in enumerate((C_GT, C_LT)):
                            ins = dve.tensor_tensor(seg[:, d], cm[:, mask].unsqueeze(1).to_broadcast([P, HEADS, P]),
                                                    row(adt, d).unsqueeze(2).to_broadcast([P, HEADS, P]), ALU.mult)
                        ins.then_inc(seg_ready, 1)
                        dve.wait_ge(y_done, i * 2 + (u + 2))
                        xc = one_of(xtok, c).rearrange("p (h c) -> p h c", h=HEADS)
                        for d in range(2):
                            own.add(dve.tensor_tensor(xdt[:, 0, d].rearrange("p (h c) -> p h c", h=HEADS), xc,
                                                      row(dt, d).unsqueeze(2).to_broadcast([P, HEADS, HD]), ALU.mult))
                        dve.wait_ge(cb_done, i * 2 + (u + 1))
                        for d, mask in enumerate((C_LE, C_GE)):
                            own.add(dve.tensor_tensor(cb[:, d], cb_ps[:, 0:2 * P].rearrange("p (g l) -> p g l", g=2),
                                                      cm[:, mask].unsqueeze(1).to_broadcast([P, 2, P]), ALU.mult))
                        own.wait()
                        dve.wait_ge(decayed, i * 2 + (u + 1))
                        dg = m[:].rearrange("p d g h l -> p (d g) h l")
                        dve.tensor_tensor(dg, dg, cb[:].rearrange("p d g l -> p (d g) l").unsqueeze(2).to_broadcast(
                            [P, 4, G, P]), ALU.mult).then_inc(m_ready, 1)
                        dve.wait_ge(y_done, i * 2 + (u + 3))
                        hv = lambda ap: ap.rearrange("p (h c) -> p h c", h=HEADS)
                        dec = lambda k, d: decay[:, k, bass.ds(c, 1), d, :].rearrange("p o h -> p (o h)").unsqueeze(
                            2).to_broadcast([P, HEADS, HD])
                        own.add(dve.tensor_tensor(hv(acc[:]), hv(off_ps[:, 0]), dec(0, 0), ALU.mult))
                        own.link(dve.tensor_tensor(hv(tmp[:]), hv(off_ps[:, 1]), dec(2, 1), ALU.mult))
                        own.link(dve.tensor_tensor(acc[:], acc[:], tmp[:], ALU.add))
                        own.add(dve.tensor_tensor(acc[:], acc[:], y_ps[:], ALU.add))
                        own.link(dve.tensor_tensor(tmp[:], one_of(xtok, c), drow[:], ALU.mult))
                        own.link(dve.tensor_tensor(acc[:], acc[:], tmp[:], ALU.add))
                        dve.tensor_tensor(one_of(y, c), acc[:], one_of(zt, c), ALU.mult).then_inc(gated, 1)
                own.leave(NT // 2)

            @block.tensor
            def _(pe):
                pe.sem_inc(seg_done, 1)
                pe.sem_inc(y_done, 2)
                with pe.Fori(0, NT // 2) as i:
                    for u in range(2):
                        c = i * 2 + u
                        pe.wait_ge(loaded[u], i * 16 + 16)
                        pe.wait_ge(m_ready, i * 2 + (u + 1))
                        for g in range(2):
                            mm = pe.matmul(cb_ps[:, g * P:(g + 1) * P], bcT[:, u, g], bcT[:, u, 2 + g],
                                           start=True, stop=True)
                        mm.then_inc(cb_done, 1)
                        pe.wait_ge(seg_ready, i * 2 + (u + 1))
                        for d, mask in enumerate((C_LE, C_GE)):
                            for h in range(HEADS):
                                n = d * HEADS + h
                                mm = pe.matmul(seg_ps[:, n * P:(n + 1) * P], seg[:, d, h], cm[:, mask],
                                               start=True, stop=True)
                        mm.then_inc(seg_done, 1)
                        pe.wait_ge(gated, i * 2 + (u + 1))
                        pe.sem_inc(passed, 1)
                        for d in range(2):
                            for g in range(2):
                                pe.matmul(off_ps[:, d, g * 256:(g + 1) * 256], bcT[:, u, 2 + g],
                                          one_of(entering[d], c)[:, g * 256:(g + 1) * 256], start=True, stop=True)
                        pe.wait_ge(m_ready, i * 2 + (u + 2))
                        for h in range(HEADS):
                            for d in range(2):
                                mm = pe.matmul(y_ps[:, h * HD:(h + 1) * HD], m[:, d, h // G, h % G],
                                               xdt[:, 0, d, h * HD:(h + 1) * HD], start=(d == 0), stop=(d == 1))
                        mm.then_inc(y_done, 1)

            @block.scalar
            def _(act):
                act.sem_inc(m_ready, 1)
                with act.Fori(0, NT // 2) as i:
                    for u in range(2):
                        act.wait_ge(seg_done, i * 2 + (u + 2))
                        act.wait_ge(y_done, i * 2 + (u + 2))
                        act.activation(m[:].rearrange("p d g h l -> p (d g h l)"), seg_ps[:], ACT.Exp
                                       ).then_inc(decayed, 1)

        with ExitStack() as c4:
            sb, ps, sem = scope(nc, c4)
            junk = sb("s4_junk", [P, SSD_W])
            yn = sb("s4_yn", [P, 2, SSD_W])
            oT = sb("s4_oT", [P, 2, 4, P])
            t_ps = ps("s4_t", [P, 2, SSD_W])
            squared, root, var, normed, turned, copied, steps = (
                sem(f"s4_{n}") for n in ("sq", "root", "var", "normed", "turned", "copied", "dve"))
            stored = pair_of(sem, "s4_stored")
            block = c4.enter_context(nc.Block())

            @block.scalar
            def _(act):
                for c in range(NT):
                    if c:
                        act.wait_ge(squared, c)
                    act.activation(junk[:], y[:, c, :], ACT.Square, accum_out=ssq[:, c:c + 1]).then_inc(squared, 1)
                act.wait_ge(var, 1)
                act.activation(ssq[:], ssq[:], ACT.Sqrt).then_inc(root, 1)
                act.sem_inc(copied, 2)
                act.sem_inc(stored[0], 16)
                act.sem_inc(stored[1], 16)
                with act.Fori(0, NT // 2) as i:
                    for u in range(2):
                        act.wait_ge(turned, i * 2 + (u + 3))
                        act.wait_ge(stored[u], i * 16 + 16)
                        act.activation(oT[:, u].rearrange("p b t -> p (b t)"), t_ps[:, u], ACT.Copy).then_inc(copied, 1)
                        act.wait_ge(copied, i * 2 + (u + 3))
                        act.dma_start(mixT[4:8, :, bass.ds(i * (2 * P) + u * P, P)].rearrange("b p t -> p b t"),
                                      oT[:, u]).then_inc(stored[u], 16)
                for u in range(2):
                    act.wait_ge(stored[u], 16 * (1 + NT // 2))

            @block.vector
            def _(dve):
                own = Steps(dve, steps)
                dve.wait_ge(squared, NT)
                dve.tensor_scalar(ssq[:], ssq[:], 1.0 / SSD_W, EPS, ALU.mult, ALU.add).then_inc(var, 1)
                dve.wait_ge(root, 1)
                own.link(dve.reciprocal(ssq[:], ssq[:]))
                with dve.Fori(0, NT // 2) as i:
                    for u in range(2):
                        dve.wait_ge(turned, i * 2 + (u + 1))
                        dve.scalar_tensor_tensor(yn[:, u], one_of(y, i * 2 + u), ssq[:, bass.ds(i * 2 + u, 1)], nrow[:],
                                                 ALU.mult, ALU.mult).then_inc(normed, 1)

            @block.tensor
            def _(pe):
                pe.sem_inc(turned, 2)
                with pe.Fori(0, NT // 2) as i:
                    for u in range(2):
                        pe.wait_ge(normed, i * 2 + (u + 1))
                        pe.wait_ge(copied, i * 2 + (u + 1))
                        for b in range(4):
                            mm = pe.transpose(t_ps[:, u, b * P:(b + 1) * P], yn[:, u, b * P:(b + 1) * P], cm[:, C_IDENT])
                        mm.then_inc(turned, 1)


def project_out(nc, mixT, w_out, x, w_row, ident, x2, hT):
    with ExitStack() as ctx:
        sb, ps, sem = scope(nc, ctx)
        idm, wrow = sb("po_ident", [P, P]), sb("po_wrow", [P, D])
        w = [sb(f"po_w_{part}", [P, KD, D], F32R) for part in ("hi", "lo")]
        wraw = sb("po_wraw", [P, 2, D])
        mraw = sb("po_mraw", [P, 2, KD * P])
        mx = [sb(f"po_m_{part}", [P, 2, KD * P], F32R) for part in ("hi", "lo")]
        xin, xo, xs = sb("po_x", [P, 2, D]), sb("po_x2", [P, 2, D]), sb("po_xs", [P, D])
        ssq, rstd = sb("po_ssq", [P, 2]), sb("po_rstd", [P, 2])
        acc, xT = ps("po_acc", [P, 2, D]), ps("po_xT", [P, 2, D])
        consts_in, w_in = sem("po_consts_in"), pair_of(sem, "po_w_in")
        m_in, stored = pair_of(sem, "po_m_in"), pair_of(sem, "po_stored")
        w_hi, w_split, m_split, summed, added, squared, var, root, scaled, turned, hi_done, lo_done, steps = (
            sem(f"po_{n}") for n in ("w_hi", "w_split", "m_split", "summed", "added", "squared", "var", "root",
                                     "scaled", "turned", "hi", "lo", "dve"))
        block = ctx.enter_context(nc.Block())

        def tok(r, u):
            return bass.ds(r * (2 * P) + u * P, P)

        @block.sync
        def _(sp):
            for k in range(2):
                sp.dma_start(wraw[:, k], w_out[k]).then_inc(w_in[k], 16)
            sp.dma_start(idm[:], ident).then_inc(consts_in, 16)
            sp.dma_start(wrow[:], rows_bcast(w_row, D)).then_inc(consts_in, 16)
            for k in range(2, KD):
                sp.wait_ge(w_split, k - 1)
                sp.dma_start(wraw[:, k % 2], w_out[k]).then_inc(w_in[k % 2], 16)
            with sp.Fori(0, NT // 2) as i:
                for u in range(2):
                    sp.wait_ge(m_split, i * 2 + (u + 1))
                    sp.wait_ge(added, i * 2 + (u + 1))
                    sp.dma_start(mraw[:, u].rearrange("p (k t) -> p k t", k=KD),
                                 mixT[:, :, tok(i, u)].rearrange("b p t -> p b t")).then_inc(m_in[u], 16)
                    sp.dma_start(xin[:, u], x[tok(i, u), :]).then_inc(m_in[u], 16)

        @block.tensor
        def _(pe):
            pe.sem_inc(lo_done, 2)

            def products(r, u):
                pe.wait_ge(m_split, r * 2 + (u + 3))
                pe.wait_ge(added, r * 2 + (u + 1))
                for k in range(KD):
                    for n, (a, b) in enumerate(PRODUCTS):
                        for h in range(2):
                            mm = pe.matmul(acc[:, u, h * 512:(h + 1) * 512], mx[a][:, u, k * P:(k + 1) * P],
                                           w[b][:, k, h * 512:(h + 1) * 512], start=(k + n == 0),
                                           stop=(k == KD - 1 and n == 2))
                mm.then_inc(summed, 1)

            def turn(r, u):
                pe.wait_ge(scaled, r * 2 + (u + 1))
                pe.wait_ge(lo_done, r * 2 + (u + 1))
                for k in range(KD):
                    mm = pe.transpose(xT[:, u, k * P:(k + 1) * P], xs[:, k * P:(k + 1) * P], idm[:])
                mm.then_inc(turned, 1)

            pe.wait_ge(w_split, KD)
            pe.wait_ge(consts_in, 32)
            products(0, 0)

            def step(r, u):
                products(r + u, 1 - u)
                turn(r, u)
            rounds(pe, NT - 1, step)
            turn(NT // 2 - 1, 1)

        @block.scalar
        def _(act):
            act.sem_inc(stored[0], 16)
            act.sem_inc(stored[1], 16)
            for k in range(KD):
                act.wait_ge(w_in[k % 2], 16 * (k // 2 + 1))
                act.activation(w[0][:, k], wraw[:, k % 2], ACT.Copy).then_inc(w_hi, 1)

            def stats(r, u):
                act.wait_ge(added, r * 2 + (u + 3))
                act.activation(xs[:], xo[:, u], ACT.Square, accum_out=ssq[:, u:u + 1]).then_inc(squared, 1)
                act.wait_ge(var, r * 2 + (u + 1))
                act.activation(rstd[:, u:u + 1], ssq[:, u:u + 1], ACT.Sqrt).then_inc(root, 1)
                act.dma_start(x2[tok(r, u), :], xo[:, u]).then_inc(stored[u], 16)

            def hi(r, u):
                act.wait_ge(turned, r * 2 + (u + 1))
                act.activation(hT[0][:, :, tok(r, u)], xT[:, u].rearrange("p (k t) -> p k t", k=KD), ACT.Copy
                               ).then_inc(hi_done, 1)

            def step(r, u):
                stats(r, u)
                hi(r, u)
            rounds(act, NT, step)
            for u in range(2):
                act.wait_ge(stored[u], 16 * (1 + NT // 2))

        @block.vector
        def _(dve):
            own = Steps(dve, steps)
            dve.sem_inc(m_split, 2)
            dve.sem_inc(added, 2)
            for k in range(KD):
                dve.wait_ge(w_hi, k + 1)
                dve.tensor_tensor(w[1][:, k], wraw[:, k % 2], w[0][:, k].bitcast(F32), ALU.subtract).then_inc(w_split, 1)

            def parts(r, u):
                dve.wait_ge(m_in[u], r * 32 + 32)
                if not (isinstance(r, int) and r == 0):
                    dve.wait_ge(summed, r * 2 + (u - 1))
                split(dve, own, mx[0][:, u], mx[1][:, u], mraw[:, u]).then_inc(m_split, 1)

            def norm(r, u):
                dve.wait_ge(summed, r * 2 + (u + 1))
                dve.wait_ge(stored[u], r * 16 + 16)
                dve.tensor_tensor(xo[:, u], acc[:, u], xin[:, u], ALU.add).then_inc(added, 1)
                dve.wait_ge(squared, r * 2 + (u + 1))
                dve.tensor_scalar(ssq[:, u:u + 1], ssq[:, u:u + 1], 1.0 / D, EPS, ALU.mult, ALU.add).then_inc(var, 1)
                dve.wait_ge(root, r * 2 + (u + 1))
                own.link(dve.reciprocal(rstd[:, u:u + 1], rstd[:, u:u + 1]))
                dve.scalar_tensor_tensor(xs[:], xo[:, u], rstd[:, u:u + 1], wrow[:], ALU.mult, ALU.mult
                                         ).then_inc(scaled, 1)

            def lo(r, u):
                dve.wait_ge(hi_done, r * 2 + (u + 1))
                dve.tensor_tensor(hT[1][:, :, tok(r, u)], xT[:, u].rearrange("p (k t) -> p k t", k=KD),
                                  hT[0][:, :, tok(r, u)].bitcast(F32), ALU.subtract).then_inc(lo_done, 1)

            dve.wait_ge(consts_in, 32)
            parts(0, 0)
            parts(0, 1)
            with dve.Fori(0, NT // 2 - 1) as i:
                own.enter(i, 4)
                for u in range(2):
                    norm(i, u)
                    parts(i + 1, u)
                    lo(i, u)
            own.leave(NT // 2 - 1)
            for u in range(2):
                norm(NT // 2 - 1, u)
                lo(NT // 2 - 1, u)


RECTS = [(0, 1, 16), (1, 1, 8), (2, 2, 5), (4, 4, 3), (8, 8, 1)]
NCAND = sum(na * nb for _, na, nb in RECTS)


def row_starts():
    starts, at = [], 0
    for _, na, nb in RECTS:
        for _ in range(na):
            starts.append(at)
            at += nb
    return starts


def retrieve(nc, hT, w_query, keysT, starts, tabs):
    KZ = KD * P
    with ExitStack() as ctx:
        sb, ps, sem = scope(nc, ctx)
        wraw = sb("pk_wraw", [P, 2, KZ])
        w = [sb(f"pk_w_{part}", [P, 2, KZ], F32R) for part in ("hi", "lo")]
        keys = sb("pk_keys", [P, 2, P])
        qT = sb("pk_qT", [P, 2, T])
        s = sb("pk_s", [P, 2, NT, NKEY])
        rest = sb("pk_rest", [P, 2, NT, NKEY])
        sv = sb("pk_sv", [P, 2, NT, TOPK])
        si = sb("pk_si", [P, 2, NT, TOPK], U32)
        sif = sb("pk_sif", [P, 2, NT, TOPK], BF16)
        dif = sb("pk_dif", [P, NT, TOPK], BF16)
        cand = sb("pk_cand", [P, NT, NCAND])
        crest = sb("pk_crest", [P, NT, NCAND])
        cv = sb("pk_cv", [P, NT, TOPK])
        ci = sb("pk_ci", [P, NT, TOPK], U32)
        cf, base, second = sb("pk_cf", [P, NT, TOPK]), sb("pk_base", [P, NT, TOPK]), sb("pk_second", [P, NT, TOPK])
        hot = sb("pk_hot", [P, NT, TOPK, TOPK], BF16)
        prod = sb("pk_prod", [P, 2, NT, TOPK, TOPK], BF16)
        st = sb("pk_starts", [P, 3, TOPK])
        stb = sb("pk_starts_b", [P, 3, TOPK], BF16)
        den = sb("pk_den", [P, NT])
        acc = ps("pk_acc", [P, 2, 3 * 512])
        consts_in, w_in, keys_in = sem("pk_consts_in"), pair_of(sem, "pk_w_in"), sem("pk_keys_in")
        w_hi, w_split, summed, q_ready, scored, s_ready, s_read, exp_in, exp_out, steps, passed = (
            sem(f"pk_{n}") for n in ("w_hi", "w_split", "summed", "q", "scored", "s", "s_read", "exp_in", "exp_out",
                                     "dve", "passed"))
        block = ctx.enter_context(nc.Block())

        @block.sync
        def _(sp):
            sp.dma_start(st[:], rows_bcast(starts, 3 * TOPK)).then_inc(consts_in, 16)
            with sp.Fori(0, HEADS) as h:
                for z in range(2):
                    sp.wait_ge(w_split, h * 2 + (z + 1))
                    sp.dma_start(wraw[:, z], one(w_query, h * 2 + z)).then_inc(w_in[z], 16)
                sp.wait_ge(scored, h * 2 + 2)
                sp.dma_start(keys[:], keysT[bass.ds(h * 2, 2)].rearrange("z p n -> p z n")).then_inc(keys_in, 16)

        @block.tensor
        def _(pe):
            pe.sem_inc(scored, 2)
            pe.sem_inc(summed, 2)
            with pe.Fori(0, HEADS) as h:
                for z in range(2):
                    pe.wait_ge(w_split, h * 2 + (z + 3))
                    pe.wait_ge(s_ready, h * 2 + (z + 1))
                    for k in range(KD):
                        for n, (a, b) in enumerate(PRODUCTS):
                            for t0, tn in SEGS:
                                mm = pe.matmul(acc[:, z, t0:t0 + tn], w[a][:, z, k * P:(k + 1) * P],
                                               hT[b][:, k, t0:t0 + tn], start=(k + n == 0),
                                               stop=(k == KD - 1 and n == 2))
                    mm.then_inc(summed, 1)
                pe.wait_ge(keys_in, h * 16 + 16)
                for z in range(2):
                    pe.wait_ge(q_ready, h * 2 + (z + 1))
                    for t in range(NT):
                        mm = pe.matmul(acc[:, z, t * P:(t + 1) * P], qT[:, z, t * P:(t + 1) * P], keys[:, z],
                                       start=True, stop=True)
                    mm.then_inc(scored, 1)

        @block.scalar
        def _(act):
            act.sem_inc(s_ready, 2)

            def hi(h):
                for z in range(2):
                    act.wait_ge(w_in[z], h * 16 + 16)
                    act.wait_ge(summed, h * 2 + (z + 1))
                    act.activation(w[0][:, z], wraw[:, z], ACT.Copy).then_inc(w_hi, 1)

            def scores_out(h):
                for z in range(2):
                    act.wait_ge(summed, h * 2 + (z + 3))
                    act.activation(qT[:, z], acc[:, z, 0:T], ACT.Copy).then_inc(q_ready, 1)
                for z in range(2):
                    act.wait_ge(scored, h * 2 + (z + 3))
                    act.wait_ge(s_read, h + 1)
                    act.activation(s[:, z].rearrange("p t n -> p (t n)"), acc[:, z, 0:T], ACT.Copy).then_inc(s_ready, 1)

            def exps(h):
                act.wait_ge(exp_in, h + 1)
                act.activation(cv[:], cv[:], ACT.Exp).then_inc(exp_out, 1)

            hi(0)
            with act.Fori(0, HEADS - 1) as h:
                scores_out(h)
                hi(h + 1)
                exps(h)
            scores_out(HEADS - 1)
            exps(HEADS - 1)

        @block.vector
        def _(dve):
            own = Steps(dve, steps)
            dve.sem_inc(w_split, 2)
            dve.sem_inc(s_read, 1)

            def parts(h):
                for z in range(2):
                    dve.wait_ge(w_hi, h * 2 + (z + 1))
                    dve.tensor_tensor(w[1][:, z], wraw[:, z], w[0][:, z].bitcast(F32), ALU.subtract).then_inc(w_split, 1)

            def over(items):
                for ins in items:
                    last = ins
                    own.add(ins)
                own.wait()
                dve.sem_inc(passed, 1)

            def each(f):
                over(f(z, t) for z in range(2) for t in range(NT))

            def topk(h):
                dve.wait_ge(s_ready, h * 2 + 4)
                dve.sem_inc(passed, 1)
                each(lambda z, t: dve.max(sv[:, z, t, 0:8], s[:, z, t]))
                for z in range(2):
                    for t in range(NT):
                        own.add(dve.max_index(si[:, z, t, 0:8], sv[:, z, t, 0:8], s[:, z, t]))
                each(lambda z, t: dve.match_replace(rest[:, z, t], sv[:, z, t, 0:8], s[:, z, t], LOWEST))
                dve.sem_inc(s_read, 1)
                each(lambda z, t: dve.max(sv[:, z, t, 8:16], rest[:, z, t]))
                each(lambda z, t: dve.max_index(si[:, z, t, 8:16], sv[:, z, t, 8:16], rest[:, z, t]))
                own.add(dve.tensor_copy(sif[:], si[:]))
                at, made = 0, []
                for a0, na, nb in RECTS:
                    made.append(dve.tensor_tensor(
                        cand[:, :, at:at + na * nb].rearrange("p t (a b) -> p t a b", a=na),
                        sv[:, 0, :, a0:a0 + na].unsqueeze(3).to_broadcast([P, NT, na, nb]),
                        sv[:, 1, :, 0:nb].unsqueeze(2).to_broadcast([P, NT, na, nb]), ALU.add))
                    own.add(made[-1])
                    at += na * nb
                own.wait()
                dve.sem_inc(passed, 1)
                over(dve.max(cv[:, t, 0:8], cand[:, t]) for t in range(NT))
                for t in range(NT):
                    own.add(dve.max_index(ci[:, t, 0:8], cv[:, t, 0:8], cand[:, t]))
                over(dve.match_replace(crest[:, t], cv[:, t, 0:8], cand[:, t], LOWEST) for t in range(NT))
                over(dve.max(cv[:, t, 8:16], crest[:, t]) for t in range(NT))
                over(dve.max_index(ci[:, t, 8:16], cv[:, t, 8:16], crest[:, t]) for t in range(NT))
                own.add(dve.tensor_copy(cf[:], ci[:]))
                own.add(dve.tensor_copy(dif[:, :, 0:1], sif[:, 0, :, 0:1]))
                own.add(dve.tensor_tensor(dif[:, :, 1:TOPK], sif[:, 0, :, 1:TOPK], sif[:, 0, :, 0:TOPK - 1], ALU.subtract))
                own.link(dve.tensor_copy(den[:], cv[:, :, 0:1].rearrange("p t o -> p (t o)")))
                dve.tensor_tensor(cv[:], cv[:], den[:].unsqueeze(2).to_broadcast([P, NT, TOPK]), ALU.subtract
                                  ).then_inc(exp_in, 1)
                flat = lambda ap: ap.rearrange("p t k -> p (t k)").unsqueeze(2).to_broadcast([P, NT * TOPK, TOPK])
                row = lambda n: st[:, n].unsqueeze(1).to_broadcast([P, NT * TOPK, TOPK])
                hot2 = hot[:].rearrange("p t k a -> p (t k) a")
                by_tile = lambda ap: ap.unsqueeze(2).to_broadcast([P, NT, TOPK, TOPK])
                sums = lambda out, n: dve.tensor_reduce(out, prod[:, n].rearrange("p t k a -> p (t k) a"), AX.X, ALU.add)
                col = tabs_cols(h)
                own.link(dve.tensor_tensor(hot2, flat(cf[:]), row(0), ALU.is_ge))
                own.add(dve.tensor_tensor(prod[:, 0], hot[:], by_tile(dif[:]), ALU.mult))
                own.link(dve.tensor_tensor(prod[:, 1].rearrange("p t k a -> p (t k) a"), hot2,
                                           stb[:, 1].unsqueeze(1).to_broadcast([P, NT * TOPK, TOPK]), ALU.mult))
                own.add(sums(second[:].rearrange("p t k -> p (t k)"), 0))
                own.link(sums(base[:].rearrange("p t k -> p (t k)"), 1))
                own.add(dve.tensor_copy(tabs[0][:, :, col], second[:]))
                own.link(dve.tensor_tensor(cf[:], cf[:], base[:], ALU.subtract))
                own.link(dve.tensor_tensor(hot2, flat(cf[:]), row(2), ALU.is_equal))
                own.link(dve.tensor_tensor(prod[:, 0], hot[:], by_tile(sif[:, 1]), ALU.mult))
                own.link(sums(second[:].rearrange("p t k -> p (t k)"), 0))
                own.add(dve.tensor_copy(tabs[1][:, :, col], second[:]))
                dve.wait_ge(exp_out, h + 1)
                own.link(dve.tensor_reduce(den[:], cv[:], AX.X, ALU.add))
                own.link(dve.reciprocal(den[:], den[:]))
                own.link(dve.tensor_tensor(tabs[2][:, :, col], cv[:], den[:].unsqueeze(2).to_broadcast([P, NT, TOPK]),
                                           ALU.mult))

            def tabs_cols(h):
                return bass.ds(h * TOPK, TOPK)

            dve.wait_ge(consts_in, 16)
            own.link(dve.tensor_copy(stb[:], st[:]))
            parts(0)
            with dve.Fori(0, HEADS - 1) as h:
                own.enter(h, 174)
                parts(h + 1)
                topk(h)
            own.leave(HEADS - 1)
            topk(HEADS - 1)



def turn_tables(nc, tabs, ident, tabsT):
    with ExitStack() as ctx:
        sb, ps, sem = scope(nc, ctx)
        idm = sb("tt_ident", [P, P])
        tp = ps("tt_ps", [P, 2, 1024])
        loaded, turned, copied = sem("tt_in"), sem("tt_turned"), sem("tt_copied")
        block = ctx.enter_context(nc.Block())
        steps = [(n, h) for n in range(3) for h in range(2)]

        @block.sync
        def _(sp):
            sp.dma_start(idm[:], ident).then_inc(loaded, 16)

        @block.tensor
        def _(pe):
            pe.wait_ge(loaded, 16)
            for m, (n, h) in enumerate(steps):
                if m > 1:
                    pe.wait_ge(copied, m - 1)
                for t in range(NT // 2):
                    mm = pe.transpose(tp[:, m % 2, t * P:(t + 1) * P], tabs[n][:, h * (NT // 2) + t], idm[:])
                mm.then_inc(turned, 1)

        @block.scalar
        def _(act):
            for m, (n, h) in enumerate(steps):
                act.wait_ge(turned, m + 1)
                act.activation(tabsT[n][:, h * HALF:(h + 1) * HALF], tp[:, m % 2, 0:HALF], ACT.Copy).then_inc(copied, 1)


def gate_table(nc, tabsT, iota, gates):
    GROUP, BUFS = 4, 4
    PER = TB // GROUP
    with ExitStack() as ctx:
        sb, ps, sem = scope(nc, ctx)
        io = sb("gt_iota", [P, P])
        left, right = (sb(f"gt_{n}", [P, BUFS, GROUP, P]) for n in ("left", "right"))
        stage = sb("gt_stage", [P, 2, P * TB])
        prod = ps("gt_prod", [P, BUFS, 512])
        loaded, built, summed, copied = sem("gt_in"), sem("gt_built"), sem("gt_summed"), sem("gt_copied")
        stored = pair_of(sem, "gt_stored")
        block = ctx.enter_context(nc.Block())
        N = T // TB

        @block.sync
        def _(sp):
            sp.dma_start(io[:], iota).then_inc(loaded, 16)
            sp.sem_inc(stored[0], 16)
            sp.sem_inc(stored[1], 16)
            with sp.Fori(0, N // 2) as i:
                for u in range(2):
                    sp.wait_ge(copied, i * (2 * PER) + (u + 1) * PER + BUFS)
                    sp.dma_start(one(gates, i * 2 + u), stage[:, u]).then_inc(stored[u], 16)
            for u in range(2):
                sp.wait_ge(stored[u], 16 * (1 + N // 2))

        @block.vector
        def _(dve):
            dve.wait_ge(loaded, 16)
            with dve.Fori(0, N // 2) as i:
                for g in range(2 * PER):
                    dve.wait_ge(summed, i * (2 * PER) + (g + 1))
                    for t in range(GROUP):
                        col = bass.ds(i * (2 * TB) + (g * GROUP + t), 1)
                        dve.tensor_scalar(left[:, g % BUFS, t], io[:], tabsT[0][:, col], tabsT[2][:, col],
                                          ALU.is_equal, ALU.mult)
                        ins = dve.tensor_scalar(right[:, g % BUFS, t], io[:], tabsT[1][:, col], None, ALU.is_equal)
                    ins.then_inc(built, 1)

        @block.tensor
        def _(pe):
            pe.sem_inc(summed, BUFS)
            with pe.Fori(0, N // 2) as i:
                for g in range(2 * PER):
                    pe.wait_ge(built, i * (2 * PER) + (g + 1))
                    pe.wait_ge(copied, i * (2 * PER) + (g + 1))
                    for t in range(GROUP):
                        mm = pe.matmul(prod[:, g % BUFS, t * P:(t + 1) * P], left[:, g % BUFS, t],
                                       right[:, g % BUFS, t], start=True, stop=True)
                    mm.then_inc(summed, 1)

        @block.scalar
        def _(act):
            act.sem_inc(copied, BUFS)
            with act.Fori(0, N // 2) as i:
                for u in range(2):
                    act.wait_ge(stored[u], i * 16 + 16)
                    by_token = stage[:, u].rearrange("p (j t) -> p t j", t=TB)
                    for g in range(PER):
                        n = u * PER + g
                        act.wait_ge(summed, i * (2 * PER) + (n + 1 + BUFS))
                        act.activation(by_token[:, g * GROUP:(g + 1) * GROUP, :],
                                       prod[:, n % BUFS].rearrange("p (t j) -> p t j", t=GROUP), ACT.Copy
                                       ).then_inc(copied, 1)


def experts(nc, hT, up, vp, gates, x2, w_row, out):
    GROUPS = NKEY // 2
    SEG = HALF // 2
    BANKS, OUTS = 4, 2 * NTH
    with ExitStack() as ctx:
        sb, ps, sem = scope(nc, ctx)
        acc = sb("ex_acc", [P, NTH, D])
        uraw, vraw = sb("ex_uraw", [P, 2, D]), sb("ex_vraw", [P, 2, D])
        uu = [sb(f"ex_u_{part}", [P, 2, D], F32R) for part in ("hi", "lo")]
        vv = [sb(f"ex_v_{part}", [P, 2, 2, D], F32R) for part in ("hi", "lo")]
        aa = [sb(f"ex_a_{part}", [P, 2, 2, HALF], F32R) for part in ("hi", "lo")]
        gt = sb("ex_gates", [P, 2, HALF // TB, 2 * TB])
        gl = sb("ex_gelu", [P, 2 * HALF])
        wrow = sb("ex_wrow", [P, D])
        ssq = sb("ex_ssq", [P, NTH])
        hps = ps("ex_h", [P, 2, 2, 512])
        ops_ = ps("ex_out", [P, BANKS, 512])
        u_in, v_in, g_in = pair_of(sem, "ex_u_in"), pair_of(sem, "ex_v_in"), pair_of(sem, "ex_g_in")
        acc_in, w_in, stored = sem("ex_acc_in"), sem("ex_w_in"), sem("ex_stored")
        u_hi, u_split, v_hi, v_split, h_done, gelu_done, a_ready, out_done, added, squared, var, root, normed, steps = (
            sem(f"ex_{n}") for n in ("u_hi", "u_split", "v_hi", "v_split", "h_done", "gelu", "a", "out_done", "added",
                                     "squared", "var", "root", "normed", "dve"))
        passed = sem("ex_passed")
        block = ctx.enter_context(nc.Block())
        A_CR, OUT_CR, ADD_CR = 2, 2 * OUTS, OUTS

        def sweep(eng, n_loop, first, body, last):
            with eng.Fori(0, 2) as s:
                first(s)
                with eng.Fori(0, n_loop) as i:
                    for u in range(2):
                        body(s, i, u)
                last(s)

        @block.sync
        def _(sp):
            sp.dma_start(wrow[:], rows_bcast(w_row, D)).then_inc(w_in, 16)

            def first(s):
                sp.wait_ge(stored, s * (16 * NTH) + 16 * NTH)
                sp.dma_start(acc[:], x2[bass.ds(s * HALF, HALF), :].rearrange("(t p) d -> p t d", p=P)
                             ).then_inc(acc_in, 16)

            def load(s, i, u):
                for c in range(2):
                    sp.wait_ge(u_split, s * (2 * GROUPS) + i * 4 + (2 * u + c + 1))
                    sp.dma_start(uraw[:, c], one(up, i * 4 + (2 * u + c))).then_inc(u_in[c], 16)
                for c in range(2):
                    sp.wait_ge(v_split, s * (2 * GROUPS) + i * 4 + (2 * u + c + 1))
                    sp.dma_start(vraw[:, c], one(vp, i * 4 + (2 * u + c))).then_inc(v_in[c], 16)
                sp.wait_ge(a_ready, s * (2 * GROUPS) + i * 4 + 2 * u)
                sp.dma_start(gt[:, u], gates[bass.ds(s * (HALF // TB), HALF // TB), :, bass.ds(i * (4 * TB) + u * (2 * TB), 2 * TB)]
                             .rearrange("b p n -> p b n")).then_inc(g_in[u], 16)
            sweep(sp, GROUPS // 2, first, load, lambda s: None)

        @block.tensor
        def _(pe):
            pe.sem_inc(h_done, 2)
            pe.sem_inc(out_done, OUT_CR)

            def hidden(s, i, o):
                for c in range(2):
                    n = s * (2 * GROUPS) + i * 4 + (2 * o + c)
                    pe.wait_ge(u_split, n + 3)
                    pe.wait_ge(gelu_done, n + 1)
                    for k in range(KD):
                        for m, (a, b) in enumerate(PRODUCTS):
                            for h in range(2):
                                mm = pe.matmul(hps[:, c, h, 0:SEG], uu[a][:, c, k * P:(k + 1) * P],
                                               hT[b][:, k, bass.ds(s * HALF + h * SEG, SEG)],
                                               start=(k + m == 0), stop=(k == KD - 1 and m == 2))
                    mm.then_inc(h_done, 1)

            def project(s, i, o):
                gb = o % 2
                n0 = s * (GROUPS * OUTS) + i * (2 * OUTS) + o * OUTS
                pe.wait_ge(a_ready, s * (2 * GROUPS) + i * 4 + (2 * o + 2 + A_CR))
                pe.wait_ge(v_split, s * (2 * GROUPS) + i * 4 + (2 * o + 2 + 2))
                for m in range(OUTS):
                    t, h = m // 2, m % 2
                    bank = (gb * OUTS + m) % BANKS
                    pe.wait_ge(added, n0 + (m + 1 - BANKS + ADD_CR))
                    for c in range(2):
                        for x, (a, b) in enumerate(PRODUCTS):
                            mm = pe.matmul(ops_[:, bank], aa[a][:, gb, c, t * P:(t + 1) * P],
                                           vv[b][:, gb, c, h * 512:(h + 1) * 512],
                                           start=(c + x == 0), stop=(c == 1 and x == 2))
                    mm.then_inc(out_done, 1)

            def body(s, i, u):
                hidden(s, i, u + 1)
                project(s, i, u)

            def last(s):
                hidden(s, GROUPS // 2 - 1, 1)
                project(s, GROUPS // 2 - 1, 0)
                project(s, GROUPS // 2 - 1, 1)
            sweep(pe, GROUPS // 2 - 1, lambda s: hidden(s, 0, 0), body, last)

        @block.scalar
        def _(act):
            act.sem_inc(gelu_done, 2)
            act.sem_inc(stored, 16 * NTH)

            def u_parts(s, i, o):
                for c in range(2):
                    act.wait_ge(u_in[c], s * (16 * GROUPS) + i * 32 + (16 * o + 16))
                    act.wait_ge(h_done, s * (2 * GROUPS) + i * 4 + (2 * o + c + 1))
                    act.activation(uu[0][:, c], uraw[:, c], ACT.Copy).then_inc(u_hi, 1)

            def v_parts(s, i, o):
                act.wait_ge(out_done, s * (GROUPS * OUTS) + i * (2 * OUTS) + (o + 1) * OUTS)
                for c in range(2):
                    act.wait_ge(v_in[c], s * (16 * GROUPS) + i * 32 + (16 * o + 16))
                    act.activation(vv[0][:, o % 2, c], vraw[:, c], ACT.Copy).then_inc(v_hi, 1)

            def gelus(s, i, o):
                for c in range(2):
                    n = s * (2 * GROUPS) + i * 4 + (2 * o + c)
                    act.wait_ge(h_done, n + 3)
                    act.wait_ge(a_ready, n + 1)
                    act.activation(gl[:, c * HALF:(c + 1) * HALF].rearrange("p (h t) -> p h t", h=2),
                                   hps[:, c, :, 0:SEG], ACT.Gelu).then_inc(gelu_done, 1)

            def step(s, i, o):
                gelus(s, i, o)
                u_parts(s, i, o + 1)
                v_parts(s, i, o + 1)

            def first(s):
                u_parts(s, 0, 0)
                v_parts(s, 0, 0)
                step(s, 0, 0)

            def last(s):
                gelus(s, GROUPS // 2 - 1, 1)
                act.wait_ge(added, s * (GROUPS * OUTS) + (GROUPS * OUTS + ADD_CR))
                for t in range(NTH):
                    act.wait_ge(squared, s * NTH + t + 1)
                    act.activation(gl[:, 0:D], acc[:, t, :], ACT.Square, accum_out=ssq[:, t:t + 1]).then_inc(squared, 1)
                act.wait_ge(var, s + 1)
                act.activation(ssq[:], ssq[:], ACT.Sqrt).then_inc(root, 1)
                for t in range(NTH):
                    act.wait_ge(normed, s * NTH + t + 1)
                    act.dma_start(out[bass.ds(s * HALF + t * P, P), :], acc[:, t, :]).then_inc(stored, 16)
            act.sem_inc(squared, 1)
            sweep(act, GROUPS // 2 - 1, first, lambda s, i, u: step(s, i, u + 1), last)
            act.wait_ge(stored, 16 * NTH * 3)

        @block.vector
        def _(dve):
            own = Steps(dve, steps)
            dve.sem_inc(u_split, 2)
            dve.sem_inc(v_split, 2)
            dve.sem_inc(a_ready, A_CR)
            dve.sem_inc(added, ADD_CR)

            def u_parts(s, i, o):
                for c in range(2):
                    dve.wait_ge(u_hi, s * (2 * GROUPS) + i * 4 + (2 * o + c + 1))
                    dve.tensor_tensor(uu[1][:, c], uraw[:, c], uu[0][:, c].bitcast(F32), ALU.subtract
                                      ).then_inc(u_split, 1)

            def v_parts(s, i, o):
                for c in range(2):
                    dve.wait_ge(v_hi, s * (2 * GROUPS) + i * 4 + (2 * o + c + 1))
                    dve.tensor_tensor(vv[1][:, o % 2, c], vraw[:, c], vv[0][:, o % 2, c].bitcast(F32), ALU.subtract
                                      ).then_inc(v_split, 1)

            def gated(s, i, o):
                gb = o % 2
                dve.wait_ge(g_in[gb], s * (8 * GROUPS) + i * 16 + (16 * (o // 2) + 16))
                dve.wait_ge(out_done, s * (GROUPS * OUTS) + i * (2 * OUTS) + (o + 1) * OUTS)
                for c in range(2):
                    dve.wait_ge(gelu_done, s * (2 * GROUPS) + i * 4 + (2 * o + c + 3))
                    g = gl[:, c * HALF:(c + 1) * HALF]
                    by_block = g.rearrange("p (b t) -> p b t", t=TB)
                    own.link(dve.tensor_tensor(by_block, by_block, gt[:, gb, :, c * TB:(c + 1) * TB], ALU.mult))
                    own.link(dve.tensor_copy(aa[0][:, gb, c], g))
                    dve.tensor_tensor(aa[1][:, gb, c], g, aa[0][:, gb, c].bitcast(F32), ALU.subtract
                                      ).then_inc(a_ready, 1)

            def adds(s, i, o):
                n0 = s * (GROUPS * OUTS) + i * (2 * OUTS) + o * OUTS
                for m in range(OUTS):
                    t, h = m // 2, m % 2
                    dve.wait_ge(out_done, n0 + (m + 1 + OUT_CR))
                    dve.wait_ge(added, n0 + (m + 1))
                    part = acc[:, t, h * 512:(h + 1) * 512]
                    dve.tensor_tensor(part, part, ops_[:, ((o % 2) * OUTS + m) % BANKS], ALU.add).then_inc(added, 1)

            def step(s, i, o):
                gated(s, i, o)
                u_parts(s, i, o + 1)
                adds(s, i, o - 1)
                v_parts(s, i, o + 1)

            with dve.Fori(0, 2) as s:
                own.enter(s, 4 * GROUPS + 1)
                u_parts(s, 0, 0)
                v_parts(s, 0, 0)
                gated(s, 0, 0)
                u_parts(s, 0, 1)
                v_parts(s, 0, 1)
                dve.wait_ge(acc_in, s * 16 + 16)
                dve.sem_inc(passed, 1)
                with dve.Fori(0, GROUPS // 2 - 1) as i:
                    own.enter(i, 8)
                    step(s, i, 1)
                    step(s, i, 2)
                own.leave(GROUPS // 2 - 1)
                gated(s, GROUPS // 2 - 1, 1)
                adds(s, GROUPS // 2 - 1, 0)
                adds(s, GROUPS // 2 - 1, 1)
                dve.wait_ge(squared, s * NTH + (NTH + 1))
                dve.tensor_scalar(ssq[:], ssq[:], 1.0 / D, EPS, ALU.mult, ALU.add).then_inc(var, 1)
                dve.wait_ge(root, s + 1)
                own.link(dve.reciprocal(ssq[:], ssq[:]))
                dve.wait_ge(w_in, 16)
                for t in range(NTH):
                    dve.scalar_tensor_tensor(acc[:, t, :], acc[:, t, :], ssq[:, t:t + 1], wrow[:],
                                             ALU.mult, ALU.mult).then_inc(normed, 1)
            own.leave(2)


def encoder_layer(nc, x, norm_mix, w_in, bias_tab, conv_w, conv_b, dt_bias, a_log, d_row, ssd_norm, w_out,
                  norm_ffn, w_query, keysT, up, vp, norm_final, consts, starts, iota, ident, out):
    projT = nc.dram_tensor("projT", [NB_IN, P, T], F32).ap()
    xbcT = nc.dram_tensor("xbcT", [8, P, T], F32).ap()
    mixT = nc.dram_tensor("mixT", [KD, P, T], F32).ap()
    x2 = nc.dram_tensor("x2", [T, D], F32).ap()
    gates = nc.dram_tensor("gates", [T // TB, P, P * TB], F32).ap()

    def parts_of(ctx, name):
        return [ctx.enter_context(nc.sbuf_tensor(f"{name}_{part}", [P, KD, T], F32R)) for part in ("hi", "lo")]

    with ExitStack() as ctx:
        hT = parts_of(ctx, "hm")
        norm_inputs(nc, x, norm_mix, ident, hT)
        project_in(nc, w_in, hT, projT)
    conv_silu(nc, projT, conv_w, conv_b, xbcT)
    attention(nc, projT, bias_tab, ident, mixT)
    ssd(nc, projT, xbcT, dt_bias, a_log, d_row, ssd_norm, consts, mixT)
    with ExitStack() as ctx:
        hT = parts_of(ctx, "hf")
        project_out(nc, mixT, w_out, x, norm_ffn, ident, x2, hT)
        with ExitStack() as tables:
            tabsT = [tables.enter_context(nc.sbuf_tensor(f"tabsT{n}", [P, T], F32)) for n in range(3)]
            with ExitStack() as c:
                tabs = [c.enter_context(nc.sbuf_tensor(f"tabs{n}", [P, NT, P], F32)) for n in range(3)]
                retrieve(nc, hT, w_query, keysT, starts, tabs)
                turn_tables(nc, tabs, ident, tabsT)
            gate_table(nc, tabsT, iota, gates)
        experts(nc, hT, up, vp, gates, x2, norm_final, out)


def _bias_layout(np, rpb):
    q, k = np.arange(GRID_W)[:, None], np.arange(GRID_W)[None]
    first = np.clip(q - 8, 0, GRID_W - 16)
    inside = (k >= first) & (k < first + 16)
    dc = np.clip(k - q, -15, 15) + 15
    tab = np.full((HEADS, P, 25, GRID_W), -1.0e30, np.float32)
    for half in range(2):
        for e in range(25):
            dr = (e if e < 16 else e - 13) - half
            if 0 <= dr <= 14 and (e, half) not in ((16, 1), (24, 0)):
                tab[:, 64 * half:64 * half + 64, e] = np.where(inside, rpb[:, dr][:, dc], np.float32(-1.0e30))
    return tab.reshape(HEADS, P, 25 * GRID_W)


def kernel(**inputs):
    import numpy as np
    import concourse.bacc as _bacc
    from concourse.bass_utils import run_bass_kernel_spmd as _run

    a = {k: np.asarray(v) for k, v in inputs.items()}
    w_in = np.zeros((D, NB_IN * P), np.float32)
    w_in[:, :a["w_in"].shape[2]] = a["w_in"][0]
    u, l = np.arange(P)[:, None], np.arange(P)[None]
    s = np.array(row_starts(), np.float32)
    arrays = {
        "x": np.concatenate([a["x_prompt"][0], a["x_sample"][0]], 0),
        "norm_mix": a["norm_mix_w"][0],
        "w_in": w_in.reshape(KD, P, NB_IN, P).transpose(2, 1, 0, 3).reshape(NB_IN, P, KD * P),
        "bias_tab": _bias_layout(np, a["rpb"][0]),
        "conv_w": a["conv_w"][0].reshape(CONV_TAPS, 8, P).transpose(2, 1, 0).reshape(P, 8 * CONV_TAPS),
        "conv_b": a["conv_b"][0].reshape(8, P).T,
        "dt_bias": a["dt_bias"][0].reshape(2 * HEADS),
        "a_log": a["a_log"][0].reshape(2 * HEADS),
        "d_row": np.repeat(a["d_skip"][0], HD),
        "ssd_norm": a["ssd_norm_w"][0],
        "w_out": a["w_out"][0].reshape(KD, P, D),
        "norm_ffn": a["norm_ffn_w"][0],
        "w_query": a["w_query"][0].reshape(KD, P, 2 * HEADS, P).transpose(2, 1, 0, 3).reshape(2 * HEADS, P, KD * P),
        "keysT": a["sub_keys"][0].reshape(2 * HEADS, NKEY, P).transpose(0, 2, 1),
        "up": a["expert_u"][0].reshape(NKEY, NKEY, KD, P).transpose(1, 3, 2, 0).reshape(NKEY, P, D),
        "vp": a["expert_v"][0].reshape(NKEY, NKEY, D).transpose(1, 0, 2),
        "norm_final": a["norm_final_w"],
        "consts": np.stack([u == l, u <= l, u > l, u >= l, u < l, u >= 0 * l], 1).astype(np.float32),
        "starts": np.concatenate([s, np.diff(s, prepend=0), np.arange(TOPK)]).astype(np.float32),
        "iota": np.tile(np.arange(P, dtype=np.float32), (P, 1)),
        "ident": np.eye(P, dtype=np.float32),
    }
    nc = _bacc.Bacc("TRN2", target_bir_lowering=False, num_devices=1)
    feeds, args = {}, {}
    for name, v in arrays.items():
        v = np.ascontiguousarray(v)
        feeds[f"in_{name}"] = v
        args[name] = nc.dram_tensor(f"in_{name}", v.shape, mybir.dt.from_np(v.dtype), kind="ExternalInput").ap()
    args["out"] = nc.dram_tensor("out_y", (T, D), F32, kind="ExternalOutput").ap()
    encoder_layer(nc, **args)
    y = _run(nc, [feeds], core_ids=[0]).results[0]["out_y"]
    return y[None, :SEQ_P], y[None, SEQ_P:]
```

```python
from contextlib import ExitStack

import concourse.bass as bass
from concourse import mybir

ALU = mybir.AluOpType
ACT = mybir.ActivationFunctionType
AX = mybir.AxisListType
F32 = mybir.dt.float32
F32R = mybir.dt.float32r
BF16 = mybir.dt.bfloat16
U32 = mybir.dt.uint32

P = 128
D = 1024
KD = D // P
SEQ_P, SEQ_S = 256, 1024
T = SEQ_P + SEQ_S
NT = T // P
SEGS = [(0, 512), (512, 512), (1024, 256)]
EPS = 1e-6
GRID_W = 64
HEADS = 8
HD = 64
SSD_W = HEADS * HD
NB_IN = 25
BLK_Z, BLK_XBC, BLK_DT = 12, 16, 24
CONV_TAPS = 5
PAD_T = T + 6
CONV_T = T + 2
BIAS_GEN, BIAS_INT = 16 * GRID_W, 9 * GRID_W
TOPK = 16
NKEY = 128
LOWEST = -3.0e38
HALF = T // 2
NTH = HALF // P
TB = 64
PRODUCTS = [(0, 0), (1, 0), (0, 1)]


class Steps:

    def __init__(self, eng, sem):
        self.eng, self.sem, self.base, self.k, self.outer = eng, sem, 0, 0, []

    def enter(self, i, per):
        self.outer.append((self.base, self.k, per))
        self.base, self.k = i * per + self.base + self.k, 0

    def leave(self, n):
        base, k, per = self.outer.pop()
        assert self.k == per, (self.k, per)
        self.base, self.k = base, k + n * per

    def add(self, ins):
        self.k += 1
        ins.then_inc(self.sem, 1)

    def wait(self):
        self.eng.wait_ge(self.sem, self.base + self.k)

    def link(self, ins):
        self.add(ins)
        self.wait()


def scope(nc, ctx):
    sems = []

    def sb(name, shape, dt=F32):
        return ctx.enter_context(nc.sbuf_tensor(name, shape, dt))

    def ps(name, shape, dt=F32):
        return ctx.enter_context(nc.psum_tensor(name, shape, dt))

    def sem(name):
        sems.append(nc.alloc_semaphore(name))
        return sems[-1]

    def clear():
        if sems:
            nc.clear_and_free_semaphores(sems)
            nc.all_engine_barrier()

    ctx.callback(clear)
    return sb, ps, sem


def pair_of(sem, name):
    return [sem(name + "0"), sem(name + "1")]


def rounds(eng, n, step):
    with eng.Fori(0, n // 2) as i:
        for u in range(2):
            step(i, u)
    if n % 2:
        step(n // 2, 0)


def rows_bcast(dram, n, parts=P):
    return bass.AP(tensor=dram.tensor, offset=dram.offset, ap=[[0, parts], [1, n]])


def one(ap, r):
    return ap[bass.ds(r, 1)].rearrange("o p c -> p (o c)")


def norm_inputs(nc, x, w_row, ident, hT):
    with ExitStack() as ctx:
        sb, ps, sem = scope(nc, ctx)
        xall = sb("n1_x", [P, NT, D])
        junk = sb("n1_junk", [P, D])
        wrow = sb("n1_w", [P, D])
        idm = sb("n1_ident", [P, P])
        ssq = sb("n1_ssq", [P, NT])
        rstd = sb("n1_rstd", [P, NT])
        xs = sb("n1_xs", [P, 2, D])
        xT = ps("n1_xT", [P, 2, D])
        consts_in, x_in = sem("n1_consts_in"), [sem(f"n1_x_in{t}") for t in range(NT)]
        squared, var_ready, root_ready = sem("n1_squared"), sem("n1_var"), sem("n1_root")
        dve_steps, scaled, turned = sem("n1_dve"), sem("n1_scaled"), sem("n1_turned")
        hi_done, lo_done = sem("n1_hi"), sem("n1_lo")
        block = ctx.enter_context(nc.Block())

        @block.sync
        def _(sp):
            for t in range(NT):
                sp.dma_start(xall[:, t, :], x[t * P:(t + 1) * P, :]).then_inc(x_in[t], 16)
            sp.dma_start(wrow[:], rows_bcast(w_row, D)).then_inc(consts_in, 16)
            sp.dma_start(idm[:], ident).then_inc(consts_in, 16)

        @block.scalar
        def _(act):
            for t in range(NT):
                act.wait_ge(x_in[t], 16)
                if t:
                    act.wait_ge(squared, t)
                act.activation(junk[:], xall[:, t, :], ACT.Square, accum_out=ssq[:, t:t + 1]).then_inc(squared, 1)
            act.wait_ge(var_ready, 1)
            act.activation(rstd[:], ssq[:], ACT.Sqrt).then_inc(root_ready, 1)
            with act.Fori(0, NT // 2) as i:
                for u in range(2):
                    act.wait_ge(turned, i * 2 + (u + 1))
                    act.activation(hT[0][:, :, bass.ds(i * (2 * P) + u * P, P)],
                                   xT[:, u].rearrange("p (k t) -> p k t", k=KD), ACT.Copy).then_inc(hi_done, 1)

        @block.vector
        def _(dve):
            own = Steps(dve, dve_steps)
            dve.wait_ge(squared, NT)
            dve.tensor_scalar(ssq[:], ssq[:], 1.0 / D, EPS, ALU.mult, ALU.add).then_inc(var_ready, 1)
            dve.wait_ge(root_ready, 1)
            own.link(dve.reciprocal(rstd[:], rstd[:]))
            dve.wait_ge(consts_in, 32)
            with dve.Fori(0, NT // 2) as i:
                for u in range(2):
                    dve.scalar_tensor_tensor(xs[:, u], one_of(xall, i * 2 + u),
                                             rstd[:, bass.ds(i * 2 + u, 1)], wrow[:],
                                             ALU.mult, ALU.mult).then_inc(scaled, 1)
                for u in range(2):
                    dve.wait_ge(hi_done, i * 2 + (u + 1))
                    tok = bass.ds(i * (2 * P) + u * P, P)
                    dve.tensor_tensor(hT[1][:, :, tok], xT[:, u].rearrange("p (k t) -> p k t", k=KD),
                                      hT[0][:, :, tok].bitcast(F32), ALU.subtract).then_inc(lo_done, 1)

        @block.tensor
        def _(pe):
            pe.sem_inc(lo_done, 2)
            pe.wait_ge(consts_in, 32)
            with pe.Fori(0, NT // 2) as i:
                for u in range(2):
                    pe.wait_ge(scaled, i * 2 + (u + 1))
                    pe.wait_ge(lo_done, i * 2 + (u + 1))
                    for k in range(KD):
                        mm = pe.transpose(xT[:, u, k * P:(k + 1) * P], xs[:, u, k * P:(k + 1) * P], idm[:])
                    mm.then_inc(turned, 1)


def one_of(ap, r):
    return ap[:, bass.ds(r, 1), :].rearrange("p o d -> p (o d)")


def split(dve, own, hi, lo, raw):
    own.link(dve.tensor_copy(hi, raw))
    return dve.tensor_tensor(lo, raw, hi.bitcast(F32), ALU.subtract)


def project_in(nc, w_blocks, hT, conv_w, conv_b, projT, xbcT):
    PLAIN, CONV = BLK_XBC, 8
    with ExitStack() as ctx:
        sb, ps, sem = scope(nc, ctx)
        wraw = sb("pi_wraw", [P, 2, KD * P])
        w = [sb(f"pi_w_{part}", [P, 2, KD * P], F32R) for part in ("hi", "lo")]
        res = sb("pi_out", [P, 2, T])
        taps, bias = sb("pi_taps", [P, CONV * CONV_TAPS]), sb("pi_bias", [P, CONV])
        xp = sb("pi_x", [P, 2, PAD_T])
        y, z = sb("pi_y", [P, 2, CONV_T]), sb("pi_z", [P, 2, CONV_T])
        acc = ps("pi_acc", [P, 2, 3 * 512])
        w_in, consts_in = pair_of(sem, "pi_w_in"), sem("pi_consts_in")
        split_done, dve_steps = sem("pi_split"), sem("pi_dve")
        summed, copied, pads, convolved, squashed = (
            sem(f"pi_{n}") for n in ("summed", "copied", "pads", "conv", "silu"))
        stored, conv_stored = pair_of(sem, "pi_stored"), pair_of(sem, "pi_cstored")
        block = ctx.enter_context(nc.Block())

        @block.sync
        def _(sp):
            def load(r, u):
                sp.wait_ge(split_done, r * 2 + (u + 1))
                sp.dma_start(wraw[:, u], one(w_blocks, r * 2 + u)).then_inc(w_in[u], 16)
            sp.dma_start(taps[:], conv_w).then_inc(consts_in, 16)
            sp.dma_start(bias[:], conv_b).then_inc(consts_in, 16)
            rounds(sp, NB_IN, load)

        @block.vector
        def _(dve):
            own = Steps(dve, dve_steps)
            dve.sem_inc(split_done, 2)
            dve.memset(xp[:], 0.0).then_inc(pads, 1)

            def parts(r, u):
                dve.wait_ge(w_in[u], r * 16 + 16)
                dve.wait_ge(summed, r * 2 + (u + 1))
                split(dve, own, w[0][:, u], w[1][:, u], wraw[:, u]).then_inc(split_done, 1)

            def convolve(i, u):
                b = i * 2 + u
                dve.wait_ge(copied, b + (PLAIN + 3))
                dve.wait_ge(squashed, b + 1)
                tap = [taps[:, bass.ds(i * (2 * CONV_TAPS) + (u * CONV_TAPS + j), 1)] for j in range(CONV_TAPS)]
                own.link(dve.tensor_scalar(y[:, u], xp[:, u, 0:CONV_T], tap[0], None, ALU.mult))
                for j in range(1, CONV_TAPS):
                    ins = dve.scalar_tensor_tensor(y[:, u], xp[:, u, j:j + CONV_T], tap[j], y[:, u],
                                                   ALU.mult, ALU.add)
                    if j < CONV_TAPS - 1:
                        own.link(ins)
                    else:
                        ins.then_inc(convolved, 1)

            with dve.Fori(0, PLAIN // 2) as i:
                own.enter(i, 2)
                for u in range(2):
                    parts(i, u)
            own.leave(PLAIN // 2)
            parts(PLAIN // 2, 0)
            dve.wait_ge(consts_in, 32)
            dve.sem_inc(pads, 1)
            with dve.Fori(0, CONV // 2) as i:
                own.enter(i, 2 * CONV_TAPS)
                for u in range(2):
                    parts(i + (PLAIN // 2 + u), 1 - u)
                    convolve(i, u)
            own.leave(CONV // 2)

        @block.tensor
        def _(pe):
            pe.sem_inc(summed, 2)

            def block_products(r, u):
                pe.wait_ge(split_done, r * 2 + (u + 3))
                pe.wait_ge(copied, r * 2 + (u + 1))
                for k in range(KD):
                    for n, (a, b) in enumerate(PRODUCTS):
                        for t0, tn in SEGS:
                            mm = pe.matmul(acc[:, u, t0:t0 + tn], w[a][:, u, k * P:(k + 1) * P],
                                           hT[b][:, k, t0:t0 + tn], start=(k + n == 0),
                                           stop=(k == KD - 1 and n == 2))
                mm.then_inc(summed, 1)
            rounds(pe, NB_IN, block_products)

        @block.scalar
        def _(act):
            act.sem_inc(copied, 2)
            act.sem_inc(squashed, 2)
            for u in range(2):
                act.sem_inc(stored[u], 16)
                act.sem_inc(conv_stored[u], 32)

            def copy_out(r, u, turns):
                act.wait_ge(summed, r * 2 + (u + 3))
                act.wait_ge(stored[u], turns * 16 + 16)
                act.activation(res[:, u], acc[:, u, 0:T], ACT.Copy).then_inc(copied, 1)
                act.wait_ge(copied, r * 2 + (u + 3))
                act.dma_start(one(projT, r * 2 + u), res[:, u]).then_inc(stored[u], 16)

            with act.Fori(0, PLAIN // 2) as i:
                for u in range(2):
                    copy_out(i, u, i)
            act.wait_ge(pads, 2)
            with act.Fori(0, CONV // 2) as i:
                for u in range(2):
                    b = i * 2 + u
                    act.wait_ge(summed, b + (PLAIN + 3))
                    act.activation(xp[:, u, 2:2 + SEQ_P], acc[:, u, 0:SEQ_P], ACT.Copy)
                    act.activation(xp[:, u, 4 + SEQ_P:4 + T], acc[:, u, SEQ_P:T], ACT.Copy).then_inc(copied, 1)
                    act.wait_ge(convolved, b + 1)
                    act.wait_ge(conv_stored[u], i * 32 + 32)
                    act.activation(z[:, u], y[:, u], ACT.Silu, bias=bias[:, bass.ds(b, 1)]).then_inc(squashed, 1)
                    act.wait_ge(squashed, b + 3)
                    dst = one(xbcT, b)
                    act.dma_start(dst[:, 0:SEQ_P], z[:, u, 0:SEQ_P]).then_inc(conv_stored[u], 16)
                    act.dma_start(dst[:, SEQ_P:T], z[:, u, SEQ_P + 2:CONV_T]).then_inc(conv_stored[u], 16)
            copy_out(NB_IN // 2, 0, PLAIN // 2)
            act.wait_ge(stored[0], 16 * (2 + PLAIN // 2))
            act.wait_ge(stored[1], 16 * (1 + PLAIN // 2))
            for u in range(2):
                act.wait_ge(conv_stored[u], 32 * (1 + CONV // 2))


def attention_tiles():
    tiles = [(0, 0, 4 * GRID_W, 7 * GRID_W), (P, 0, 4 * GRID_W, 5 * GRID_W)]
    rows = SEQ_S // GRID_W
    for r in range(0, rows, 2):
        first = min(max(r - 4, 0), rows - 8)
        last = min(max(r + 1 - 4, 0), rows - 8) + 8
        col = BIAS_GEN if last - first == 9 else (first - r + 7) * GRID_W
        tiles.append((SEQ_P + r * GRID_W, SEQ_P + first * GRID_W, (last - first) * GRID_W, col))
    return tiles


def attention(nc, projT, bias_tab, ident, mixT):
    tiles = attention_tiles()
    NTI = len(tiles)
    KMAX = 640
    heads_in = projT.rearrange("b (h p) t -> (b h) p t", h=2)
    heads_out = mixT.rearrange("b (h p) t -> (b h) p t", h=2)
    with ExitStack() as ctx:
        sb, ps, sem = scope(nc, ctx)
        idm = sb("at_ident", [P, P])
        qraw, kraw = sb("at_qraw", [P, T]), sb("at_kraw", [P, T])
        q2, k2, klo = (sb(f"at_{n}", [P, 2, T], F32R) for n in ("q2", "k2", "klo"))
        vT = sb("at_vT", [HD, 2, T])
        bias = sb("at_bias", [P, 2, BIAS_GEN + BIAS_INT])
        v = sb("at_vtok", [P, 2, NT * HD])
        logits = sb("at_logits", [P, 2, KMAX])
        probs = sb("at_probs", [P, 2, KMAX])
        probsT = sb("at_probsT", [P, 2, KMAX])
        outT = sb("at_outT", [HD, 2, T])
        top, total, inv = sb("at_max", [P, 2]), sb("at_sum", [P, 2]), sb("at_inv", [P, 2])
        scores = ps("at_scores", [P, 2, 2, 512])
        turned = ps("at_turned", [P, 1024])
        oT = ps("at_oT", [P, 2, 512])
        ident_in, qk_in = sem("at_ident_in"), sem("at_qk_in")
        head_in, stored = pair_of(sem, "at_head_in"), pair_of(sem, "at_stored")
        head_done = sem("at_head_done")
        hi_ready, qk_ready = sem("at_hi"), sem("at_qk")
        v_turned, v_ready = sem("at_v_turned"), sem("at_v_ready")
        scored, biased = sem("at_scored"), sem("at_biased")
        max_ready, exp_ready, normed = sem("at_max_ready"), sem("at_exp"), sem("at_normed")
        p_turned, pT_ready = sem("at_p_turned"), sem("at_pT")
        weighed, o_ready = sem("at_weighed"), sem("at_o")
        dve_steps, passed = sem("at_dve"), sem("at_passed")
        block = ctx.enter_context(nc.Block())

        def cut(n):
            kn = tiles[n][2]
            return (2, kn // 2) if kn > 512 else (1, kn)

        def keyed(ap, n):
            pieces, w = cut(n)
            return ap.rearrange("p (c k) -> p c k", c=pieces)

        @block.sync
        def _(sp):
            sp.dma_start(idm[:], ident).then_inc(ident_in, 16)

            def load_qk(h):
                for half in (0, HD):
                    sp.dma_start(qraw[half:half + HD, :], one(heads_in, h)).then_inc(qk_in, 16)
                    sp.dma_start(kraw[half:half + HD, :], one(heads_in, h + HEADS)).then_inc(qk_in, 16)

            load_qk(0)
            with sp.Fori(0, HEADS // 2) as i:
                for u in range(2):
                    sp.wait_ge(qk_ready, i * 2 + (u + 2))
                    load_qk(i * 2 + (u + 1))
                    sp.wait_ge(head_done, i * 2 + (u + 1))
                    sp.dma_start(vT[:, u], one(heads_in, i * 2 + (16 + u))).then_inc(head_in[u], 16)
                    sp.dma_start(bias[:, u], one(bias_tab, i * 2 + u)).then_inc(head_in[u], 16)

        @block.tensor
        def _(pe):
            pe.sem_inc(head_done, 2)
            pe.wait_ge(ident_in, 16)
            with pe.Fori(0, HEADS // 2) as i:
                for u in range(2):
                    n0 = i * (2 * NTI) + u * NTI

                    def score(n):
                        q0, k0, kn, _ = tiles[n]
                        pe.wait_ge(biased, n0 + (n + 1))
                        pieces, w = cut(n)
                        for c in range(pieces):
                            keys = slice(k0 + c * w, k0 + (c + 1) * w)
                            pe.matmul(scores[:, n % 2, c, 0:w], q2[:, u, q0:q0 + P], k2[:, u, keys],
                                      start=True, stop=False)
                            mm = pe.matmul(scores[:, n % 2, c, 0:w], q2[0:HD, u, q0:q0 + P], klo[0:HD, u, keys],
                                           start=False, stop=True)
                        mm.then_inc(scored, 1)

                    def turn(n):
                        kn = tiles[n][2]
                        pe.wait_ge(normed, n0 + (n + 1))
                        if n == 0:
                            pe.wait_ge(v_ready, i * 2 + (u + 1))
                        else:
                            pe.wait_ge(pT_ready, n0 + (n + 1))
                        for c in range(0, kn, P):
                            w = min(P, kn - c)
                            mm = pe.transpose(turned[0:w, c:c + P], probs[:, n % 2, c:c + w], idm[:])
                        mm.then_inc(p_turned, 1)

                    def weigh(n):
                        q0, k0, kn, _ = tiles[n]
                        pe.wait_ge(pT_ready, n0 + (n + 2))
                        pe.wait_ge(o_ready, n0 + (n + 1))
                        for c in range(0, kn, P):
                            w = min(P, kn - c)
                            vt = (k0 + c) // P
                            mm = pe.matmul(oT[0:HD, n % 2, 0:P], v[0:w, u, vt * HD:(vt + 1) * HD],
                                           probsT[0:w, n % 2, c:c + P], start=(c == 0), stop=(c + P >= kn))
                        mm.then_inc(weighed, 1)

                    pe.wait_ge(qk_ready, i * 2 + (u + 2))
                    score(0)
                    score(1)
                    pe.wait_ge(head_in[u], i * 32 + 32)
                    pe.wait_ge(pT_ready, n0 + 1)
                    pe.sem_inc(passed, 1)
                    for t in range(NT):
                        mm = pe.transpose(turned[:, t * HD:(t + 1) * HD], vT[:, u, t * P:(t + 1) * P],
                                          idm[0:HD, 0:HD])
                    mm.then_inc(v_turned, 1)
                    for n in range(NTI):
                        turn(n)
                        if n + 2 < NTI:
                            score(n + 2)
                        weigh(n)
                    pe.wait_ge(weighed, n0 + NTI)
                    pe.sem_inc(head_done, 1)

        @block.vector
        def _(dve):
            own = Steps(dve, dve_steps)
            dve.sem_inc(qk_ready, 1)
            dve.sem_inc(biased, 2)
            dve.sem_inc(o_ready, 2)
            dve.sem_inc(stored[0], 16)
            dve.sem_inc(stored[1], 16)

            def lows(h, u):
                dve.wait_ge(hi_ready, h + 1)
                own.add(dve.tensor_tensor(q2[HD:P, u], qraw[HD:P, :], q2[HD:P, u].bitcast(F32), ALU.subtract))
                own.link(dve.tensor_tensor(klo[0:HD, u], kraw[0:HD, :], k2[0:HD, u].bitcast(F32), ALU.subtract))
                dve.sem_inc(qk_ready, 1)

            lows(0, 0)
            with dve.Fori(0, HEADS // 2) as i:
                own.enter(i, 2 * NTI + 4)
                for u in range(2):
                    n0 = i * (2 * NTI) + u * NTI

                    def bias_and_max(n):
                        _, _, kn, col = tiles[n]
                        pieces, w = cut(n)
                        dve.wait_ge(scored, n0 + (n + 1))
                        dve.wait_ge(exp_ready, n0 + (n + 1))
                        if n == 0:
                            dve.wait_ge(head_in[u], i * 32 + 32)
                        dve.scalar_tensor_tensor(keyed(logits[:, n % 2, 0:kn], n), scores[:, n % 2, 0:pieces, 0:w],
                                                 HD ** -0.5, keyed(bias[:, u, col:col + kn], n),
                                                 ALU.mult, ALU.add).then_inc(biased, 1)
                        dve.wait_ge(biased, n0 + (n + 3))
                        dve.tensor_reduce(top[:, n % 2:n % 2 + 1], logits[:, n % 2, 0:kn], AX.X, ALU.max,
                                          negate=True).then_inc(max_ready, 1)

                    def norm(n):
                        _, _, kn, _ = tiles[n]
                        dve.wait_ge(exp_ready, n0 + (n + 3))
                        own.link(dve.reciprocal(inv[:, n % 2:n % 2 + 1], total[:, n % 2:n % 2 + 1]))
                        dve.tensor_scalar(probs[:, n % 2, 0:kn], probs[:, n % 2, 0:kn], inv[:, n % 2:n % 2 + 1],
                                          None, ALU.mult).then_inc(normed, 1)

                    def take(n):
                        q0 = tiles[n][0]
                        dve.wait_ge(weighed, n0 + (n + 1))
                        if n == 0:
                            dve.wait_ge(stored[u], i * 16 + 16)
                        dve.tensor_copy(outT[:, u, q0:q0 + P], oT[0:HD, n % 2, 0:P]).then_inc(o_ready, 1)

                    bias_and_max(0)
                    bias_and_max(1)
                    norm(0)
                    dve.wait_ge(v_turned, i * 2 + (u + 1))
                    dve.wait_ge(head_done, i * 2 + (u + 1))
                    dve.tensor_copy(v[:, u], turned[:, 0:NT * HD]).then_inc(v_ready, 1)
                    for n in range(NTI):
                        if n + 1 < NTI:
                            norm(n + 1)
                        if n + 2 < NTI:
                            bias_and_max(n + 2)
                        if n:
                            take(n - 1)
                        if n == 4:
                            lows(i * 2 + (u + 1), 1 - u)
                    take(NTI - 1)
            own.leave(HEADS // 2)

        @block.scalar
        def _(act):
            act.sem_inc(exp_ready, 2)
            act.sem_inc(pT_ready, 1)

            def highs(h, u):
                act.wait_ge(qk_in, h * 64 + 64)
                act.wait_ge(head_done, h + 1)
                act.activation(q2[:, u], qraw[:], ACT.Copy)
                act.activation(k2[:, u], kraw[:], ACT.Copy).then_inc(hi_ready, 1)

            highs(0, 0)
            with act.Fori(0, HEADS // 2) as i:
                for u in range(2):
                    n0 = i * (2 * NTI) + u * NTI

                    def exp(n):
                        kn = tiles[n][2]
                        act.wait_ge(max_ready, n0 + (n + 1))
                        act.wait_ge(p_turned, n0 + (n - 1)) if n > 1 else act.wait_ge(pT_ready, n0 + 1)
                        act.activation(probs[:, n % 2, 0:kn], logits[:, n % 2, 0:kn], ACT.Exp,
                                       bias=top[:, n % 2:n % 2 + 1], accum_out=total[:, n % 2:n % 2 + 1]
                                       ).then_inc(exp_ready, 1)

                    def copy_turned(n):
                        kn = tiles[n][2]
                        full = kn // P * P
                        act.wait_ge(p_turned, n0 + (n + 1))
                        act.wait_ge(o_ready, n0 + (n + 1))
                        ins = act.activation(probsT[:, n % 2, 0:full], turned[:, 0:full], ACT.Copy)
                        if kn > full:
                            ins = act.activation(probsT[0:kn - full, n % 2, full:full + P],
                                                 turned[0:kn - full, full:full + P], ACT.Copy)
                        ins.then_inc(pT_ready, 1)

                    exp(0)
                    exp(1)
                    for n in range(NTI):
                        copy_turned(n)
                        if n + 2 < NTI:
                            exp(n + 2)
                        if n == 3:
                            highs(i * 2 + (u + 1), 1 - u)
                    act.wait_ge(o_ready, n0 + (NTI + 2))
                    act.dma_start(one(heads_out, i * 2 + u), outT[:, u]).then_inc(stored[u], 16)
            for u in range(2):
                act.wait_ge(stored[u], 16 * (1 + HEADS // 2))


C_IDENT, C_LE, C_GT, C_GE, C_LT, C_ONES = range(6)
CHUNKS = [range(0, SEQ_P // P), range(SEQ_P // P, NT)]
HB = HEADS * NT
LOG1P_TERMS = 9


def bc(ap, n):
    return ap.unsqueeze(3).to_broadcast([ap.shape[0], ap.shape[1], ap.shape[2], n])


def ssd(nc, projT, xbcT, dt_bias, a_log, d_row, norm_row, consts, mixT):
    G = HEADS // 2
    with ExitStack() as ctx:
        sb, _, sem = scope(nc, ctx)
        cm = sb("sd_consts", [P, 6, P])
        xtok = sb("sd_x", [P, NT, SSD_W])
        zt = sb("sd_z", [P, NT, SSD_W])
        dt = sb("sd_dt", [P, NT, 2, HEADS])
        adt = sb("sd_adt", [P, NT, 2, HEADS])
        decay = sb("sd_decay", [P, 5, NT, 2, HEADS])
        wst = sb("sd_wst", [P, NT, 2, HEADS])
        entering = [sb(f"sd_ent{d}", [P, NT, SSD_W]) for d in range(2)]
        y = sb("sd_y", [P, NT, SSD_W])
        states = [sb("sd_st0", [P, NT, SSD_W]), y]
        ssq = sb("sd_ssq", [P, NT])
        nrow = sb("sd_nrow", [P, SSD_W])
        drow = sb("sd_drow", [P, SSD_W])

        with ExitStack() as c0:
            sb, ps, sem = scope(nc, c0)
            dtT = sb("s0_dtT", [HEADS, T])
            bias = sb("s0_bias", [P, 2, HEADS])
            alog = sb("s0_alog", [P, 2, HEADS])
            raw, u, t, t2, s = (sb(f"s0_{n}", [P, NT, 2, HEADS]) for n in ("raw", "u", "t", "t2", "s"))
            dps = ps("s0_dt", [P, NT, HEADS])
            cum = ps("s0_cum", [P, 2, 512])
            loaded, turned, steps = sem("s0_in"), sem("s0_turned"), sem("s0_dve")
            neg_ready, exped, adt_ready, summed, dec_ready, a_exp = (
                sem(f"s0_{n}") for n in ("neg", "exped", "adt", "summed", "dec", "aexp"))
            block = c0.enter_context(nc.Block())

            @block.sync
            def _(sp):
                sp.dma_start(cm[:], consts).then_inc(loaded, 16)
                sp.dma_start(dtT[:], projT[BLK_DT, 0:HEADS, :]).then_inc(loaded, 16)
                sp.dma_start(bias[:].rearrange("p d h -> p (d h)"), rows_bcast(dt_bias, 2 * HEADS)).then_inc(loaded, 16)
                sp.dma_start(alog[:].rearrange("p d h -> p (d h)"), rows_bcast(a_log, 2 * HEADS)).then_inc(loaded, 16)
                sp.dma_start(drow[:], rows_bcast(d_row, SSD_W)).then_inc(loaded, 16)
                sp.dma_start(nrow[:], rows_bcast(norm_row, SSD_W)).then_inc(loaded, 16)

            @block.tensor
            def _(pe):
                pe.wait_ge(loaded, 96)
                for c in range(NT):
                    mm = pe.transpose(dps[:, c], dtT[:, c * P:(c + 1) * P], cm[0:HEADS, C_IDENT, 0:HEADS])
                mm.then_inc(turned, 1)
                pe.wait_ge(adt_ready, 1)
                flat = adt[:].rearrange("p c d h -> p (c d h)")
                n = 2 * HB
                for m, mask in enumerate((C_LE, C_GT, C_GE, C_LT, C_ONES)):
                    mm = pe.matmul(cum[:, m // 3, (m % 3) * n:(m % 3 + 1) * n], cm[:, mask], flat, start=True, stop=True)
                mm.then_inc(summed, 1)

            @block.vector
            def _(dve):
                own = Steps(dve, steps)
                dve.wait_ge(turned, 1)
                for d in range(2):
                    ins = dve.tensor_tensor(raw[:, :, d], dps[:], bias[:, d].unsqueeze(1).to_broadcast([P, NT, HEADS]),
                                            ALU.add)
                    own.add(ins)
                own.wait()
                own.link(dve.tensor_scalar(t[:], raw[:], -1.0, None, ALU.mult))
                dve.tensor_tensor(u[:], raw[:], t[:], ALU.min).then_inc(neg_ready, 1)
                dve.wait_ge(exped, 1)
                own.link(dve.tensor_scalar(t[:], u[:], 2.0, None, ALU.add))
                own.link(dve.reciprocal(t2[:], t[:]))
                own.link(dve.tensor_tensor(t[:], u[:], t2[:], ALU.mult))
                own.link(dve.tensor_tensor(t2[:], t[:], t[:], ALU.mult))
                own.link(dve.tensor_scalar(s[:], t2[:], 1.0 / (2 * LOG1P_TERMS + 1), None, ALU.mult))
                for m in range(LOG1P_TERMS - 1, 0, -1):
                    own.link(dve.scalar_tensor_tensor(s[:], s[:], 1.0 / (2 * m + 1), t2[:], ALU.add, ALU.mult))
                own.link(dve.scalar_tensor_tensor(s[:], s[:], 1.0, t[:], ALU.add, ALU.mult))
                own.link(dve.tensor_scalar(raw[:], raw[:], 0.0, None, ALU.max))
                own.link(dve.scalar_tensor_tensor(dt[:], s[:], 2.0, raw[:], ALU.mult, ALU.add))
                dve.wait_ge(a_exp, 1)
                dve.scalar_tensor_tensor(adt[:].rearrange("p c d h -> p c (d h)"), dt[:].rearrange("p c d h -> p c (d h)"),
                                         -1.0, alog[:].rearrange("p d h -> p (d h)").unsqueeze(1).to_broadcast([P, NT, 2 * HEADS]),
                                         ALU.mult, ALU.mult).then_inc(adt_ready, 1)
                dve.wait_ge(dec_ready, 1)
                for d in range(2):
                    own.add(dve.tensor_tensor(wst[:, :, d], dt[:, :, d], decay[:, 1 + 2 * d, :, d], ALU.mult))
                own.wait()

            @block.scalar
            def _(act):
                act.wait_ge(loaded, 96)
                act.activation(alog[:], alog[:], ACT.Exp).then_inc(a_exp, 1)
                act.wait_ge(neg_ready, 1)
                act.activation(u[:], u[:], ACT.Exp).then_inc(exped, 1)
                act.wait_ge(summed, 1)
                flat = decay[:].rearrange("p m c d h -> p (m c d h)")
                act.activation(flat[:, 0:6 * HB], cum[:, 0, 0:6 * HB], ACT.Exp)
                act.activation(flat[:, 6 * HB:10 * HB], cum[:, 1, 0:4 * HB], ACT.Exp).then_inc(dec_ready, 1)

        with ExitStack() as c1:
            sb, ps, sem = scope(nc, c1)
            xb = sb("s1_xb", [P, 2, 6, P])
            zT = sb("s1_zT", [P, 2, 4, P])
            btok = sb("s1_b", [P, 2, 2 * P])
            xw = sb("s1_xw", [P, 2, 2, SSD_W])
            x_ps, z_ps, b_ps = ps("s1_xps", [P, SSD_W]), ps("s1_zps", [P, SSD_W]), ps("s1_bps", [P, 512])
            st_ps = ps("s1_st", [P, 2, SSD_W])
            loaded = pair_of(sem, "s1_in")
            read_in, turned, x_ready, xw_ready, b_ready, z_ready, st_done, st_out = (
                sem(f"s1_{n}") for n in ("read", "turned", "x", "xw", "b", "z", "st", "stout"))
            block = c1.enter_context(nc.Block())

            @block.sync
            def _(sp):
                with sp.Fori(0, NT // 2) as i:
                    for u in range(2):
                        tok = bass.ds(i * (2 * P) + u * P, P)
                        sp.wait_ge(turned, i * 2 + (u + 1))
                        sp.dma_start(xb[:, u], xbcT[0:6, :, tok].rearrange("b p t -> p b t")).then_inc(loaded[u], 16)
                        sp.dma_start(zT[:, u], projT[BLK_Z:BLK_Z + 4, :, tok].rearrange("b p t -> p b t")
                                     ).then_inc(loaded[u], 16)

            @block.tensor
            def _(pe):
                pe.sem_inc(turned, 2)
                with pe.Fori(0, NT // 2) as i:
                    for u in range(2):
                        pe.wait_ge(loaded[u], i * 32 + 32)
                        pe.wait_ge(x_ready, i * 2 + (u + 1))
                        pe.wait_ge(b_ready, i * 2 + (u + 1))
                        pe.wait_ge(z_ready, i * 2 + (u + 1))
                        for b in range(4):
                            pe.transpose(x_ps[:, b * P:(b + 1) * P], xb[:, u, b], cm[:, C_IDENT])
                            pe.transpose(z_ps[:, b * P:(b + 1) * P], zT[:, u, b], cm[:, C_IDENT])
                        for b in range(2):
                            mm = pe.transpose(b_ps[:, b * P:(b + 1) * P], xb[:, u, 4 + b], cm[:, C_IDENT])
                        mm.then_inc(turned, 1)
                        pe.wait_ge(b_ready, i * 2 + (u + 2))
                        pe.wait_ge(xw_ready, i * 2 + (u + 1))
                        pe.wait_ge(st_out, i * 2 + (u + 1))
                        for d in range(2):
                            for g in range(2):
                                mm = pe.matmul(st_ps[:, d, g * 256:(g + 1) * 256], btok[:, u, g * P:(g + 1) * P],
                                               xw[:, u, d, g * 256:(g + 1) * 256], start=True, stop=True)
                        mm.then_inc(st_done, 1)

            @block.vector
            def _(dve):
                dve.sem_inc(x_ready, 1)
                with dve.Fori(0, NT // 2) as i:
                    for u in range(2):
                        c = i * 2 + u
                        dve.wait_ge(turned, i * 2 + (u + 3))
                        dve.tensor_copy(one_of(xtok, c), x_ps[:]).then_inc(x_ready, 1)
                        dve.wait_ge(x_ready, i * 2 + (u + 2))
                        dve.wait_ge(st_done, i * 2 + (u + 1))
                        for d in range(2):
                            ins = dve.tensor_tensor(
                                xw[:, u, d].rearrange("p (h c) -> p h c", h=HEADS),
                                one_of(xtok, c).rearrange("p (h c) -> p h c", h=HEADS),
                                wst[:, bass.ds(c, 1), d, :].rearrange("p o h -> p (o h)").unsqueeze(2).to_broadcast(
                                    [P, HEADS, HD]), ALU.mult)
                        ins.then_inc(xw_ready, 1)

            @block.scalar
            def _(act):
                act.sem_inc(b_ready, 1)
                act.sem_inc(z_ready, 1)
                act.sem_inc(st_out, 1)
                act.sem_inc(st_done, 2)
                with act.Fori(0, NT // 2) as i:
                    for u in range(2):
                        c = i * 2 + u
                        act.wait_ge(turned, i * 2 + (u + 3))
                        act.wait_ge(st_done, i * 2 + (u + 1))
                        act.activation(btok[:, u], b_ps[:, 0:2 * P], ACT.Copy).then_inc(b_ready, 1)
                        act.activation(one_of(zt, c), z_ps[:], ACT.Silu).then_inc(z_ready, 1)
                        act.wait_ge(st_done, i * 2 + (u + 3))
                        act.activation(one_of(states[0], c), st_ps[:, 0], ACT.Copy)
                        act.activation(one_of(states[1], c), st_ps[:, 1], ACT.Copy).then_inc(st_out, 1)

        with ExitStack() as c2:
            sb, ps, sem = scope(nc, c2)
            steps = [sem("s2_fwd"), sem("s2_bwd")]
            block = c2.enter_context(nc.Block())

            def recur(eng, d):
                done = Steps(eng, steps[d])
                by_head = lambda ap: ap.rearrange("p (h c) -> p h c", h=HEADS)
                for seq in CHUNKS:
                    order = list(seq) if d == 0 else list(seq)[::-1]
                    done.link(eng.memset(entering[d][:, order[0], :], 0.0))
                    for c, nxt in zip(order, order[1:]):
                        e = entering[d]
                        done.link(eng.tensor_tensor(by_head(e[:, nxt, :]), by_head(e[:, c, :]),
                                                    decay[:, 4, c, d, :].unsqueeze(2).to_broadcast([P, HEADS, HD]),
                                                    ALU.mult))
                        done.link(eng.tensor_tensor(e[:, nxt, :], e[:, nxt, :], states[d][:, c, :], ALU.add))

            @block.vector
            def _(dve):
                recur(dve, 0)

            @block.gpsimd
            def _(pool):
                recur(pool, 1)

        with ExitStack() as c3:
            sb, ps, sem = scope(nc, c3)
            bcT = sb("s3_bcT", [P, 2, 4, P])
            seg = sb("s3_seg", [P, 2, HEADS, P])
            xdt = sb("s3_xdt", [P, 2, SSD_W])
            m = sb("s3_m", [P, 2, 2 * 2 * G * P])
            cb = sb("s3_cb", [P, 2, 2, P])
            tmp, acc = sb("s3_tmp", [P, 2, SSD_W]), sb("s3_acc", [P, SSD_W])
            seg_ps = ps("s3_seg_ps", [P, 2 * HEADS * P])
            cb_ps, y_ps, off_ps = ps("s3_cb_ps", [P, 512]), ps("s3_y_ps", [P, SSD_W]), ps("s3_off_ps", [P, 2, SSD_W])
            loaded = pair_of(sem, "s3_in")
            seg_ready, seg_done, cb_done, cb_read, decayed, m_ready, y_done, gated = (
                sem(f"s3_{n}") for n in ("seg", "segdone", "cbdone", "cbread", "decayed", "m", "y", "gated"))
            steps, passed, passed_pool = sem("s3_dve"), sem("s3_passed"), sem("s3_passed_pool")
            xdt_ready, ps_read, seg_read = sem("s3_xdt_ready"), sem("s3_ps_read"), sem("s3_seg_read")
            block = c3.enter_context(nc.Block())

            def row(ap, c, d):
                return ap[:, bass.ds(c, 1), d, :].rearrange("p o h -> p (o h)")

            @block.sync
            def _(sp):
                with sp.Fori(0, NT // 2) as i:
                    for u in range(2):
                        sp.wait_ge(y_done, i * 2 + (u + 1))
                        sp.dma_start(bcT[:, u], xbcT[4:8, :, bass.ds(i * (2 * P) + u * P, P)].rearrange("b p t -> p b t")
                                     ).then_inc(loaded[u], 16)

            @block.gpsimd
            def _(pool):
                with pool.Fori(0, NT // 2) as i:
                    for u in range(2):
                        pool.wait_ge(seg_done, i * 2 + (u + 1))
                        pool.sem_inc(passed_pool, 1)
                        for d, mask in enumerate((C_GT, C_LT)):
                            ins = pool.tensor_tensor(seg[:, d], cm[:, mask].unsqueeze(1).to_broadcast([P, HEADS, P]),
                                                     row(adt, i * 2 + u, d).unsqueeze(2).to_broadcast([P, HEADS, P]),
                                                     ALU.mult)
                        ins.then_inc(seg_ready, 1)

            @block.vector
            def _(dve):
                own = Steps(dve, steps)
                dve.sem_inc(gated, 1)
                dve.sem_inc(cb_read, 1)
                dve.sem_inc(m_ready, 1)

                hv = lambda ap: ap.rearrange("p (h c) -> p h c", h=HEADS)

                def masked(r, u):
                    c = r * 2 + u
                    dve.wait_ge(cb_done, c + 1)
                    dve.wait_ge(m_ready, c + 1)
                    for d, mask in enumerate((C_LE, C_GE)):
                        own.add(dve.tensor_tensor(cb[:, d], cb_ps[:, 0:2 * P].rearrange("p (g l) -> p g l", g=2),
                                                  cm[:, mask].unsqueeze(1).to_broadcast([P, 2, P]), ALU.mult))
                    own.wait()
                    dve.sem_inc(cb_read, 1)
                    dve.wait_ge(decayed, c + 1)
                    dg = m[:, u].rearrange("p (x h l) -> p x h l", x=4, h=G)
                    dve.tensor_tensor(dg, dg, cb[:].rearrange("p d g l -> p (d g) l").unsqueeze(2).to_broadcast(
                        [P, 4, G, P]), ALU.mult).then_inc(m_ready, 1)

                def weigh(r, u):
                    c = r * 2 + u
                    dve.wait_ge(y_done, c + 2)
                    for d in range(2):
                        ins = dve.tensor_tensor(hv(xdt[:, d]), hv(one_of(xtok, c)),
                                                row(dt, c, d).unsqueeze(2).to_broadcast([P, HEADS, HD]), ALU.mult)
                    ins.then_inc(xdt_ready, 1)

                def gather(r, u):
                    c = r * 2 + u
                    dec = lambda k, d: decay[:, k, bass.ds(c, 1), d, :].rearrange("p o h -> p (o h)").unsqueeze(
                        2).to_broadcast([P, HEADS, HD])
                    own.add(dve.tensor_tensor(tmp[:, 1], one_of(xtok, c), drow[:], ALU.mult))
                    dve.wait_ge(y_done, c + 3)
                    dve.wait_ge(gated, c + 1)
                    own.add(dve.tensor_tensor(hv(acc[:]), hv(off_ps[:, 0]), dec(0, 0), ALU.mult))
                    own.link(dve.tensor_tensor(hv(tmp[:, 0]), hv(off_ps[:, 1]), dec(2, 1), ALU.mult))
                    own.link(dve.tensor_tensor(acc[:], acc[:], tmp[:, 0], ALU.add))
                    own.link(dve.tensor_tensor(acc[:], acc[:], y_ps[:], ALU.add))
                    dve.sem_inc(ps_read, 1)
                    own.link(dve.tensor_tensor(acc[:], acc[:], tmp[:, 1], ALU.add))
                    dve.tensor_tensor(one_of(y, c), acc[:], one_of(zt, c), ALU.mult).then_inc(gated, 1)

                masked(0, 0)
                weigh(0, 0)

                with dve.Fori(0, NT // 2 - 1) as i:
                    own.enter(i, 2 * 8)
                    for u in range(2):
                        masked(i + u, 1 - u)
                        gather(i, u)
                        weigh(i + u, 1 - u)
                own.leave(NT // 2 - 1)
                masked(NT // 2 - 1, 1)
                gather(NT // 2 - 1, 0)
                weigh(NT // 2 - 1, 1)
                gather(NT // 2 - 1, 1)

            @block.tensor
            def _(pe):
                pe.sem_inc(seg_done, 1)
                pe.sem_inc(y_done, 2)

                def sums(r, u):
                    c = r * 2 + u
                    pe.wait_ge(loaded[u], r * 16 + 16)
                    pe.wait_ge(cb_read, c + 1)
                    for g in range(2):
                        mm = pe.matmul(cb_ps[:, g * P:(g + 1) * P], bcT[:, u, g], bcT[:, u, 2 + g],
                                       start=True, stop=True)
                    mm.then_inc(cb_done, 1)
                    pe.wait_ge(seg_ready, c + 1)
                    pe.wait_ge(seg_read, c + 1)
                    for d, mask in enumerate((C_LE, C_GE)):
                        for h in range(HEADS):
                            n = d * HEADS + h
                            mm = pe.matmul(seg_ps[:, n * P:(n + 1) * P], seg[:, d, h], cm[:, mask],
                                           start=True, stop=True)
                    mm.then_inc(seg_done, 1)

                def products(r, u):
                    c = r * 2 + u
                    pe.wait_ge(ps_read, c + 1)
                    pe.sem_inc(passed, 1)
                    for d in range(2):
                        for g in range(2):
                            pe.matmul(off_ps[:, d, g * 256:(g + 1) * 256], bcT[:, u, 2 + g],
                                      one_of(entering[d], c)[:, g * 256:(g + 1) * 256], start=True, stop=True)
                    pe.wait_ge(m_ready, c + 2)
                    pe.wait_ge(xdt_ready, c + 1)
                    for h in range(HEADS):
                        for d in range(2):
                            x = (d * HEADS + h) * P
                            mm = pe.matmul(y_ps[:, h * HD:(h + 1) * HD], m[:, u, x:x + P],
                                           xdt[:, d, h * HD:(h + 1) * HD], start=(d == 0), stop=(d == 1))
                    mm.then_inc(y_done, 1)

                sums(0, 0)
                with pe.Fori(0, NT // 2 - 1) as i:
                    for u in range(2):
                        sums(i + u, 1 - u)
                        products(i, u)
                sums(NT // 2 - 1, 1)
                products(NT // 2 - 1, 0)
                products(NT // 2 - 1, 1)

            @block.scalar
            def _(act):
                act.sem_inc(seg_read, 1)
                act.sem_inc(ps_read, 1)
                with act.Fori(0, NT // 2) as i:
                    for u in range(2):
                        act.wait_ge(seg_done, i * 2 + (u + 2))
                        act.wait_ge(y_done, i * 2 + (u + 1))
                        act.activation(m[:, u], seg_ps[:], ACT.Exp).then_inc(decayed, 1)
                        act.wait_ge(decayed, i * 2 + (u + 1))
                        act.sem_inc(seg_read, 1)

        with ExitStack() as c4:
            sb, ps, sem = scope(nc, c4)
            junk = sb("s4_junk", [P, SSD_W])
            yn = sb("s4_yn", [P, 2, SSD_W])
            oT = sb("s4_oT", [P, 2, 4, P])
            t_ps = ps("s4_t", [P, 2, SSD_W])
            squared, root, var, normed, turned, copied, steps = (
                sem(f"s4_{n}") for n in ("sq", "root", "var", "normed", "turned", "copied", "dve"))
            stored = pair_of(sem, "s4_stored")
            block = c4.enter_context(nc.Block())

            @block.scalar
            def _(act):
                for c in range(NT):
                    if c:
                        act.wait_ge(squared, c)
                    act.activation(junk[:], y[:, c, :], ACT.Square, accum_out=ssq[:, c:c + 1]).then_inc(squared, 1)
                act.wait_ge(var, 1)
                act.activation(ssq[:], ssq[:], ACT.Sqrt).then_inc(root, 1)
                act.sem_inc(copied, 2)
                act.sem_inc(stored[0], 16)
                act.sem_inc(stored[1], 16)
                with act.Fori(0, NT // 2) as i:
                    for u in range(2):
                        act.wait_ge(turned, i * 2 + (u + 3))
                        act.wait_ge(stored[u], i * 16 + 16)
                        act.activation(oT[:, u].rearrange("p b t -> p (b t)"), t_ps[:, u], ACT.Copy).then_inc(copied, 1)
                        act.wait_ge(copied, i * 2 + (u + 3))
                        act.dma_start(mixT[4:8, :, bass.ds(i * (2 * P) + u * P, P)].rearrange("b p t -> p b t"),
                                      oT[:, u]).then_inc(stored[u], 16)
                for u in range(2):
                    act.wait_ge(stored[u], 16 * (1 + NT // 2))

            @block.vector
            def _(dve):
                own = Steps(dve, steps)
                dve.wait_ge(squared, NT)
                dve.tensor_scalar(ssq[:], ssq[:], 1.0 / SSD_W, EPS, ALU.mult, ALU.add).then_inc(var, 1)
                dve.wait_ge(root, 1)
                own.link(dve.reciprocal(ssq[:], ssq[:]))
                with dve.Fori(0, NT // 2) as i:
                    for u in range(2):
                        dve.wait_ge(turned, i * 2 + (u + 1))
                        dve.scalar_tensor_tensor(yn[:, u], one_of(y, i * 2 + u), ssq[:, bass.ds(i * 2 + u, 1)], nrow[:],
                                                 ALU.mult, ALU.mult).then_inc(normed, 1)

            @block.tensor
            def _(pe):
                pe.sem_inc(turned, 2)
                with pe.Fori(0, NT // 2) as i:
                    for u in range(2):
                        pe.wait_ge(normed, i * 2 + (u + 1))
                        pe.wait_ge(copied, i * 2 + (u + 1))
                        for b in range(4):
                            mm = pe.transpose(t_ps[:, u, b * P:(b + 1) * P], yn[:, u, b * P:(b + 1) * P], cm[:, C_IDENT])
                        mm.then_inc(turned, 1)


def project_out(nc, mixT, w_out, x, w_row, ident, x2, hT):
    with ExitStack() as ctx:
        sb, ps, sem = scope(nc, ctx)
        idm, wrow = sb("po_ident", [P, P]), sb("po_wrow", [P, D])
        w = [sb(f"po_w_{part}", [P, KD, D], F32R) for part in ("hi", "lo")]
        wraw = sb("po_wraw", [P, 2, D])
        mraw = sb("po_mraw", [P, 2, KD * P])
        mx = [sb(f"po_m_{part}", [P, 2, KD * P], F32R) for part in ("hi", "lo")]
        xin, xo, xs = sb("po_x", [P, 2, D]), sb("po_x2", [P, 2, D]), sb("po_xs", [P, D])
        ssq, rstd = sb("po_ssq", [P, 2]), sb("po_rstd", [P, 2])
        acc, xT = ps("po_acc", [P, 2, D]), ps("po_xT", [P, 2, D])
        consts_in, w_in = sem("po_consts_in"), pair_of(sem, "po_w_in")
        m_in, stored = pair_of(sem, "po_m_in"), pair_of(sem, "po_stored")
        w_hi, w_split, m_split, summed, added, squared, var, root, scaled, turned, hi_done, lo_done, steps = (
            sem(f"po_{n}") for n in ("w_hi", "w_split", "m_split", "summed", "added", "squared", "var", "root",
                                     "scaled", "turned", "hi", "lo", "dve"))
        block = ctx.enter_context(nc.Block())

        def tok(r, u):
            return bass.ds(r * (2 * P) + u * P, P)

        @block.sync
        def _(sp):
            for k in range(2):
                sp.dma_start(wraw[:, k], w_out[k]).then_inc(w_in[k], 16)
            sp.dma_start(idm[:], ident).then_inc(consts_in, 16)
            sp.dma_start(wrow[:], rows_bcast(w_row, D)).then_inc(consts_in, 16)
            for k in range(2, KD):
                sp.wait_ge(w_split, k - 1)
                sp.dma_start(wraw[:, k % 2], w_out[k]).then_inc(w_in[k % 2], 16)
            with sp.Fori(0, NT // 2) as i:
                for u in range(2):
                    sp.wait_ge(m_split, i * 2 + (u + 1))
                    sp.wait_ge(added, i * 2 + (u + 1))
                    sp.dma_start(mraw[:, u].rearrange("p (k t) -> p k t", k=KD),
                                 mixT[:, :, tok(i, u)].rearrange("b p t -> p b t")).then_inc(m_in[u], 16)
                    sp.dma_start(xin[:, u], x[tok(i, u), :]).then_inc(m_in[u], 16)

        @block.tensor
        def _(pe):
            pe.sem_inc(lo_done, 2)

            def products(r, u):
                pe.wait_ge(m_split, r * 2 + (u + 3))
                pe.wait_ge(added, r * 2 + (u + 1))
                for k in range(KD):
                    for n, (a, b) in enumerate(PRODUCTS):
                        for h in range(2):
                            mm = pe.matmul(acc[:, u, h * 512:(h + 1) * 512], mx[a][:, u, k * P:(k + 1) * P],
                                           w[b][:, k, h * 512:(h + 1) * 512], start=(k + n == 0),
                                           stop=(k == KD - 1 and n == 2))
                mm.then_inc(summed, 1)

            def turn(r, u):
                pe.wait_ge(scaled, r * 2 + (u + 1))
                pe.wait_ge(lo_done, r * 2 + (u + 1))
                for k in range(KD):
                    mm = pe.transpose(xT[:, u, k * P:(k + 1) * P], xs[:, k * P:(k + 1) * P], idm[:])
                mm.then_inc(turned, 1)

            pe.wait_ge(w_split, KD)
            pe.wait_ge(consts_in, 32)
            products(0, 0)

            def step(r, u):
                products(r + u, 1 - u)
                turn(r, u)
            rounds(pe, NT - 1, step)
            turn(NT // 2 - 1, 1)

        @block.scalar
        def _(act):
            act.sem_inc(stored[0], 16)
            act.sem_inc(stored[1], 16)
            for k in range(KD):
                act.wait_ge(w_in[k % 2], 16 * (k // 2 + 1))
                act.activation(w[0][:, k], wraw[:, k % 2], ACT.Copy).then_inc(w_hi, 1)

            def stats(r, u):
                act.wait_ge(added, r * 2 + (u + 3))
                act.activation(xs[:], xo[:, u], ACT.Square, accum_out=ssq[:, u:u + 1]).then_inc(squared, 1)
                act.wait_ge(var, r * 2 + (u + 1))
                act.activation(rstd[:, u:u + 1], ssq[:, u:u + 1], ACT.Sqrt).then_inc(root, 1)
                act.dma_start(x2[tok(r, u), :], xo[:, u]).then_inc(stored[u], 16)

            def hi(r, u):
                act.wait_ge(turned, r * 2 + (u + 1))
                act.activation(hT[0][:, :, tok(r, u)], xT[:, u].rearrange("p (k t) -> p k t", k=KD), ACT.Copy
                               ).then_inc(hi_done, 1)

            def step(r, u):
                stats(r, u)
                hi(r, u)
            rounds(act, NT, step)
            for u in range(2):
                act.wait_ge(stored[u], 16 * (1 + NT // 2))

        @block.vector
        def _(dve):
            own = Steps(dve, steps)
            dve.sem_inc(m_split, 2)
            dve.sem_inc(added, 2)
            for k in range(KD):
                dve.wait_ge(w_hi, k + 1)
                dve.tensor_tensor(w[1][:, k], wraw[:, k % 2], w[0][:, k].bitcast(F32), ALU.subtract).then_inc(w_split, 1)

            def parts(r, u):
                dve.wait_ge(m_in[u], r * 32 + 32)
                if not (isinstance(r, int) and r == 0):
                    dve.wait_ge(summed, r * 2 + (u - 1))
                split(dve, own, mx[0][:, u], mx[1][:, u], mraw[:, u]).then_inc(m_split, 1)

            def norm(r, u):
                dve.wait_ge(summed, r * 2 + (u + 1))
                dve.wait_ge(stored[u], r * 16 + 16)
                dve.tensor_tensor(xo[:, u], acc[:, u], xin[:, u], ALU.add).then_inc(added, 1)
                dve.wait_ge(squared, r * 2 + (u + 1))
                dve.tensor_scalar(ssq[:, u:u + 1], ssq[:, u:u + 1], 1.0 / D, EPS, ALU.mult, ALU.add).then_inc(var, 1)
                dve.wait_ge(root, r * 2 + (u + 1))
                own.link(dve.reciprocal(rstd[:, u:u + 1], rstd[:, u:u + 1]))
                dve.scalar_tensor_tensor(xs[:], xo[:, u], rstd[:, u:u + 1], wrow[:], ALU.mult, ALU.mult
                                         ).then_inc(scaled, 1)

            def lo(r, u):
                dve.wait_ge(hi_done, r * 2 + (u + 1))
                dve.tensor_tensor(hT[1][:, :, tok(r, u)], xT[:, u].rearrange("p (k t) -> p k t", k=KD),
                                  hT[0][:, :, tok(r, u)].bitcast(F32), ALU.subtract).then_inc(lo_done, 1)

            dve.wait_ge(consts_in, 32)
            parts(0, 0)
            parts(0, 1)
            with dve.Fori(0, NT // 2 - 1) as i:
                own.enter(i, 4)
                for u in range(2):
                    norm(i, u)
                    parts(i + 1, u)
                    lo(i, u)
            own.leave(NT // 2 - 1)
            for u in range(2):
                norm(NT // 2 - 1, u)
                lo(NT // 2 - 1, u)


RECTS = [(0, 1, 16), (1, 1, 8), (2, 2, 5), (4, 4, 3), (8, 8, 1)]
NCAND = sum(na * nb for _, na, nb in RECTS)


def row_starts():
    starts, at = [], 0
    for _, na, nb in RECTS:
        for _ in range(na):
            starts.append(at)
            at += nb
    return starts


def retrieve(nc, hT, w_query, keysT, starts, tabs):
    KZ = KD * P
    with ExitStack() as ctx:
        sb, ps, sem = scope(nc, ctx)
        wraw = sb("pk_wraw", [P, 2, KZ])
        w = [sb(f"pk_w_{part}", [P, 2, KZ], F32R) for part in ("hi", "lo")]
        keys = sb("pk_keys", [P, 2, P])
        qT = sb("pk_qT", [P, 2, T])
        s = sb("pk_s", [P, 2, NT, NKEY])
        rest = sb("pk_rest", [P, 2, NT, NKEY])
        sv = sb("pk_sv", [P, 2, NT, TOPK])
        si = sb("pk_si", [P, 2, NT, TOPK], U32)
        sif = sb("pk_sif", [P, 2, NT, TOPK], BF16)
        dif = sb("pk_dif", [P, NT, TOPK], BF16)
        cand = sb("pk_cand", [P, NT, NCAND])
        crest = sb("pk_crest", [P, NT, NCAND])
        cv = sb("pk_cv", [P, NT, TOPK])
        ci = sb("pk_ci", [P, NT, TOPK], U32)
        cf = sb("pk_cf", [P, NT, TOPK], BF16)
        small, wide = ([sb(f"pk_{name}{n}", [P, NT * TOPK, n], BF16 if name == "small" or n == 8 else F32)
                        for n in (8, 4, 2, 1)] for name in ("small", "wide"))
        hot = sb("pk_hot", [P, NT, TOPK, TOPK], BF16)
        prod = sb("pk_prod", [P, 2, NT, TOPK, TOPK], BF16)
        st = sb("pk_starts", [P, 3, TOPK])
        stb = sb("pk_starts_b", [P, 3, TOPK], BF16)
        den = sb("pk_den", [P, NT])
        acc = ps("pk_acc", [P, 2, 3 * 512])
        consts_in, w_in, keys_in = sem("pk_consts_in"), pair_of(sem, "pk_w_in"), sem("pk_keys_in")
        w_hi, w_split, summed, q_ready, scored, s_ready, s_read, exp_in, exp_out, steps, passed = (
            sem(f"pk_{n}") for n in ("w_hi", "w_split", "summed", "q", "scored", "s", "s_read", "exp_in", "exp_out",
                                     "dve", "passed"))
        block = ctx.enter_context(nc.Block())

        @block.sync
        def _(sp):
            sp.dma_start(st[:], rows_bcast(starts, 3 * TOPK)).then_inc(consts_in, 16)
            with sp.Fori(0, HEADS) as h:
                for z in range(2):
                    sp.wait_ge(w_split, h * 2 + (z + 1))
                    sp.dma_start(wraw[:, z], one(w_query, h * 2 + z)).then_inc(w_in[z], 16)
                sp.wait_ge(scored, h * 2 + 2)
                sp.dma_start(keys[:], keysT[bass.ds(h * 2, 2)].rearrange("z p n -> p z n")).then_inc(keys_in, 16)

        @block.tensor
        def _(pe):
            pe.sem_inc(scored, 2)
            pe.sem_inc(summed, 2)
            with pe.Fori(0, HEADS) as h:
                pe.wait_ge(keys_in, h * 16 + 16)
                for z in range(2):
                    pe.wait_ge(w_split, h * 2 + (z + 3))
                    pe.wait_ge(s_ready, h * 2 + (z + 1))
                    for k in range(KD):
                        for n, (a, b) in enumerate(PRODUCTS):
                            for t0, tn in SEGS:
                                mm = pe.matmul(acc[:, z, t0:t0 + tn], w[a][:, z, k * P:(k + 1) * P],
                                               hT[b][:, k, t0:t0 + tn], start=(k + n == 0),
                                               stop=(k == KD - 1 and n == 2))
                    mm.then_inc(summed, 1)
                    pe.wait_ge(q_ready, h * 2 + (z + 1))
                    for t in range(NT):
                        mm = pe.matmul(acc[:, z, t * P:(t + 1) * P], qT[:, z, t * P:(t + 1) * P], keys[:, z],
                                       start=True, stop=True)
                    mm.then_inc(scored, 1)

        @block.scalar
        def _(act):
            act.sem_inc(s_ready, 2)

            def hi(h, z):
                act.wait_ge(w_in[z], h * 16 + 16)
                act.wait_ge(summed, h * 2 + (z + 1))
                act.activation(w[0][:, z], wraw[:, z], ACT.Copy).then_inc(w_hi, 1)

            def scores_out(h, z, more=True):
                act.wait_ge(summed, h * 2 + (z + 3))
                act.activation(qT[:, z], acc[:, z, 0:T], ACT.Copy).then_inc(q_ready, 1)
                if more:
                    hi(h + 1, z)
                act.wait_ge(scored, h * 2 + (z + 3))
                act.wait_ge(s_read, h + 1)
                act.activation(s[:, z].rearrange("p t n -> p (t n)"), acc[:, z, 0:T], ACT.Copy).then_inc(s_ready, 1)

            def exps(h):
                act.wait_ge(exp_in, h + 1)
                act.activation(cv[:], cv[:], ACT.Exp).then_inc(exp_out, 1)

            for z in range(2):
                hi(0, z)
            for z in range(2):
                scores_out(0, z)
            with act.Fori(0, HEADS - 2) as h:
                scores_out(h + 1, 0)
                exps(h)
                scores_out(h + 1, 1)
            scores_out(HEADS - 1, 0, False)
            exps(HEADS - 2)
            scores_out(HEADS - 1, 1, False)
            exps(HEADS - 1)

        @block.vector
        def _(dve):
            own = Steps(dve, steps)
            dve.sem_inc(w_split, 2)
            dve.sem_inc(s_read, 1)

            def lo(h, z):
                dve.wait_ge(w_hi, h * 2 + (z + 1))
                dve.tensor_tensor(w[1][:, z], wraw[:, z], w[0][:, z].bitcast(F32), ALU.subtract).then_inc(w_split, 1)

            def over(items):
                for ins in items:
                    last = ins
                    own.add(ins)
                own.wait()
                dve.sem_inc(passed, 1)

            def each(f):
                over(f(z, t) for z in range(2) for t in range(NT))

            def topk(h, more=True):
                for z in range(2):
                    if more:
                        lo(h + 1, z)
                    dve.wait_ge(s_ready, h * 2 + (z + 3))
                    dve.sem_inc(passed, 1)
                    for t in range(NT):
                        own.add(dve.max(sv[:, z, t, 0:8], s[:, z, t]))
                own.wait()
                dve.sem_inc(passed, 1)
                for z in range(2):
                    for t in range(NT):
                        own.add(dve.max_index(si[:, z, t, 0:8], sv[:, z, t, 0:8], s[:, z, t]))
                each(lambda z, t: dve.match_replace(rest[:, z, t], sv[:, z, t, 0:8], s[:, z, t], LOWEST))
                dve.sem_inc(s_read, 1)
                each(lambda z, t: dve.max(sv[:, z, t, 8:16], rest[:, z, t]))
                each(lambda z, t: dve.max_index(si[:, z, t, 8:16], sv[:, z, t, 8:16], rest[:, z, t]))
                own.add(dve.tensor_copy(sif[:], si[:]))
                at, made = 0, []
                for a0, na, nb in RECTS:
                    made.append(dve.tensor_tensor(
                        cand[:, :, at:at + na * nb].rearrange("p t (a b) -> p t a b", a=na),
                        sv[:, 0, :, a0:a0 + na].unsqueeze(3).to_broadcast([P, NT, na, nb]),
                        sv[:, 1, :, 0:nb].unsqueeze(2).to_broadcast([P, NT, na, nb]), ALU.add))
                    own.add(made[-1])
                    at += na * nb
                own.wait()
                dve.sem_inc(passed, 1)
                over(dve.max(cv[:, t, 0:8], cand[:, t]) for t in range(NT))
                for t in range(NT):
                    own.add(dve.max_index(ci[:, t, 0:8], cv[:, t, 0:8], cand[:, t]))
                over(dve.match_replace(crest[:, t], cv[:, t, 0:8], cand[:, t], LOWEST) for t in range(NT))
                over(dve.max(cv[:, t, 8:16], crest[:, t]) for t in range(NT))
                over(dve.max_index(ci[:, t, 8:16], cv[:, t, 8:16], crest[:, t]) for t in range(NT))
                own.add(dve.tensor_copy(cf[:], ci[:]))
                own.add(dve.tensor_copy(dif[:, :, 0:1], sif[:, 0, :, 0:1]))
                own.add(dve.tensor_tensor(dif[:, :, 1:TOPK], sif[:, 0, :, 1:TOPK], sif[:, 0, :, 0:TOPK - 1], ALU.subtract))
                own.link(dve.tensor_copy(den[:], cv[:, :, 0:1].rearrange("p t o -> p (t o)")))
                dve.tensor_tensor(cv[:], cv[:], den[:].unsqueeze(2).to_broadcast([P, NT, TOPK]), ALU.subtract
                                  ).then_inc(exp_in, 1)
                flat = lambda ap: ap.rearrange("p t k -> p (t k)").unsqueeze(2).to_broadcast([P, NT * TOPK, TOPK])
                row = lambda n: stb[:, n].unsqueeze(1).to_broadcast([P, NT * TOPK, TOPK])
                hot2 = hot[:].rearrange("p t k a -> p (t k) a")
                by_tile = lambda ap: ap.unsqueeze(2).to_broadcast([P, NT, TOPK, TOPK])

                def sums(n, tree):
                    left = prod[:, n].rearrange("p t k a -> p (t k) a")
                    for to in tree:
                        w = to.shape[2]
                        own.link(dve.tensor_tensor(to[:], left[:, :, 0:w], left[:, :, w:2 * w], ALU.add))
                        left = to
                    return left[:].rearrange("p (t k) o -> p t (k o)", t=NT)

                col = tabs_cols(h)
                own.link(dve.tensor_tensor(hot2, flat(cf[:]), row(0), ALU.is_ge))
                own.add(dve.tensor_tensor(prod[:, 0], hot[:], by_tile(dif[:]), ALU.mult))
                own.link(dve.tensor_tensor(prod[:, 1].rearrange("p t k a -> p (t k) a"), hot2, row(1), ALU.mult))
                own.add(dve.tensor_copy(tabs[0][:, :, col], sums(0, wide)))
                own.link(dve.tensor_tensor(cf[:], cf[:], sums(1, small), ALU.subtract))
                own.link(dve.tensor_tensor(hot2, flat(cf[:]), row(2), ALU.is_equal))
                own.link(dve.tensor_tensor(prod[:, 0], hot[:], by_tile(sif[:, 1]), ALU.mult))
                own.add(dve.tensor_copy(tabs[1][:, :, col], sums(0, small)))
                dve.wait_ge(exp_out, h + 1)
                own.link(dve.tensor_reduce(den[:], cv[:], AX.X, ALU.add))
                own.link(dve.reciprocal(den[:], den[:]))
                own.link(dve.tensor_tensor(tabs[2][:, :, col], cv[:], den[:].unsqueeze(2).to_broadcast([P, NT, TOPK]),
                                           ALU.mult))

            def tabs_cols(h):
                return bass.ds(h * TOPK, TOPK)

            dve.wait_ge(consts_in, 16)
            own.link(dve.tensor_copy(stb[:], st[:]))
            for z in range(2):
                lo(0, z)
            with dve.Fori(0, HEADS - 1) as h:
                own.enter(h, 183)
                topk(h)
            own.leave(HEADS - 1)
            topk(HEADS - 1, False)



def turn_tables(nc, tabs, ident, tabsT):
    with ExitStack() as ctx:
        sb, ps, sem = scope(nc, ctx)
        idm = sb("tt_ident", [P, P])
        tp = ps("tt_ps", [P, 2, 1024])
        loaded, turned, copied = sem("tt_in"), sem("tt_turned"), sem("tt_copied")
        block = ctx.enter_context(nc.Block())
        steps = [(n, h) for n in range(3) for h in range(2)]

        @block.sync
        def _(sp):
            sp.dma_start(idm[:], ident).then_inc(loaded, 16)

        @block.tensor
        def _(pe):
            pe.wait_ge(loaded, 16)
            for m, (n, h) in enumerate(steps):
                if m > 1:
                    pe.wait_ge(copied, m - 1)
                for t in range(NT // 2):
                    mm = pe.transpose(tp[:, m % 2, t * P:(t + 1) * P], tabs[n][:, h * (NT // 2) + t], idm[:])
                mm.then_inc(turned, 1)

        @block.scalar
        def _(act):
            for m, (n, h) in enumerate(steps):
                act.wait_ge(turned, m + 1)
                act.activation(tabsT[n][:, h * HALF:(h + 1) * HALF], tp[:, m % 2, 0:HALF], ACT.Copy).then_inc(copied, 1)


def gate_table(nc, tabsT, iota, iota_t, gates):
    GROUP = iota_t.shape[1] // P
    BY_POOL = 10
    PER = TB // GROUP
    BODY = 2 * PER
    QUADS = GROUP // 4
    with ExitStack() as ctx:
        sb, ps, sem = scope(nc, ctx)
        io = sb("gt_iota", [P, P])
        io_t = sb("gt_iota_t", [P, P * GROUP], BF16)
        hot = sb("gt_hot", [P, 2, P * GROUP], BF16)
        left, right = (sb(f"gt_{n}", [P, 2, GROUP, P]) for n in ("left", "right"))
        stage = sb("gt_stage", [P, 2, P * TB])
        io_raw = stage[:, 0, 0:P * GROUP]
        prod = ps("gt_prod", [P, 2 * QUADS, 512])
        loaded, dve_steps, hot_ready, right_ready, pool_done, act_done, summed, copied, passed = (
            sem(f"gt_{n}") for n in ("in", "dve", "hot", "right", "pool", "act", "summed", "copied", "passed"))
        stored, quads_done = pair_of(sem, "gt_stored"), sem("gt_quads")
        block = ctx.enter_context(nc.Block())
        N = T // TB

        @block.sync
        def _(sp):
            sp.dma_start(io[:], iota).then_inc(loaded, 16)
            sp.dma_start(io_raw, iota_t).then_inc(loaded, 16)
            sp.sem_inc(stored[0], 16)
            sp.sem_inc(stored[1], 16)
            with sp.Fori(0, N // 2) as i:
                for u in range(2):
                    sp.wait_ge(copied, i * (BODY * QUADS) + ((u + 1) * PER * QUADS + 2 * QUADS))
                    sp.dma_start(one(gates, i * 2 + u), stage[:, u]).then_inc(stored[u], 16)
            for u in range(2):
                sp.wait_ge(stored[u], 16 * (1 + N // 2))

        def tokens(i, g):
            return bass.ds(i * (BODY * GROUP) + g * GROUP, GROUP)

        @block.vector
        def _(dve):
            dve.wait_ge(loaded, 32)
            dve.tensor_copy(io_t[:], io_raw).then_inc(dve_steps, 1)
            dve.wait_ge(dve_steps, 1)
            with dve.Fori(0, N // 2) as i:
                for g in range(BODY):
                    n = i * BODY + (g + 1)
                    dve.wait_ge(pool_done, n)
                    dve.wait_ge(act_done, n)
                    dve.tensor_tensor(hot[:, g % 2].rearrange("p (i t) -> p i t", t=GROUP),
                                      io_t[:].rearrange("p (i t) -> p i t", t=GROUP),
                                      tabsT[0][:, tokens(i, g)].unsqueeze(1).to_broadcast([P, P, GROUP]),
                                      ALU.is_equal).then_inc(hot_ready, 1)
                    dve.wait_ge(summed, n)
                    dve.tensor_tensor(right[:, g % 2], io[:].unsqueeze(1).to_broadcast([P, GROUP, P]),
                                      tabsT[1][:, tokens(i, g)].unsqueeze(2).to_broadcast([P, GROUP, P]),
                                      ALU.is_equal).then_inc(right_ready, 1)

        @block.gpsimd
        def _(pool):
            pool.sem_inc(pool_done, 2)
            with pool.Fori(0, N // 2) as i:
                for g in range(BODY):
                    n = i * BODY + (g + 1)
                    pool.wait_ge(hot_ready, n)
                    pool.wait_ge(summed, n)
                    pool.sem_inc(passed, 1)
                    pool.tensor_tensor(left[:, g % 2, 0:BY_POOL],
                                       hot[:, g % 2].rearrange("p (i t) -> p t i", t=GROUP)[:, 0:BY_POOL],
                                       tabsT[2][:, bass.ds(i * (BODY * GROUP) + g * GROUP, BY_POOL)].unsqueeze(
                                           2).to_broadcast([P, BY_POOL, P]), ALU.mult).then_inc(pool_done, 1)

        @block.tensor
        def _(pe):
            pe.sem_inc(summed, 2)
            with pe.Fori(0, N // 2) as i:
                for g in range(BODY):
                    n = i * BODY + (g + 1)
                    pe.wait_ge(right_ready, n)
                    pe.wait_ge(pool_done, n + 2)
                    pe.wait_ge(act_done, n + 2)
                    for q in range(QUADS):
                        pe.wait_ge(copied, i * (BODY * QUADS) + (g * QUADS + q + 1))
                        for t in range(4 * q, 4 * q + 4):
                            mm = pe.matmul(prod[:, (g % 2) * QUADS + q, (t % 4) * P:(t % 4 + 1) * P],
                                           left[:, g % 2, t], right[:, g % 2, t], start=True, stop=True)
                        mm.then_inc(quads_done, 1)
                    pe.wait_ge(quads_done, i * (BODY * QUADS) + (g + 1) * QUADS)
                    pe.sem_inc(summed, 1)

        @block.scalar
        def _(act):
            act.sem_inc(copied, 2 * QUADS)
            act.sem_inc(act_done, 2)

            def weigh(i, g):
                act.wait_ge(hot_ready, i * BODY + (g + 1))
                act.wait_ge(summed, i * BODY + (g + 1))
                by_token = hot[:, g % 2].rearrange("p (i t) -> p t i", t=GROUP)
                for t in range(BY_POOL, GROUP):
                    ins = act.activation(left[:, g % 2, t], by_token[:, t], ACT.Copy,
                                         scale=tabsT[2][:, bass.ds(i * (BODY * GROUP) + (g * GROUP + t), 1)])
                ins.then_inc(act_done, 1)

            def take(i, g):
                u = g // PER
                if g % PER == 0:
                    act.wait_ge(stored[u], i * 16 + 16)
                by_token = stage[:, u].rearrange("p (j t) -> p t j", t=TB)
                for q in range(QUADS):
                    t0 = (g % PER) * GROUP + 4 * q
                    act.wait_ge(quads_done, i * (BODY * QUADS) + (g * QUADS + q + 1))
                    act.activation(by_token[:, t0:t0 + 4, :], prod[:, (g % 2) * QUADS + q].rearrange(
                        "p (t j) -> p t j", t=4), ACT.Copy).then_inc(copied, 1)

            with act.Fori(0, N // 2) as i:
                for g in range(BODY):
                    weigh(i, g)
                    if g:
                        take(i, g - 1)
                take(i, BODY - 1)


def experts(nc, hT, up, vp, gates, x2, w_row, out):
    GROUPS = NKEY // 2
    SEG = HALF // 2
    BANKS, OUTS = 4, 2 * NTH
    with ExitStack() as ctx:
        sb, ps, sem = scope(nc, ctx)
        acc = sb("ex_acc", [P, NTH, D])
        uraw, vraw = sb("ex_uraw", [P, 2, D]), sb("ex_vraw", [P, 2, D])
        uu = [sb(f"ex_u_{part}", [P, 2, D], F32R) for part in ("hi", "lo")]
        vv = [sb(f"ex_v_{part}", [P, 2, 2, D], F32R) for part in ("hi", "lo")]
        aa = [sb(f"ex_a_{part}", [P, 2, 2, HALF], F32R) for part in ("hi", "lo")]
        gt = sb("ex_gates", [P, 2, HALF // TB, 2 * TB])
        gl = sb("ex_gelu", [P, 2 * HALF])
        wrow = sb("ex_wrow", [P, D])
        ssq = sb("ex_ssq", [P, NTH])
        hps = ps("ex_h", [P, 2, 2, 512])
        ops_ = ps("ex_out", [P, BANKS, 512])
        u_in, v_in, g_in = pair_of(sem, "ex_u_in"), pair_of(sem, "ex_v_in"), pair_of(sem, "ex_g_in")
        acc_in, w_in, stored = sem("ex_acc_in"), sem("ex_w_in"), [sem(f"ex_stored{t}") for t in range(NTH)]
        u_hi, u_split, v_hi, v_split, h_done, gelu_done, a_ready, out_done, added, squared, var, root, normed, steps = (
            sem(f"ex_{n}") for n in ("u_hi", "u_split", "v_hi", "v_split", "h_done", "gelu", "a", "out_done", "added",
                                     "squared", "var", "root", "normed", "dve"))
        passed = sem("ex_passed")
        block = ctx.enter_context(nc.Block())
        A_CR, OUT_CR, ADD_CR = 2, 2 * OUTS, OUTS

        def sweep(eng, n_loop, first, body, last):
            for s in range(2):
                first(s)
                with eng.Fori(0, n_loop) as i:
                    for u in range(2):
                        body(s, i, u)
                last(s)

        @block.sync
        def _(sp):
            sp.dma_start(wrow[:], rows_bcast(w_row, D)).then_inc(w_in, 16)

            def load(s, i, u):
                for c in range(2):
                    sp.wait_ge(u_split, s * (2 * GROUPS) + i * 4 + (2 * u + c + 1))
                    sp.dma_start(uraw[:, c], one(up, i * 4 + (2 * u + c))).then_inc(u_in[c], 16)
                for c in range(2):
                    sp.wait_ge(v_split, s * (2 * GROUPS) + i * 4 + (2 * u + c + 1))
                    sp.dma_start(vraw[:, c], one(vp, i * 4 + (2 * u + c))).then_inc(v_in[c], 16)
                sp.wait_ge(a_ready, s * (2 * GROUPS) + i * 4 + 2 * u)
                sp.dma_start(gt[:, u], gates[bass.ds(s * (HALF // TB), HALF // TB), :, bass.ds(i * (4 * TB) + u * (2 * TB), 2 * TB)]
                             .rearrange("b p n -> p b n")).then_inc(g_in[u], 16)
            sweep(sp, GROUPS // 2, lambda s: None, load, lambda s: None)

        @block.gpsimd
        def _(pool):
            for s in range(2):
                for t in range(NTH):
                    if s:
                        pool.wait_ge(stored[t], 16)
                    pool.dma_start(acc[:, t], x2[s * HALF + t * P:s * HALF + (t + 1) * P, :]).then_inc(acc_in, 16)

        @block.tensor
        def _(pe):
            pe.sem_inc(h_done, 2)
            pe.sem_inc(out_done, OUT_CR)

            def hidden(s, i, o):
                for c in range(2):
                    n = s * (2 * GROUPS) + i * 4 + (2 * o + c)
                    pe.wait_ge(u_split, n + 3)
                    pe.wait_ge(gelu_done, n + 1)
                    for k in range(KD):
                        for m, (a, b) in enumerate(PRODUCTS):
                            for h in range(2):
                                mm = pe.matmul(hps[:, c, h, 0:SEG], uu[a][:, c, k * P:(k + 1) * P],
                                               hT[b][:, k, bass.ds(s * HALF + h * SEG, SEG)],
                                               start=(k + m == 0), stop=(k == KD - 1 and m == 2))
                    mm.then_inc(h_done, 1)

            def project(s, i, o):
                gb = o % 2
                n0 = s * (GROUPS * OUTS) + i * (2 * OUTS) + o * OUTS
                pe.wait_ge(a_ready, s * (2 * GROUPS) + i * 4 + (2 * o + 2 + A_CR))
                pe.wait_ge(v_split, s * (2 * GROUPS) + i * 4 + (2 * o + 2 + 2))
                for m in range(OUTS):
                    t, h = m // 2, m % 2
                    bank = (gb * OUTS + m) % BANKS
                    pe.wait_ge(added, n0 + (m + 1 - BANKS + ADD_CR))
                    for c in range(2):
                        for x, (a, b) in enumerate(PRODUCTS):
                            mm = pe.matmul(ops_[:, bank], aa[a][:, gb, c, t * P:(t + 1) * P],
                                           vv[b][:, gb, c, h * 512:(h + 1) * 512],
                                           start=(c + x == 0), stop=(c == 1 and x == 2))
                    mm.then_inc(out_done, 1)

            def body(s, i, u):
                hidden(s, i, u + 1)
                project(s, i, u)

            def last(s):
                hidden(s, GROUPS // 2 - 1, 1)
                project(s, GROUPS // 2 - 1, 0)
                project(s, GROUPS // 2 - 1, 1)
            sweep(pe, GROUPS // 2 - 1, lambda s: hidden(s, 0, 0), body, last)

        @block.scalar
        def _(act):
            act.sem_inc(gelu_done, 2)

            def u_part(s, i, o, c):
                act.wait_ge(u_in[c], s * (16 * GROUPS) + i * 32 + (16 * o + 16))
                act.wait_ge(h_done, s * (2 * GROUPS) + i * 4 + (2 * o + c + 1))
                act.activation(uu[0][:, c], uraw[:, c], ACT.Copy).then_inc(u_hi, 1)

            def group_0(s):
                for c in range(2):
                    u_part(s, 0, 0, c)
                v_parts(s, 0, 0)

            def v_parts(s, i, o):
                act.wait_ge(out_done, s * (GROUPS * OUTS) + i * (2 * OUTS) + (o + 1) * OUTS)
                for c in range(2):
                    act.wait_ge(v_in[c], s * (16 * GROUPS) + i * 32 + (16 * o + 16))
                    act.activation(vv[0][:, o % 2, c], vraw[:, c], ACT.Copy).then_inc(v_hi, 1)

            def gelu(s, i, o, c):
                n = s * (2 * GROUPS) + i * 4 + (2 * o + c)
                act.wait_ge(h_done, n + 3)
                act.wait_ge(a_ready, n + 1)
                act.activation(gl[:, c * HALF:(c + 1) * HALF].rearrange("p (h t) -> p h t", h=2),
                               hps[:, c, :, 0:SEG], ACT.Gelu).then_inc(gelu_done, 1)

            def step(s, i, o):
                for c in range(2):
                    gelu(s, i, o, c)
                    u_part(s, i, o + 1, c)
                v_parts(s, i, o + 1)

            def last(s):
                for c in range(2):
                    gelu(s, GROUPS // 2 - 1, 1, c)
                if s == 0:
                    group_0(1)
                for t in range(NTH):
                    act.wait_ge(added, (s + 1) * GROUPS * OUTS - OUTS + 2 * (t + 1) + ADD_CR)
                    act.wait_ge(squared, s * NTH + t + 1)
                    act.activation(gl[:, 0:D], acc[:, t, :], ACT.Square, accum_out=ssq[:, t:t + 1]).then_inc(squared, 1)
                act.wait_ge(var, s + 1)
                act.activation(ssq[:], ssq[:], ACT.Sqrt).then_inc(root, 1)
                for t in range(NTH):
                    act.wait_ge(normed, s * NTH + t + 1)
                    act.dma_start(out[s * HALF + t * P:s * HALF + (t + 1) * P, :], acc[:, t, :]).then_inc(stored[t], 16)
            group_0(0)
            act.sem_inc(squared, 1)
            sweep(act, GROUPS // 2 - 1, lambda s: step(s, 0, 0), lambda s, i, u: step(s, i, u + 1), last)
            for t in range(NTH):
                act.wait_ge(stored[t], 32)

        @block.vector
        def _(dve):
            own = Steps(dve, steps)
            dve.sem_inc(u_split, 2)
            dve.sem_inc(v_split, 2)
            dve.sem_inc(a_ready, A_CR)
            dve.sem_inc(added, ADD_CR)

            def u_part(s, i, o, c):
                dve.wait_ge(u_hi, s * (2 * GROUPS) + i * 4 + (2 * o + c + 1))
                dve.tensor_tensor(uu[1][:, c], uraw[:, c], uu[0][:, c].bitcast(F32), ALU.subtract
                                  ).then_inc(u_split, 1)

            def group_0(s):
                for c in range(2):
                    u_part(s, 0, 0, c)
                v_parts(s, 0, 0)

            def v_parts(s, i, o):
                for c in range(2):
                    dve.wait_ge(v_hi, s * (2 * GROUPS) + i * 4 + (2 * o + c + 1))
                    dve.tensor_tensor(vv[1][:, o % 2, c], vraw[:, c], vv[0][:, o % 2, c].bitcast(F32), ALU.subtract
                                      ).then_inc(v_split, 1)

            def gated(s, i, o, c):
                gb = o % 2
                dve.wait_ge(g_in[gb], s * (8 * GROUPS) + i * 16 + (16 * (o // 2) + 16))
                dve.wait_ge(out_done, s * (GROUPS * OUTS) + i * (2 * OUTS) + (o + 1) * OUTS)
                dve.wait_ge(gelu_done, s * (2 * GROUPS) + i * 4 + (2 * o + c + 3))
                g = gl[:, c * HALF:(c + 1) * HALF]
                by_block = g.rearrange("p (b t) -> p b t", t=TB)
                own.link(dve.tensor_tensor(by_block, by_block, gt[:, gb, :, c * TB:(c + 1) * TB], ALU.mult))
                own.link(dve.tensor_copy(aa[0][:, gb, c], g))
                dve.tensor_tensor(aa[1][:, gb, c], g, aa[0][:, gb, c].bitcast(F32), ALU.subtract
                                  ).then_inc(a_ready, 1)

            def adds(s, i, o, which=range(OUTS)):
                n0 = s * (GROUPS * OUTS) + i * (2 * OUTS) + o * OUTS
                for m in which:
                    t, h = m // 2, m % 2
                    dve.wait_ge(out_done, n0 + (m + 1 + OUT_CR))
                    dve.wait_ge(added, n0 + (m + 1))
                    part = acc[:, t, h * 512:(h + 1) * 512]
                    dve.tensor_tensor(part, part, ops_[:, ((o % 2) * OUTS + m) % BANKS], ALU.add).then_inc(added, 1)

            def step(s, i, o):
                gated(s, i, o, 0)
                u_part(s, i, o + 1, 0)
                gated(s, i, o, 1)
                adds(s, i, o - 1, range(2))
                u_part(s, i, o + 1, 1)
                adds(s, i, o - 1, range(2, OUTS))
                v_parts(s, i, o + 1)

            group_0(0)
            for s in range(2):
                for c in range(2):
                    gated(s, 0, 0, c)
                    u_part(s, 0, 1, c)
                v_parts(s, 0, 1)
                dve.wait_ge(acc_in, (s + 1) * 16 * NTH)
                dve.sem_inc(passed, 1)
                with dve.Fori(0, GROUPS // 2 - 1) as i:
                    own.enter(i, 8)
                    step(s, i, 1)
                    step(s, i, 2)
                own.leave(GROUPS // 2 - 1)
                for c in range(2):
                    gated(s, GROUPS // 2 - 1, 1, c)
                adds(s, GROUPS // 2 - 1, 0)
                if s == 0:
                    group_0(1)
                adds(s, GROUPS // 2 - 1, 1)
                dve.wait_ge(squared, s * NTH + (NTH + 1))
                dve.tensor_scalar(ssq[:], ssq[:], 1.0 / D, EPS, ALU.mult, ALU.add).then_inc(var, 1)
                dve.wait_ge(root, s + 1)
                own.link(dve.reciprocal(ssq[:], ssq[:]))
                dve.wait_ge(w_in, 16)
                for t in range(NTH):
                    dve.scalar_tensor_tensor(acc[:, t, :], acc[:, t, :], ssq[:, t:t + 1], wrow[:],
                                             ALU.mult, ALU.mult).then_inc(normed, 1)


def encoder_layer(nc, x, norm_mix, w_in, bias_tab, conv_w, conv_b, dt_bias, a_log, d_row, ssd_norm, w_out,
                  norm_ffn, w_query, keysT, up, vp, norm_final, consts, starts, iota, iota_t,
                  ident, out):
    projT = nc.dram_tensor("projT", [NB_IN, P, T], F32).ap()
    xbcT = nc.dram_tensor("xbcT", [8, P, T], F32).ap()
    mixT = nc.dram_tensor("mixT", [KD, P, T], F32).ap()
    x2 = nc.dram_tensor("x2", [T, D], F32).ap()
    gates = nc.dram_tensor("gates", [T // TB, P, P * TB], F32).ap()

    def parts_of(ctx, name):
        return [ctx.enter_context(nc.sbuf_tensor(f"{name}_{part}", [P, KD, T], F32R)) for part in ("hi", "lo")]

    with ExitStack() as ctx:
        hT = parts_of(ctx, "hm")
        norm_inputs(nc, x, norm_mix, ident, hT)
        project_in(nc, w_in, hT, conv_w, conv_b, projT, xbcT)
    attention(nc, projT, bias_tab, ident, mixT)
    ssd(nc, projT, xbcT, dt_bias, a_log, d_row, ssd_norm, consts, mixT)
    with ExitStack() as ctx:
        hT = parts_of(ctx, "hf")
        project_out(nc, mixT, w_out, x, norm_ffn, ident, x2, hT)
        with ExitStack() as tables:
            tabsT = [tables.enter_context(nc.sbuf_tensor(f"tabsT{n}", [P, T], F32 if n else BF16)) for n in range(3)]
            with ExitStack() as c:
                tabs = [c.enter_context(nc.sbuf_tensor(f"tabs{n}", [P, NT, P], F32)) for n in range(3)]
                retrieve(nc, hT, w_query, keysT, starts, tabs)
                turn_tables(nc, tabs, ident, tabsT)
            gate_table(nc, tabsT, iota, iota_t, gates)
        experts(nc, hT, up, vp, gates, x2, norm_final, out)


def _bias_layout(np, rpb):
    q, k = np.arange(GRID_W)[:, None], np.arange(GRID_W)[None]
    first = np.clip(q - 8, 0, GRID_W - 16)
    inside = (k >= first) & (k < first + 16)
    dc = np.clip(k - q, -15, 15) + 15
    tab = np.full((HEADS, P, 25, GRID_W), -1.0e30, np.float32)
    for half in range(2):
        for e in range(25):
            dr = (e if e < 16 else e - 13) - half
            if 0 <= dr <= 14 and (e, half) not in ((16, 1), (24, 0)):
                tab[:, 64 * half:64 * half + 64, e] = np.where(inside, rpb[:, dr][:, dc], np.float32(-1.0e30))
    return tab.reshape(HEADS, P, 25 * GRID_W)


def kernel(**inputs):
    import numpy as np
    import concourse.bacc as _bacc
    from concourse.bass_utils import run_bass_kernel_spmd as _run

    a = {k: np.asarray(v) for k, v in inputs.items()}
    w_in = np.zeros((D, NB_IN * P), np.float32)
    w_in[:, :a["w_in"].shape[2]] = a["w_in"][0]
    u, l = np.arange(P)[:, None], np.arange(P)[None]
    s = np.array(row_starts(), np.float32)
    arrays = {
        "x": np.concatenate([a["x_prompt"][0], a["x_sample"][0]], 0),
        "norm_mix": a["norm_mix_w"][0],
        "w_in": w_in.reshape(KD, P, NB_IN, P).transpose(2, 1, 0, 3).reshape(NB_IN, P, KD * P),
        "bias_tab": _bias_layout(np, a["rpb"][0]),
        "conv_w": a["conv_w"][0].reshape(CONV_TAPS, 8, P).transpose(2, 1, 0).reshape(P, 8 * CONV_TAPS),
        "conv_b": a["conv_b"][0].reshape(8, P).T,
        "dt_bias": a["dt_bias"][0].reshape(2 * HEADS),
        "a_log": a["a_log"][0].reshape(2 * HEADS),
        "d_row": np.repeat(a["d_skip"][0], HD),
        "ssd_norm": a["ssd_norm_w"][0],
        "w_out": a["w_out"][0].reshape(KD, P, D),
        "norm_ffn": a["norm_ffn_w"][0],
        "w_query": a["w_query"][0].reshape(KD, P, 2 * HEADS, P).transpose(2, 1, 0, 3).reshape(2 * HEADS, P, KD * P),
        "keysT": a["sub_keys"][0].reshape(2 * HEADS, NKEY, P).transpose(0, 2, 1),
        "up": a["expert_u"][0].reshape(NKEY, NKEY, KD, P).transpose(1, 3, 2, 0).reshape(NKEY, P, D),
        "vp": a["expert_v"][0].reshape(NKEY, NKEY, D).transpose(1, 0, 2),
        "norm_final": a["norm_final_w"],
        "consts": np.stack([u == l, u <= l, u > l, u >= l, u < l, u >= 0 * l], 1).astype(np.float32),
        "starts": np.concatenate([s, np.diff(s, prepend=0), np.arange(TOPK)]).astype(np.float32),
        "iota": np.tile(np.arange(P, dtype=np.float32), (P, 1)),
        "iota_t": np.tile(np.repeat(np.arange(P, dtype=np.float32), 16), (P, 1)),
        "ident": np.eye(P, dtype=np.float32),
    }
    nc = _bacc.Bacc("TRN2", target_bir_lowering=False, num_devices=1)
    feeds, args = {}, {}
    for name, v in arrays.items():
        v = np.ascontiguousarray(v)
        feeds[f"in_{name}"] = v
        args[name] = nc.dram_tensor(f"in_{name}", v.shape, mybir.dt.from_np(v.dtype), kind="ExternalInput").ap()
    args["out"] = nc.dram_tensor("out_y", (T, D), F32, kind="ExternalOutput").ap()
    encoder_layer(nc, **args)
    y = _run(nc, [feeds], core_ids=[0]).results[0]["out_y"]
    return y[None, :SEQ_P], y[None, SEQ_P:]
```

```python
from contextlib import ExitStack

import concourse.bass as bass
from concourse import mybir

ALU = mybir.AluOpType
ACT = mybir.ActivationFunctionType
AX = mybir.AxisListType
F32 = mybir.dt.float32
F32R = mybir.dt.float32r
BF16 = mybir.dt.bfloat16
U32 = mybir.dt.uint32

P = 128
D = 1024
KD = D // P
SEQ_P, SEQ_S = 256, 1024
T = SEQ_P + SEQ_S
NT = T // P
SEGS = [(0, 512), (512, 512), (1024, 256)]
EPS = 1e-6
GRID_W = 64
HEADS = 8
HD = 64
SSD_W = HEADS * HD
NB_IN = 25
BLK_Z, BLK_XBC, BLK_DT = 12, 16, 24
CONV_TAPS = 5
PAD_T = T + 6
CONV_T = T + 2
BIAS_GEN, BIAS_INT = 16 * GRID_W, 9 * GRID_W
TOPK = 16
NKEY = 128
LOWEST = -3.0e38
HALF = T // 2
NTH = HALF // P
TB = 64
PRODUCTS = [(0, 0), (1, 0), (0, 1)]


class Steps:

    def __init__(self, eng, sem):
        self.eng, self.sem, self.base, self.k, self.outer = eng, sem, 0, 0, []

    def enter(self, i, per):
        self.outer.append((self.base, self.k, per))
        self.base, self.k = i * per + self.base + self.k, 0

    def leave(self, n):
        base, k, per = self.outer.pop()
        assert self.k == per, (self.k, per)
        self.base, self.k = base, k + n * per

    def add(self, ins):
        self.k += 1
        ins.then_inc(self.sem, 1)

    def wait(self):
        self.eng.wait_ge(self.sem, self.base + self.k)

    def link(self, ins):
        self.add(ins)
        self.wait()


def scope(nc, ctx):
    sems = []

    def sb(name, shape, dt=F32):
        return ctx.enter_context(nc.sbuf_tensor(name, shape, dt))

    def ps(name, shape, dt=F32):
        return ctx.enter_context(nc.psum_tensor(name, shape, dt))

    def sem(name):
        sems.append(nc.alloc_semaphore(name))
        return sems[-1]

    def clear():
        if sems:
            nc.clear_and_free_semaphores(sems)
            nc.all_engine_barrier()

    ctx.callback(clear)
    return sb, ps, sem


def pair_of(sem, name):
    return [sem(name + "0"), sem(name + "1")]


def rounds(eng, n, step):
    with eng.Fori(0, n // 2) as i:
        for u in range(2):
            step(i, u)
    if n % 2:
        step(n // 2, 0)


def rows_bcast(dram, n, parts=P):
    return bass.AP(tensor=dram.tensor, offset=dram.offset, ap=[[0, parts], [1, n]])


def one(ap, r):
    return ap[bass.ds(r, 1)].rearrange("o p c -> p (o c)")


def norm_inputs(nc, x, w_row, ident, hT):
    with ExitStack() as ctx:
        sb, ps, sem = scope(nc, ctx)
        xall = sb("n1_x", [P, NT, D])
        junk = sb("n1_junk", [P, D])
        wrow = sb("n1_w", [P, D])
        idm = sb("n1_ident", [P, P])
        ssq = sb("n1_ssq", [P, NT])
        rstd = sb("n1_rstd", [P, NT])
        xs = sb("n1_xs", [P, 2, D])
        xT = ps("n1_xT", [P, 2, D])
        consts_in, x_in = sem("n1_consts_in"), [sem(f"n1_x_in{t}") for t in range(NT)]
        squared, var_ready, root_ready = sem("n1_squared"), sem("n1_var"), sem("n1_root")
        dve_steps, scaled, turned = sem("n1_dve"), sem("n1_scaled"), sem("n1_turned")
        hi_done, lo_done = sem("n1_hi"), sem("n1_lo")
        block = ctx.enter_context(nc.Block())

        @block.sync
        def _(sp):
            for t in range(NT):
                sp.dma_start(xall[:, t, :], x[t * P:(t + 1) * P, :]).then_inc(x_in[t], 16)
                if t == 0:
                    sp.dma_start(wrow[:], rows_bcast(w_row, D)).then_inc(consts_in, 16)
                    sp.dma_start(idm[:], ident).then_inc(consts_in, 16)

        @block.scalar
        def _(act):
            def squares(t):
                act.wait_ge(x_in[t], 16)
                if t:
                    act.wait_ge(squared, t)
                act.activation(junk[:], xall[:, t, :], ACT.Square, accum_out=ssq[:, t:t + 1]).then_inc(squared, 1)

            def root(t):
                act.wait_ge(var_ready, t + 1)
                act.activation(rstd[:, t:t + 1], ssq[:, t:t + 1], ACT.Sqrt).then_inc(root_ready, 1)

            def hi(t):
                act.wait_ge(turned, t + 1)
                act.activation(hT[0][:, :, t * P:(t + 1) * P], xT[:, t % 2].rearrange("p (k t) -> p k t", k=KD),
                               ACT.Copy).then_inc(hi_done, 1)

            squares(0)
            root(0)
            for t in range(NT):
                if t + 1 < NT:
                    squares(t + 1)
                    root(t + 1)
                hi(t)

        @block.vector
        def _(dve):
            own = Steps(dve, dve_steps)

            def variance(t):
                dve.wait_ge(squared, t + 1)
                dve.tensor_scalar(ssq[:, t:t + 1], ssq[:, t:t + 1], 1.0 / D, EPS, ALU.mult, ALU.add).then_inc(var_ready, 1)

            def scale(t):
                dve.wait_ge(root_ready, t + 1)
                own.link(dve.reciprocal(rstd[:, t:t + 1], rstd[:, t:t + 1]))
                dve.scalar_tensor_tensor(xs[:, t % 2], xall[:, t], rstd[:, t:t + 1], wrow[:],
                                         ALU.mult, ALU.mult).then_inc(scaled, 1)

            def lo(t):
                dve.wait_ge(hi_done, t + 1)
                tok = slice(t * P, (t + 1) * P)
                dve.tensor_tensor(hT[1][:, :, tok], xT[:, t % 2].rearrange("p (k t) -> p k t", k=KD),
                                  hT[0][:, :, tok].bitcast(F32), ALU.subtract).then_inc(lo_done, 1)

            dve.wait_ge(consts_in, 32)
            variance(0)
            scale(0)
            for t in range(NT):
                if t + 1 < NT:
                    variance(t + 1)
                    scale(t + 1)
                lo(t)

        @block.tensor
        def _(pe):
            pe.sem_inc(lo_done, 2)
            pe.wait_ge(consts_in, 32)
            with pe.Fori(0, NT // 2) as i:
                for u in range(2):
                    pe.wait_ge(scaled, i * 2 + (u + 1))
                    pe.wait_ge(lo_done, i * 2 + (u + 1))
                    for k in range(KD):
                        mm = pe.transpose(xT[:, u, k * P:(k + 1) * P], xs[:, u, k * P:(k + 1) * P], idm[:])
                    mm.then_inc(turned, 1)


def one_of(ap, r):
    return ap[:, bass.ds(r, 1), :].rearrange("p o d -> p (o d)")


def split(dve, own, hi, lo, raw):
    own.link(dve.tensor_copy(hi, raw))
    return dve.tensor_tensor(lo, raw, hi.bitcast(F32), ALU.subtract)


def project_in(nc, w_blocks, hT, conv_w, conv_b, projT, xbcT):
    PLAIN, CONV = BLK_XBC, 8
    with ExitStack() as ctx:
        sb, ps, sem = scope(nc, ctx)
        wraw = sb("pi_wraw", [P, 2, KD * P])
        w = [sb(f"pi_w_{part}", [P, 2, KD * P], F32R) for part in ("hi", "lo")]
        res = sb("pi_out", [P, 2, T])
        taps, bias = sb("pi_taps", [P, CONV * CONV_TAPS]), sb("pi_bias", [P, CONV])
        xp = sb("pi_x", [P, 2, PAD_T])
        y, z = sb("pi_y", [P, 2, CONV_T]), sb("pi_z", [P, 2, CONV_T])
        acc = ps("pi_acc", [P, 2, 3 * 512])
        w_in, consts_in = pair_of(sem, "pi_w_in"), sem("pi_consts_in")
        split_done, dve_steps = sem("pi_split"), sem("pi_dve")
        summed, copied, pads, convolved, squashed = (
            sem(f"pi_{n}") for n in ("summed", "copied", "pads", "conv", "silu"))
        stored, conv_stored = pair_of(sem, "pi_stored"), pair_of(sem, "pi_cstored")
        block = ctx.enter_context(nc.Block())

        @block.sync
        def _(sp):
            def load(r, u):
                sp.wait_ge(split_done, r * 2 + (u + 1))
                sp.dma_start(wraw[:, u], one(w_blocks, r * 2 + u)).then_inc(w_in[u], 16)
            sp.dma_start(taps[:], conv_w).then_inc(consts_in, 16)
            sp.dma_start(bias[:], conv_b).then_inc(consts_in, 16)
            rounds(sp, NB_IN, load)

        @block.vector
        def _(dve):
            own = Steps(dve, dve_steps)
            dve.sem_inc(split_done, 2)
            dve.memset(xp[:], 0.0).then_inc(pads, 1)

            def parts(r, u):
                dve.wait_ge(w_in[u], r * 16 + 16)
                dve.wait_ge(summed, r * 2 + (u + 1))
                split(dve, own, w[0][:, u], w[1][:, u], wraw[:, u]).then_inc(split_done, 1)

            def convolve(i, u):
                b = i * 2 + u
                dve.wait_ge(copied, b + (PLAIN + 3))
                dve.wait_ge(squashed, b + 1)
                tap = [taps[:, bass.ds(i * (2 * CONV_TAPS) + (u * CONV_TAPS + j), 1)] for j in range(CONV_TAPS)]
                own.link(dve.tensor_scalar(y[:, u], xp[:, u, 0:CONV_T], tap[0], None, ALU.mult))
                for j in range(1, CONV_TAPS):
                    ins = dve.scalar_tensor_tensor(y[:, u], xp[:, u, j:j + CONV_T], tap[j], y[:, u],
                                                   ALU.mult, ALU.add)
                    if j < CONV_TAPS - 1:
                        own.link(ins)
                    else:
                        ins.then_inc(convolved, 1)

            with dve.Fori(0, PLAIN // 2) as i:
                own.enter(i, 2)
                for u in range(2):
                    parts(i, u)
            own.leave(PLAIN // 2)
            parts(PLAIN // 2, 0)
            dve.wait_ge(consts_in, 32)
            dve.sem_inc(pads, 1)
            with dve.Fori(0, CONV // 2) as i:
                own.enter(i, 2 * CONV_TAPS)
                for u in range(2):
                    parts(i + (PLAIN // 2 + u), 1 - u)
                    convolve(i, u)
            own.leave(CONV // 2)

        @block.tensor
        def _(pe):
            pe.sem_inc(summed, 2)

            def block_products(r, u):
                pe.wait_ge(split_done, r * 2 + (u + 3))
                pe.wait_ge(copied, r * 2 + (u + 1))
                for k in range(KD):
                    for n, (a, b) in enumerate(PRODUCTS):
                        for t0, tn in SEGS:
                            mm = pe.matmul(acc[:, u, t0:t0 + tn], w[a][:, u, k * P:(k + 1) * P],
                                           hT[b][:, k, t0:t0 + tn], start=(k + n == 0),
                                           stop=(k == KD - 1 and n == 2))
                mm.then_inc(summed, 1)
            rounds(pe, NB_IN, block_products)

        @block.scalar
        def _(act):
            act.sem_inc(copied, 2)
            act.sem_inc(squashed, 2)
            for u in range(2):
                act.sem_inc(stored[u], 16)
                act.sem_inc(conv_stored[u], 32)

            def copy_out(r, u, turns):
                act.wait_ge(summed, r * 2 + (u + 3))
                act.wait_ge(stored[u], turns * 16 + 16)
                act.activation(res[:, u], acc[:, u, 0:T], ACT.Copy).then_inc(copied, 1)
                act.wait_ge(copied, r * 2 + (u + 3))
                act.dma_start(one(projT, r * 2 + u), res[:, u]).then_inc(stored[u], 16)

            with act.Fori(0, PLAIN // 2) as i:
                for u in range(2):
                    copy_out(i, u, i)
            act.wait_ge(pads, 2)
            with act.Fori(0, CONV // 2) as i:
                for u in range(2):
                    b = i * 2 + u
                    act.wait_ge(summed, b + (PLAIN + 3))
                    act.activation(xp[:, u, 2:2 + SEQ_P], acc[:, u, 0:SEQ_P], ACT.Copy)
                    act.activation(xp[:, u, 4 + SEQ_P:4 + T], acc[:, u, SEQ_P:T], ACT.Copy).then_inc(copied, 1)
                    act.wait_ge(convolved, b + 1)
                    act.wait_ge(conv_stored[u], i * 32 + 32)
                    act.activation(z[:, u], y[:, u], ACT.Silu, bias=bias[:, bass.ds(b, 1)]).then_inc(squashed, 1)
                    act.wait_ge(squashed, b + 3)
                    dst = one(xbcT, b)
                    act.dma_start(dst[:, 0:SEQ_P], z[:, u, 0:SEQ_P]).then_inc(conv_stored[u], 16)
                    act.dma_start(dst[:, SEQ_P:T], z[:, u, SEQ_P + 2:CONV_T]).then_inc(conv_stored[u], 16)
            copy_out(NB_IN // 2, 0, PLAIN // 2)
            act.wait_ge(stored[0], 16 * (2 + PLAIN // 2))
            act.wait_ge(stored[1], 16 * (1 + PLAIN // 2))
            for u in range(2):
                act.wait_ge(conv_stored[u], 32 * (1 + CONV // 2))


def attention_tiles():
    tiles = [(0, 0, 4 * GRID_W, 7 * GRID_W), (P, 0, 4 * GRID_W, 5 * GRID_W)]
    rows = SEQ_S // GRID_W
    for r in range(0, rows, 2):
        first = min(max(r - 4, 0), rows - 8)
        last = min(max(r + 1 - 4, 0), rows - 8) + 8
        col = BIAS_GEN if last - first == 9 else (first - r + 7) * GRID_W
        tiles.append((SEQ_P + r * GRID_W, SEQ_P + first * GRID_W, (last - first) * GRID_W, col))
    return tiles


def attention(nc, projT, bias_tab, ident, mixT):
    tiles = attention_tiles()
    NTI = len(tiles)
    KMAX = 640
    heads_in = projT.rearrange("b (h p) t -> (b h) p t", h=2)
    heads_out = mixT.rearrange("b (h p) t -> (b h) p t", h=2)
    with ExitStack() as ctx:
        sb, ps, sem = scope(nc, ctx)
        idm = sb("at_ident", [P, P])
        qraw, kraw = sb("at_qraw", [P, T]), sb("at_kraw", [P, T])
        q2, k2, klo = (sb(f"at_{n}", [P, 2, T], F32R) for n in ("q2", "k2", "klo"))
        vT = sb("at_vT", [HD, 2, T])
        bias = sb("at_bias", [P, 2, BIAS_GEN + BIAS_INT])
        v = sb("at_vtok", [P, 2, NT * HD])
        logits = sb("at_logits", [P, 2, KMAX])
        probs = sb("at_probs", [P, 2, KMAX])
        probsT = sb("at_probsT", [P, 2, KMAX])
        outT = sb("at_outT", [HD, 2, T])
        top, total, inv = sb("at_max", [P, 2]), sb("at_sum", [P, 2]), sb("at_inv", [P, 2])
        scores = ps("at_scores", [P, 2, 2, 512])
        turned = ps("at_turned", [P, 1024])
        oT = ps("at_oT", [P, 2, 512])
        ident_in, qk_in = sem("at_ident_in"), sem("at_qk_in")
        head_in, stored = pair_of(sem, "at_head_in"), pair_of(sem, "at_stored")
        hi_ready, lo_ready, qk_ready = sem("at_hi"), sem("at_lo"), sem("at_qk")
        v_turned, v_ready = sem("at_v_turned"), sem("at_v_ready")
        scored, biased = sem("at_scored"), sem("at_biased")
        max_ready, exp_ready, normed = sem("at_max_ready"), sem("at_exp"), sem("at_normed")
        p_turned, pT_ready = sem("at_p_turned"), sem("at_pT")
        weighed, o_ready = sem("at_weighed"), sem("at_o")
        dve_steps, passed = sem("at_dve"), sem("at_passed")
        block = ctx.enter_context(nc.Block())

        def cut(n):
            kn = tiles[n][2]
            return (2, kn // 2) if kn > 512 else (1, kn)

        def heads(eng, body):
            with eng.Fori(0, HEADS // 2 - 1) as i:
                for u in range(2):
                    body(i, u, False)
            body(HEADS // 2 - 1, 0, False)
            body(HEADS // 2 - 1, 1, True)

        def before(i, u):
            return i * (2 * NTI) + u * NTI

        def keyed(ap, n):
            pieces, w = cut(n)
            return ap.rearrange("p (c k) -> p c k", c=pieces)

        @block.sync
        def _(sp):
            sp.dma_start(idm[:], ident).then_inc(ident_in, 16)

            def load_qk(h):
                for half in (0, HD):
                    sp.dma_start(qraw[half:half + HD, :], one(heads_in, h)).then_inc(qk_in, 16)
                    sp.dma_start(kraw[half:half + HD, :], one(heads_in, h + HEADS)).then_inc(qk_in, 16)

            def body(i, u, last):
                sp.wait_ge(weighed, before(i, u) + NTI)
                sp.dma_start(vT[:, u], one(heads_in, i * 2 + (16 + u))).then_inc(head_in[u], 16)
                sp.dma_start(bias[:, u], one(bias_tab, i * 2 + u)).then_inc(head_in[u], 16)
                if not last:
                    sp.wait_ge(qk_ready, i * 2 + (u + 2))
                    load_qk(i * 2 + (u + 1))

            load_qk(0)
            heads(sp, body)

        @block.tensor
        def _(pe):
            pe.sem_inc(weighed, 2 * NTI)
            pe.wait_ge(ident_in, 16)

            def score(i, u, n):
                q0, k0, kn, _ = tiles[n]
                pe.wait_ge(biased, before(i, u) + (n + 1))
                pieces, w = cut(n)
                for c in range(pieces):
                    keys = slice(k0 + c * w, k0 + (c + 1) * w)
                    pe.matmul(scores[:, n % 2, c, 0:w], q2[:, u, q0:q0 + P], k2[:, u, keys],
                              start=True, stop=False)
                    mm = pe.matmul(scores[:, n % 2, c, 0:w], q2[0:HD, u, q0:q0 + P], klo[0:HD, u, keys],
                                   start=False, stop=True)
                mm.then_inc(scored, 1)

            def turn(i, u, n):
                kn = tiles[n][2]
                pe.wait_ge(normed, before(i, u) + (n + 1))
                if n == 0:
                    pe.wait_ge(v_ready, i * 2 + (u + 1))
                else:
                    pe.wait_ge(pT_ready, before(i, u) + (n + 1))
                for c in range(0, kn, P):
                    w = min(P, kn - c)
                    mm = pe.transpose(turned[0:w, c:c + P], probs[:, n % 2, c:c + w], idm[:])
                mm.then_inc(p_turned, 1)

            def weigh(i, u, n):
                q0, k0, kn, _ = tiles[n]
                pe.wait_ge(pT_ready, before(i, u) + (n + 2))
                pe.wait_ge(o_ready, before(i, u) + (n + 1))
                for c in range(0, kn, P):
                    w = min(P, kn - c)
                    vt = (k0 + c) // P
                    mm = pe.matmul(oT[0:HD, n % 2, 0:P], v[0:w, u, vt * HD:(vt + 1) * HD],
                                   probsT[0:w, n % 2, c:c + P], start=(c == 0), stop=(c + P >= kn))
                mm.then_inc(weighed, 1)

            def body(i, u, last):
                pe.wait_ge(head_in[u], i * 32 + 32)
                pe.wait_ge(pT_ready, before(i, u) + 1)
                pe.sem_inc(passed, 1)
                for t in range(NT):
                    mm = pe.transpose(turned[:, t * HD:(t + 1) * HD], vT[:, u, t * P:(t + 1) * P],
                                      idm[0:HD, 0:HD])
                mm.then_inc(v_turned, 1)
                for n in range(NTI):
                    if n + 2 < NTI:
                        score(i, u, n + 2)
                    elif not last:
                        if n + 2 == NTI:
                            pe.wait_ge(qk_ready, i * 2 + (u + 3))
                        score(i + u, 1 - u, n + 2 - NTI)
                    turn(i, u, n)
                    if n:
                        weigh(i, u, n - 1)
                weigh(i, u, NTI - 1)

            pe.wait_ge(qk_ready, 2)
            score(0, 0, 0)
            score(0, 0, 1)
            heads(pe, body)

        @block.gpsimd
        def _(pool):
            pool.sem_inc(qk_ready, 1)

            def lows(h, u):
                pool.wait_ge(hi_ready, h + 1)
                pool.tensor_tensor(q2[HD:P, u], qraw[HD:P, :], q2[HD:P, u].bitcast(F32), ALU.subtract
                                   ).then_inc(lo_ready, 1)
                pool.tensor_tensor(klo[0:HD, u], kraw[0:HD, :], k2[0:HD, u].bitcast(F32), ALU.subtract
                                   ).then_inc(lo_ready, 1)
                pool.wait_ge(lo_ready, h * 2 + 2)
                pool.sem_inc(qk_ready, 1)

            with pool.Fori(0, HEADS // 2) as i:
                for u in range(2):
                    lows(i * 2 + u, u)

        @block.vector
        def _(dve):
            own = Steps(dve, dve_steps)
            dve.sem_inc(biased, 2)
            dve.sem_inc(o_ready, 2)
            dve.sem_inc(stored[0], 16)
            dve.sem_inc(stored[1], 16)

            def bias_and_max(i, u, n):
                _, _, kn, col = tiles[n]
                pieces, w = cut(n)
                dve.wait_ge(scored, before(i, u) + (n + 1))
                dve.wait_ge(exp_ready, before(i, u) + (n + 1))
                if n == 0:
                    dve.wait_ge(head_in[u], i * 32 + 32)
                dve.scalar_tensor_tensor(keyed(logits[:, n % 2, 0:kn], n), scores[:, n % 2, 0:pieces, 0:w],
                                         HD ** -0.5, keyed(bias[:, u, col:col + kn], n),
                                         ALU.mult, ALU.add).then_inc(biased, 1)
                dve.wait_ge(biased, before(i, u) + (n + 3))
                dve.tensor_reduce(top[:, n % 2:n % 2 + 1], logits[:, n % 2, 0:kn], AX.X, ALU.max,
                                  negate=True).then_inc(max_ready, 1)

            def norm(i, u, n):
                _, _, kn, _ = tiles[n]
                dve.wait_ge(exp_ready, before(i, u) + (n + 3))
                own.link(dve.reciprocal(inv[:, n % 2:n % 2 + 1], total[:, n % 2:n % 2 + 1]))
                dve.tensor_scalar(probs[:, n % 2, 0:kn], probs[:, n % 2, 0:kn], inv[:, n % 2:n % 2 + 1],
                                  None, ALU.mult).then_inc(normed, 1)

            def take(i, u, n):
                q0 = tiles[n][0]
                dve.wait_ge(weighed, before(i, u) + (n + 1 + 2 * NTI))
                if n == 0:
                    dve.wait_ge(stored[u], i * 16 + 16)
                dve.tensor_copy(outT[:, u, q0:q0 + P], oT[0:HD, n % 2, 0:P]).then_inc(o_ready, 1)

            def ahead(step, i, u, n, last):
                if n < NTI:
                    step(i, u, n)
                elif not last:
                    step(i + u, 1 - u, n - NTI)

            def body(i, u, last):
                dve.wait_ge(v_turned, i * 2 + (u + 1))
                dve.tensor_copy(v[:, u], turned[:, 0:NT * HD]).then_inc(v_ready, 1)
                for n in range(NTI):
                    ahead(bias_and_max, i, u, n + 2, last)
                    ahead(norm, i, u, n + 1, last)
                    if n:
                        take(i, u, n - 1)
                take(i, u, NTI - 1)

            bias_and_max(0, 0, 0)
            bias_and_max(0, 0, 1)
            norm(0, 0, 0)
            with dve.Fori(0, HEADS // 2 - 1) as i:
                own.enter(i, 2 * NTI)
                for u in range(2):
                    body(i, u, False)
            own.leave(HEADS // 2 - 1)
            body(HEADS // 2 - 1, 0, False)
            body(HEADS // 2 - 1, 1, True)

        @block.scalar
        def _(act):
            act.sem_inc(exp_ready, 2)
            act.sem_inc(pT_ready, 1)

            def highs(h, u, done):
                act.wait_ge(qk_in, h * 64 + 64)
                act.wait_ge(weighed, done)
                act.activation(q2[:, u], qraw[:], ACT.Copy)
                act.activation(k2[:, u], kraw[:], ACT.Copy).then_inc(hi_ready, 1)

            def exp(i, u, n, first=False):
                kn = tiles[n][2]
                act.wait_ge(max_ready, before(i, u) + (n + 1))
                if not first:
                    act.wait_ge(p_turned, before(i, u) + (n - 1))
                act.activation(probs[:, n % 2, 0:kn], logits[:, n % 2, 0:kn], ACT.Exp,
                               bias=top[:, n % 2:n % 2 + 1], accum_out=total[:, n % 2:n % 2 + 1]
                               ).then_inc(exp_ready, 1)

            def copy_turned(i, u, n):
                kn = tiles[n][2]
                full = kn // P * P
                act.wait_ge(p_turned, before(i, u) + (n + 1))
                act.wait_ge(o_ready, before(i, u) + (n + 1))
                ins = act.activation(probsT[:, n % 2, 0:full], turned[:, 0:full], ACT.Copy)
                if kn > full:
                    ins = act.activation(probsT[0:kn - full, n % 2, full:full + P],
                                         turned[0:kn - full, full:full + P], ACT.Copy)
                ins.then_inc(pT_ready, 1)

            def body(i, u, last):
                for n in range(NTI):
                    copy_turned(i, u, n)
                    if n + 2 < NTI:
                        exp(i, u, n + 2)
                    elif not last:
                        exp(i + u, 1 - u, n + 2 - NTI)
                    if n == 3 and not last:
                        highs(i * 2 + (u + 1), 1 - u, i * (2 * NTI) + (u + 2) * NTI)
                act.wait_ge(o_ready, before(i, u) + (NTI + 2))
                act.dma_start(one(heads_out, i * 2 + u), outT[:, u]).then_inc(stored[u], 16)

            highs(0, 0, NTI)
            exp(0, 0, 0, True)
            exp(0, 0, 1, True)
            heads(act, body)
            for u in range(2):
                act.wait_ge(stored[u], 16 * (1 + HEADS // 2))


C_IDENT, C_LE, C_GT, C_GE, C_LT, C_ONES = range(6)
CHUNKS = [range(0, SEQ_P // P), range(SEQ_P // P, NT)]
HB = HEADS * NT
LOG1P_TERMS = 9


def ssd(nc, projT, xbcT, dt_bias, a_log, d_row, norm_row, consts, mixT):
    G = HEADS // 2
    with ExitStack() as ctx:
        sb, _, sem = scope(nc, ctx)
        cm = sb("sd_consts", [P, 6, P])
        xtok = sb("sd_x", [P, NT, SSD_W])
        zt = sb("sd_z", [P, NT, SSD_W])
        dt = sb("sd_dt", [P, NT, 2, HEADS])
        adt = sb("sd_adt", [P, NT, 2, HEADS])
        decay = sb("sd_decay", [P, 5, NT, 2, HEADS])
        wst = sb("sd_wst", [P, NT, 2, HEADS])
        entering = [sb(f"sd_ent{d}", [P, NT, SSD_W]) for d in range(2)]
        y = sb("sd_y", [P, NT, SSD_W])
        states = [sb("sd_st0", [P, NT, SSD_W]), y]
        ssq = sb("sd_ssq", [P, NT])
        nrow = sb("sd_nrow", [P, SSD_W])
        drow = sb("sd_drow", [P, SSD_W])

        with ExitStack() as c0:
            sb, ps, sem = scope(nc, c0)
            dtT = sb("s0_dtT", [HEADS, T])
            bias = sb("s0_bias", [P, 2, HEADS])
            alog = sb("s0_alog", [P, 2, HEADS])
            raw, u, t, t2, s = (sb(f"s0_{n}", [P, NT, 2, HEADS]) for n in ("raw", "u", "t", "t2", "s"))
            dps = ps("s0_dt", [P, NT, HEADS])
            cum = ps("s0_cum", [P, 2, 512])
            loaded, turned, steps = sem("s0_in"), sem("s0_turned"), sem("s0_dve")
            neg_ready, exped, adt_ready, summed, dec_ready, a_exp = (
                sem(f"s0_{n}") for n in ("neg", "exped", "adt", "summed", "dec", "aexp"))
            block = c0.enter_context(nc.Block())

            @block.sync
            def _(sp):
                sp.dma_start(cm[:], consts).then_inc(loaded, 16)
                sp.dma_start(dtT[:], projT[BLK_DT, 0:HEADS, :]).then_inc(loaded, 16)
                sp.dma_start(bias[:].rearrange("p d h -> p (d h)"), rows_bcast(dt_bias, 2 * HEADS)).then_inc(loaded, 16)
                sp.dma_start(alog[:].rearrange("p d h -> p (d h)"), rows_bcast(a_log, 2 * HEADS)).then_inc(loaded, 16)
                sp.dma_start(drow[:], rows_bcast(d_row, SSD_W)).then_inc(loaded, 16)
                sp.dma_start(nrow[:], rows_bcast(norm_row, SSD_W)).then_inc(loaded, 16)

            @block.tensor
            def _(pe):
                pe.wait_ge(loaded, 96)
                for c in range(NT):
                    mm = pe.transpose(dps[:, c], dtT[:, c * P:(c + 1) * P], cm[0:HEADS, C_IDENT, 0:HEADS])
                mm.then_inc(turned, 1)
                pe.wait_ge(adt_ready, 1)
                flat = adt[:].rearrange("p c d h -> p (c d h)")
                n = 2 * HB
                for m, mask in enumerate((C_LE, C_GT, C_GE, C_LT, C_ONES)):
                    mm = pe.matmul(cum[:, m // 3, (m % 3) * n:(m % 3 + 1) * n], cm[:, mask], flat, start=True, stop=True)
                mm.then_inc(summed, 1)

            @block.vector
            def _(dve):
                own = Steps(dve, steps)
                dve.wait_ge(turned, 1)
                for d in range(2):
                    ins = dve.tensor_tensor(raw[:, :, d], dps[:], bias[:, d].unsqueeze(1).to_broadcast([P, NT, HEADS]),
                                            ALU.add)
                    own.add(ins)
                own.wait()
                own.link(dve.tensor_scalar(t[:], raw[:], -1.0, None, ALU.mult))
                dve.tensor_tensor(u[:], raw[:], t[:], ALU.min).then_inc(neg_ready, 1)
                dve.wait_ge(exped, 1)
                own.link(dve.tensor_scalar(t[:], u[:], 2.0, None, ALU.add))
                own.link(dve.reciprocal(t2[:], t[:]))
                own.link(dve.tensor_tensor(t[:], u[:], t2[:], ALU.mult))
                own.link(dve.tensor_tensor(t2[:], t[:], t[:], ALU.mult))
                own.link(dve.tensor_scalar(s[:], t2[:], 1.0 / (2 * LOG1P_TERMS + 1), None, ALU.mult))
                for m in range(LOG1P_TERMS - 1, 0, -1):
                    own.link(dve.scalar_tensor_tensor(s[:], s[:], 1.0 / (2 * m + 1), t2[:], ALU.add, ALU.mult))
                own.link(dve.scalar_tensor_tensor(s[:], s[:], 1.0, t[:], ALU.add, ALU.mult))
                own.link(dve.tensor_scalar(raw[:], raw[:], 0.0, None, ALU.max))
                own.link(dve.scalar_tensor_tensor(dt[:], s[:], 2.0, raw[:], ALU.mult, ALU.add))
                dve.wait_ge(a_exp, 1)
                dve.scalar_tensor_tensor(adt[:].rearrange("p c d h -> p c (d h)"), dt[:].rearrange("p c d h -> p c (d h)"),
                                         -1.0, alog[:].rearrange("p d h -> p (d h)").unsqueeze(1).to_broadcast([P, NT, 2 * HEADS]),
                                         ALU.mult, ALU.mult).then_inc(adt_ready, 1)
                dve.wait_ge(dec_ready, 1)
                for d in range(2):
                    own.add(dve.tensor_tensor(wst[:, :, d], dt[:, :, d], decay[:, 1 + 2 * d, :, d], ALU.mult))
                own.wait()

            @block.scalar
            def _(act):
                act.wait_ge(loaded, 96)
                act.activation(alog[:], alog[:], ACT.Exp).then_inc(a_exp, 1)
                act.wait_ge(neg_ready, 1)
                act.activation(u[:], u[:], ACT.Exp).then_inc(exped, 1)
                act.wait_ge(summed, 1)
                flat = decay[:].rearrange("p m c d h -> p (m c d h)")
                act.activation(flat[:, 0:6 * HB], cum[:, 0, 0:6 * HB], ACT.Exp)
                act.activation(flat[:, 6 * HB:10 * HB], cum[:, 1, 0:4 * HB], ACT.Exp).then_inc(dec_ready, 1)

        with ExitStack() as c1:
            sb, ps, sem = scope(nc, c1)
            xb = sb("s1_xb", [P, 2, 6, P])
            zT = sb("s1_zT", [P, 2, 4, P])
            btok = sb("s1_b", [P, 2, 2 * P])
            xw = sb("s1_xw", [P, 2, 2, SSD_W])
            x_ps, z_ps, b_ps = ps("s1_xps", [P, SSD_W]), ps("s1_zps", [P, SSD_W]), ps("s1_bps", [P, 512])
            st_ps = ps("s1_st", [P, 2, SSD_W])
            loaded = pair_of(sem, "s1_in")
            turned, x_ready, xw_ready, b_ready, z_ready, st_done, st_out = (
                sem(f"s1_{n}") for n in ("turned", "x", "xw", "b", "z", "st", "stout"))
            block = c1.enter_context(nc.Block())

            @block.sync
            def _(sp):
                with sp.Fori(0, NT // 2) as i:
                    for u in range(2):
                        tok = bass.ds(i * (2 * P) + u * P, P)
                        sp.wait_ge(turned, i * 2 + (u + 1))
                        sp.dma_start(xb[:, u], xbcT[0:6, :, tok].rearrange("b p t -> p b t")).then_inc(loaded[u], 16)
                        sp.dma_start(zT[:, u], projT[BLK_Z:BLK_Z + 4, :, tok].rearrange("b p t -> p b t")
                                     ).then_inc(loaded[u], 16)

            @block.tensor
            def _(pe):
                pe.sem_inc(turned, 2)

                def turn(r, u):
                    pe.wait_ge(loaded[u], r * 32 + 32)
                    pe.wait_ge(x_ready, r * 2 + (u + 1))
                    pe.wait_ge(b_ready, r * 2 + (u + 1))
                    pe.wait_ge(z_ready, r * 2 + (u + 1))
                    for b in range(4):
                        pe.transpose(x_ps[:, b * P:(b + 1) * P], xb[:, u, b], cm[:, C_IDENT])
                        pe.transpose(z_ps[:, b * P:(b + 1) * P], zT[:, u, b], cm[:, C_IDENT])
                    for b in range(2):
                        mm = pe.transpose(b_ps[:, b * P:(b + 1) * P], xb[:, u, 4 + b], cm[:, C_IDENT])
                    mm.then_inc(turned, 1)

                def own_states(r, u):
                    pe.wait_ge(b_ready, r * 2 + (u + 2))
                    pe.wait_ge(xw_ready, r * 2 + (u + 1))
                    pe.wait_ge(st_out, r * 2 + (u + 1))
                    for d in range(2):
                        for g in range(2):
                            mm = pe.matmul(st_ps[:, d, g * 256:(g + 1) * 256], btok[:, u, g * P:(g + 1) * P],
                                           xw[:, u, d, g * 256:(g + 1) * 256], start=True, stop=True)
                    mm.then_inc(st_done, 1)

                turn(0, 0)
                with pe.Fori(0, NT // 2 - 1) as i:
                    for u in range(2):
                        turn(i + u, 1 - u)
                        own_states(i, u)
                turn(NT // 2 - 1, 1)
                own_states(NT // 2 - 1, 0)
                own_states(NT // 2 - 1, 1)

            @block.vector
            def _(dve):
                dve.sem_inc(x_ready, 1)
                with dve.Fori(0, NT // 2) as i:
                    for u in range(2):
                        c = i * 2 + u
                        dve.wait_ge(turned, i * 2 + (u + 3))
                        dve.tensor_copy(one_of(xtok, c), x_ps[:]).then_inc(x_ready, 1)
                        dve.wait_ge(x_ready, i * 2 + (u + 2))
                        dve.wait_ge(st_done, i * 2 + (u + 1))
                        for d in range(2):
                            ins = dve.tensor_tensor(
                                xw[:, u, d].rearrange("p (h c) -> p h c", h=HEADS),
                                one_of(xtok, c).rearrange("p (h c) -> p h c", h=HEADS),
                                wst[:, bass.ds(c, 1), d, :].rearrange("p o h -> p (o h)").unsqueeze(2).to_broadcast(
                                    [P, HEADS, HD]), ALU.mult)
                        ins.then_inc(xw_ready, 1)

            @block.scalar
            def _(act):
                act.sem_inc(b_ready, 1)
                act.sem_inc(z_ready, 1)
                act.sem_inc(st_out, 1)
                act.sem_inc(st_done, 2)

                def turned_out(r, u):
                    c = r * 2 + u
                    act.wait_ge(turned, c + 3)
                    act.wait_ge(st_done, c + 1)
                    act.activation(btok[:, u], b_ps[:, 0:2 * P], ACT.Copy).then_inc(b_ready, 1)
                    act.activation(one_of(zt, c), z_ps[:], ACT.Silu).then_inc(z_ready, 1)

                def states_out(r, u):
                    c = r * 2 + u
                    act.wait_ge(st_done, c + 3)
                    act.activation(one_of(states[0], c), st_ps[:, 0], ACT.Copy)
                    act.activation(one_of(states[1], c), st_ps[:, 1], ACT.Copy).then_inc(st_out, 1)

                turned_out(0, 0)
                with act.Fori(0, NT // 2 - 1) as i:
                    for u in range(2):
                        turned_out(i + u, 1 - u)
                        states_out(i, u)
                turned_out(NT // 2 - 1, 1)
                states_out(NT // 2 - 1, 0)
                states_out(NT // 2 - 1, 1)

        with ExitStack() as c2:
            sb, ps, sem = scope(nc, c2)
            steps = [sem("s2_dve"), sem("s2_pool")]
            block = c2.enter_context(nc.Block())
            LATE = 6

            def recur(eng, done, parts):
                def by_head(ap, h, n):
                    return ap[:, h * HD:(h + n) * HD].rearrange("p (h c) -> p h c", h=n)

                for seq in CHUNKS:
                    order = {0: list(seq), 1: list(seq)[::-1]}
                    for d, h, n in parts:
                        done.add(eng.memset(entering[d][:, order[d][0], h * HD:(h + n) * HD], 0.0))
                    for k in range(len(seq) - 1):
                        done.wait()
                        for d, h, n in parts:
                            c, nxt, e = order[d][k], order[d][k + 1], entering[d]
                            done.add(eng.tensor_tensor(by_head(e[:, nxt], h, n), by_head(e[:, c], h, n),
                                                       decay[:, 4, c, d, h:h + n].unsqueeze(2).to_broadcast([P, n, HD]),
                                                       ALU.mult))
                        done.wait()
                        for d, h, n in parts:
                            nxt = order[d][k + 1]
                            cols = slice(h * HD, (h + n) * HD)
                            done.add(eng.tensor_tensor(entering[d][:, nxt, cols], entering[d][:, nxt, cols],
                                                       states[d][:, nxt - 1 if d == 0 else nxt + 1, cols], ALU.add))

            @block.vector
            def _(dve):
                recur(dve, Steps(dve, steps[0]), [(0, 0, HEADS), (1, LATE, HEADS - LATE)])

            @block.gpsimd
            def _(pool):
                recur(pool, Steps(pool, steps[1]), [(1, 0, LATE)])

        with ExitStack() as c3:
            sb, ps, sem = scope(nc, c3)
            bcT = sb("s3_bcT", [P, 2, 4, P])
            seg = sb("s3_seg", [P, 2, 2, HEADS, P])
            xdt = sb("s3_xdt", [P, 2, SSD_W])
            m = sb("s3_m", [P, 2, 2 * 2 * G * P])
            cb = sb("s3_cb", [P, 2, 2, P])
            tmp, acc = sb("s3_tmp", [P, 2, SSD_W]), sb("s3_acc", [P, SSD_W])
            seg_ps = ps("s3_seg_ps", [P, 2 * HEADS * P])
            cb_ps, y_ps, off_ps = ps("s3_cb_ps", [P, 512]), ps("s3_y_ps", [P, SSD_W]), ps("s3_off_ps", [P, 2, SSD_W])
            loaded = pair_of(sem, "s3_in")
            seg_ready, seg_done, cb_done, cb_read, decayed, m_ready, y_done, gated = (
                sem(f"s3_{n}") for n in ("seg", "segdone", "cbdone", "cbread", "decayed", "m", "y", "gated"))
            steps, passed, passed_pool = sem("s3_dve"), sem("s3_passed"), sem("s3_passed_pool")
            off_done, xdt_ready, ps_read, seg_read = sem("s3_off_done"), sem("s3_xdt_ready"), sem("s3_ps_read"), sem("s3_seg_read")
            block = c3.enter_context(nc.Block())

            def row(ap, c, d):
                return ap[:, bass.ds(c, 1), d, :].rearrange("p o h -> p (o h)")

            @block.sync
            def _(sp):
                with sp.Fori(0, NT // 2) as i:
                    for u in range(2):
                        sp.wait_ge(off_done, i * 2 + (u + 1))
                        sp.dma_start(bcT[:, u], xbcT[4:8, :, bass.ds(i * (2 * P) + u * P, P)].rearrange("b p t -> p b t")
                                     ).then_inc(loaded[u], 16)

            @block.gpsimd
            def _(pool):
                with pool.Fori(0, NT // 2) as i:
                    for u in range(2):
                        pool.wait_ge(seg_done, i * 2 + (u + 1))
                        pool.sem_inc(passed_pool, 1)
                        for d, mask in enumerate((C_GT, C_LT)):
                            ins = pool.tensor_tensor(seg[:, u, d], cm[:, mask].unsqueeze(1).to_broadcast([P, HEADS, P]),
                                                     row(adt, i * 2 + u, d).unsqueeze(2).to_broadcast([P, HEADS, P]),
                                                     ALU.mult)
                        ins.then_inc(seg_ready, 1)

            @block.vector
            def _(dve):
                own = Steps(dve, steps)
                dve.sem_inc(gated, 1)
                dve.sem_inc(cb_read, 1)
                dve.sem_inc(m_ready, 1)

                hv = lambda ap: ap.rearrange("p (h c) -> p h c", h=HEADS)

                def masked(r, u):
                    c = r * 2 + u
                    dve.wait_ge(cb_done, c + 1)
                    dve.wait_ge(m_ready, c + 1)
                    for d, mask in enumerate((C_LE, C_GE)):
                        own.add(dve.tensor_tensor(cb[:, d], cb_ps[:, 0:2 * P].rearrange("p (g l) -> p g l", g=2),
                                                  cm[:, mask].unsqueeze(1).to_broadcast([P, 2, P]), ALU.mult))
                    own.wait()
                    dve.sem_inc(cb_read, 1)
                    dve.wait_ge(decayed, c + 1)
                    dg = m[:, u].rearrange("p (x h l) -> p x h l", x=4, h=G)
                    dve.tensor_tensor(dg, dg, cb[:].rearrange("p d g l -> p (d g) l").unsqueeze(2).to_broadcast(
                        [P, 4, G, P]), ALU.mult).then_inc(m_ready, 1)

                def weigh(r, u):
                    c = r * 2 + u
                    dve.wait_ge(y_done, c + 2)
                    for d in range(2):
                        ins = dve.tensor_tensor(hv(xdt[:, d]), hv(one_of(xtok, c)),
                                                row(dt, c, d).unsqueeze(2).to_broadcast([P, HEADS, HD]), ALU.mult)
                    ins.then_inc(xdt_ready, 1)

                def gather(r, u):
                    c = r * 2 + u
                    dec = lambda k, d: decay[:, k, bass.ds(c, 1), d, :].rearrange("p o h -> p (o h)").unsqueeze(
                        2).to_broadcast([P, HEADS, HD])
                    own.add(dve.tensor_tensor(tmp[:, 1], one_of(xtok, c), drow[:], ALU.mult))
                    dve.wait_ge(y_done, c + 3)
                    dve.wait_ge(gated, c + 1)
                    own.add(dve.tensor_tensor(hv(acc[:]), hv(off_ps[:, 0]), dec(0, 0), ALU.mult))
                    own.link(dve.tensor_tensor(hv(tmp[:, 0]), hv(off_ps[:, 1]), dec(2, 1), ALU.mult))
                    own.link(dve.tensor_tensor(acc[:], acc[:], tmp[:, 0], ALU.add))
                    own.link(dve.tensor_tensor(acc[:], acc[:], y_ps[:], ALU.add))
                    dve.sem_inc(ps_read, 1)
                    own.link(dve.tensor_tensor(acc[:], acc[:], tmp[:, 1], ALU.add))
                    dve.tensor_tensor(one_of(y, c), acc[:], one_of(zt, c), ALU.mult).then_inc(gated, 1)

                masked(0, 0)
                weigh(0, 0)

                with dve.Fori(0, NT // 2 - 1) as i:
                    own.enter(i, 2 * 8)
                    for u in range(2):
                        masked(i + u, 1 - u)
                        gather(i, u)
                        weigh(i + u, 1 - u)
                own.leave(NT // 2 - 1)
                masked(NT // 2 - 1, 1)
                gather(NT // 2 - 1, 0)
                weigh(NT // 2 - 1, 1)
                gather(NT // 2 - 1, 1)

            @block.tensor
            def _(pe):
                pe.sem_inc(seg_done, 2)
                pe.sem_inc(y_done, 2)
                pe.sem_inc(off_done, 2)

                def sums(r, u):
                    c = r * 2 + u
                    pe.wait_ge(loaded[u], r * 16 + 16)
                    pe.wait_ge(cb_read, c + 1)
                    for g in range(2):
                        mm = pe.matmul(cb_ps[:, g * P:(g + 1) * P], bcT[:, u, g], bcT[:, u, 2 + g],
                                       start=True, stop=True)
                    mm.then_inc(cb_done, 1)
                    pe.wait_ge(seg_ready, c + 1)
                    pe.wait_ge(seg_read, c + 1)
                    for d, mask in enumerate((C_LE, C_GE)):
                        for h in range(HEADS):
                            n = d * HEADS + h
                            mm = pe.matmul(seg_ps[:, n * P:(n + 1) * P], seg[:, u, d, h], cm[:, mask],
                                           start=True, stop=True)
                    mm.then_inc(seg_done, 1)

                def products(r, u):
                    c = r * 2 + u
                    pe.wait_ge(ps_read, c + 1)
                    pe.sem_inc(passed, 1)
                    for d in range(2):
                        for g in range(2):
                            mm = pe.matmul(off_ps[:, d, g * 256:(g + 1) * 256], bcT[:, u, 2 + g],
                                         one_of(entering[d], c)[:, g * 256:(g + 1) * 256], start=True, stop=True)
                    mm.then_inc(off_done, 1)
                    pe.wait_ge(m_ready, c + 2)
                    pe.wait_ge(xdt_ready, c + 1)
                    for h in range(HEADS):
                        for d in range(2):
                            x = (d * HEADS + h) * P
                            mm = pe.matmul(y_ps[:, h * HD:(h + 1) * HD], m[:, u, x:x + P],
                                           xdt[:, d, h * HD:(h + 1) * HD], start=(d == 0), stop=(d == 1))
                    mm.then_inc(y_done, 1)

                sums(0, 0)
                with pe.Fori(0, NT // 2 - 1) as i:
                    for u in range(2):
                        sums(i + u, 1 - u)
                        products(i, u)
                sums(NT // 2 - 1, 1)
                products(NT // 2 - 1, 0)
                products(NT // 2 - 1, 1)

            @block.scalar
            def _(act):
                act.sem_inc(seg_read, 1)
                act.sem_inc(ps_read, 1)
                with act.Fori(0, NT // 2) as i:
                    for u in range(2):
                        act.wait_ge(seg_done, i * 2 + (u + 3))
                        act.wait_ge(y_done, i * 2 + (u + 1))
                        act.activation(m[:, u], seg_ps[:], ACT.Exp).then_inc(decayed, 1)
                        act.wait_ge(decayed, i * 2 + (u + 1))
                        act.sem_inc(seg_read, 1)

        with ExitStack() as c4:
            sb, ps, sem = scope(nc, c4)
            junk = sb("s4_junk", [P, SSD_W])
            yn = sb("s4_yn", [P, 2, SSD_W])
            oT = sb("s4_oT", [P, 4, 4, P])
            t_ps = ps("s4_t", [P, 2, SSD_W])
            squared, root, var, normed, turned, copied, steps = (
                sem(f"s4_{n}") for n in ("sq", "root", "var", "normed", "turned", "copied", "dve"))
            stored = [sem(f"s4_stored{n}") for n in range(4)]
            block = c4.enter_context(nc.Block())

            @block.scalar
            def _(act):
                for c in range(NT):
                    if c:
                        act.wait_ge(squared, c)
                    act.activation(junk[:], y[:, c, :], ACT.Square, accum_out=ssq[:, c:c + 1]).then_inc(squared, 1)
                act.wait_ge(var, 1)
                act.activation(ssq[:], ssq[:], ACT.Sqrt).then_inc(root, 1)
                act.sem_inc(copied, 2)
                for c in range(NT):
                    act.wait_ge(turned, c + 3)
                    if c >= 4:
                        act.wait_ge(stored[c % 4], c // 4 * 16)
                    act.activation(oT[:, c % 4].rearrange("p b t -> p (b t)"), t_ps[:, c % 2], ACT.Copy).then_inc(copied, 1)
                    act.wait_ge(copied, c + 3)
                    act.dma_start(mixT[4:8, :, c * P:(c + 1) * P].rearrange("b p t -> p b t"), oT[:, c % 4]
                                  ).then_inc(stored[c % 4], 16)
                for n in range(4):
                    act.wait_ge(stored[n], len(range(n, NT, 4)) * 16)

            @block.vector
            def _(dve):
                own = Steps(dve, steps)
                dve.wait_ge(squared, NT)
                dve.tensor_scalar(ssq[:], ssq[:], 1.0 / SSD_W, EPS, ALU.mult, ALU.add).then_inc(var, 1)
                dve.wait_ge(root, 1)
                own.link(dve.reciprocal(ssq[:], ssq[:]))
                with dve.Fori(0, NT // 2) as i:
                    for u in range(2):
                        dve.wait_ge(turned, i * 2 + (u + 1))
                        dve.scalar_tensor_tensor(yn[:, u], one_of(y, i * 2 + u), ssq[:, bass.ds(i * 2 + u, 1)], nrow[:],
                                                 ALU.mult, ALU.mult).then_inc(normed, 1)

            @block.tensor
            def _(pe):
                pe.sem_inc(turned, 2)
                with pe.Fori(0, NT // 2) as i:
                    for u in range(2):
                        pe.wait_ge(normed, i * 2 + (u + 1))
                        pe.wait_ge(copied, i * 2 + (u + 1))
                        for b in range(4):
                            mm = pe.transpose(t_ps[:, u, b * P:(b + 1) * P], yn[:, u, b * P:(b + 1) * P], cm[:, C_IDENT])
                        mm.then_inc(turned, 1)


def project_out(nc, mixT, w_out, x, w_row, ident, x2, hT):
    with ExitStack() as ctx:
        sb, ps, sem = scope(nc, ctx)
        idm, wrow = sb("po_ident", [P, P]), sb("po_wrow", [P, D])
        w = [sb(f"po_w_{part}", [P, KD, D], F32R) for part in ("hi", "lo")]
        wraw = sb("po_wraw", [P, 2, D])
        mraw = sb("po_mraw", [P, 2, KD * P])
        mx = [sb(f"po_m_{part}", [P, 2, KD * P], F32R) for part in ("hi", "lo")]
        xin, xo, xs = sb("po_x", [P, 2, D]), sb("po_x2", [P, 2, D]), sb("po_xs", [P, D])
        wraw = [wraw[:, 0], wraw[:, 1], xo[:, 0], xo[:, 1]]
        ssq, rstd = sb("po_ssq", [P, 2]), sb("po_rstd", [P, 2])
        acc, xT = ps("po_acc", [P, 2, D]), ps("po_xT", [P, 2, D])
        consts_in, w_in = sem("po_consts_in"), [sem(f"po_w_in{k}") for k in range(4)]
        m_in, stored = pair_of(sem, "po_m_in"), pair_of(sem, "po_stored")
        w_hi, w_split, m_split, summed, added, squared, var, root, scaled, turned, hi_done, lo_done, steps = (
            sem(f"po_{n}") for n in ("w_hi", "w_split", "m_split", "summed", "added", "squared", "var", "root",
                                     "scaled", "turned", "hi", "lo", "dve"))
        block = ctx.enter_context(nc.Block())

        def tok(r, u):
            return bass.ds(r * (2 * P) + u * P, P)

        @block.sync
        def _(sp):
            def load(r, u):
                sp.wait_ge(m_split, r * 2 + (u + 1))
                sp.wait_ge(added, r * 2 + (u + 1))
                sp.dma_start(mraw[:, u].rearrange("p (k t) -> p k t", k=KD),
                             mixT[:, :, tok(r, u)].rearrange("b p t -> p b t")).then_inc(m_in[u], 16)
                sp.dma_start(xin[:, u], x[tok(r, u), :]).then_inc(m_in[u], 16)

            load(0, 0)
            for k in range(4):
                sp.dma_start(wraw[k], w_out[k]).then_inc(w_in[k], 16)
            for k in range(4, KD):
                sp.wait_ge(w_split, k - 3)
                sp.dma_start(wraw[k % 4], w_out[k]).then_inc(w_in[k % 4], 16)
            sp.dma_start(idm[:], ident).then_inc(consts_in, 16)
            sp.dma_start(wrow[:], rows_bcast(w_row, D)).then_inc(consts_in, 16)
            load(0, 1)
            with sp.Fori(0, NT // 2 - 1) as i:
                for u in range(2):
                    load(i + 1, u)

        @block.tensor
        def _(pe):
            pe.sem_inc(lo_done, 2)

            def products(r, u, first=False):
                pe.wait_ge(m_split, r * 2 + (u + 3))
                pe.wait_ge(added, r * 2 + (u + 1))
                for k in range(KD):
                    if first:
                        pe.wait_ge(w_split, k + 1)
                    for n, (a, b) in enumerate(PRODUCTS):
                        for h in range(2):
                            mm = pe.matmul(acc[:, u, h * 512:(h + 1) * 512], mx[a][:, u, k * P:(k + 1) * P],
                                           w[b][:, k, h * 512:(h + 1) * 512], start=(k + n == 0),
                                           stop=(k == KD - 1 and n == 2))
                mm.then_inc(summed, 1)

            def turn(r, u):
                pe.wait_ge(scaled, r * 2 + (u + 1))
                pe.wait_ge(lo_done, r * 2 + (u + 1))
                for k in range(KD):
                    mm = pe.transpose(xT[:, u, k * P:(k + 1) * P], xs[:, k * P:(k + 1) * P], idm[:])
                mm.then_inc(turned, 1)

            products(0, 0, True)
            pe.wait_ge(consts_in, 32)

            def step(r, u):
                products(r + u, 1 - u)
                turn(r, u)
            rounds(pe, NT - 1, step)
            turn(NT // 2 - 1, 1)

        @block.scalar
        def _(act):
            act.sem_inc(stored[0], 16)
            act.sem_inc(stored[1], 16)
            for k in range(KD):
                act.wait_ge(w_in[k % 4], 16 * (k // 4 + 1))
                act.activation(w[0][:, k], wraw[k % 4], ACT.Copy).then_inc(w_hi, 1)

            def stats(r, u):
                act.wait_ge(added, r * 2 + (u + 3))
                act.activation(xs[:], xo[:, u], ACT.Square, accum_out=ssq[:, u:u + 1]).then_inc(squared, 1)
                act.wait_ge(var, r * 2 + (u + 1))
                act.activation(rstd[:, u:u + 1], ssq[:, u:u + 1], ACT.Sqrt).then_inc(root, 1)
                act.dma_start(x2[tok(r, u), :], xo[:, u]).then_inc(stored[u], 16)

            def hi(r, u):
                act.wait_ge(turned, r * 2 + (u + 1))
                act.activation(hT[0][:, :, tok(r, u)], xT[:, u].rearrange("p (k t) -> p k t", k=KD), ACT.Copy
                               ).then_inc(hi_done, 1)

            def step(r, u):
                stats(r, u)
                hi(r, u)
            rounds(act, NT, step)
            for u in range(2):
                act.wait_ge(stored[u], 16 * (1 + NT // 2))

        @block.vector
        def _(dve):
            own = Steps(dve, steps)
            dve.sem_inc(m_split, 2)
            dve.sem_inc(added, 2)
            def parts(r, u):
                dve.wait_ge(m_in[u], r * 32 + 32)
                if not (isinstance(r, int) and r == 0):
                    dve.wait_ge(summed, r * 2 + (u - 1))
                split(dve, own, mx[0][:, u], mx[1][:, u], mraw[:, u]).then_inc(m_split, 1)

            def norm(r, u):
                dve.wait_ge(summed, r * 2 + (u + 1))
                dve.wait_ge(stored[u], r * 16 + 16)
                dve.tensor_tensor(xo[:, u], acc[:, u], xin[:, u], ALU.add).then_inc(added, 1)
                dve.wait_ge(squared, r * 2 + (u + 1))
                dve.tensor_scalar(ssq[:, u:u + 1], ssq[:, u:u + 1], 1.0 / D, EPS, ALU.mult, ALU.add).then_inc(var, 1)
                dve.wait_ge(root, r * 2 + (u + 1))
                own.link(dve.reciprocal(rstd[:, u:u + 1], rstd[:, u:u + 1]))
                dve.scalar_tensor_tensor(xs[:], xo[:, u], rstd[:, u:u + 1], wrow[:], ALU.mult, ALU.mult
                                         ).then_inc(scaled, 1)

            def lo(r, u):
                dve.wait_ge(hi_done, r * 2 + (u + 1))
                dve.tensor_tensor(hT[1][:, :, tok(r, u)], xT[:, u].rearrange("p (k t) -> p k t", k=KD),
                                  hT[0][:, :, tok(r, u)].bitcast(F32), ALU.subtract).then_inc(lo_done, 1)

            for k in range(KD):
                if k == 2:
                    parts(0, 0)
                dve.wait_ge(w_hi, k + 1)
                dve.tensor_tensor(w[1][:, k], wraw[k % 4], w[0][:, k].bitcast(F32), ALU.subtract).then_inc(w_split, 1)
            dve.wait_ge(consts_in, 32)
            parts(0, 1)
            with dve.Fori(0, NT // 2 - 1) as i:
                own.enter(i, 4)
                for u in range(2):
                    norm(i, u)
                    parts(i + 1, u)
                    lo(i, u)
            own.leave(NT // 2 - 1)
            for u in range(2):
                norm(NT // 2 - 1, u)
                lo(NT // 2 - 1, u)


RECTS = [(0, 1, 16), (1, 1, 8), (2, 2, 5), (4, 4, 3), (8, 8, 1)]
NCAND = sum(na * nb for _, na, nb in RECTS)


def row_starts():
    starts, at = [], 0
    for _, na, nb in RECTS:
        for _ in range(na):
            starts.append(at)
            at += nb
    return starts


def retrieve(nc, hT, w_query, keysT, starts, tabs):
    KZ = KD * P
    with ExitStack() as ctx:
        sb, ps, sem = scope(nc, ctx)
        wraw = sb("pk_wraw", [P, 2, KZ])
        w = [sb(f"pk_w_{part}", [P, 2, KZ], F32R) for part in ("hi", "lo")]
        keys = sb("pk_keys", [P, 2, P])
        qT = sb("pk_qT", [P, 2, T])
        s = sb("pk_s", [P, 2, NT, NKEY])
        rest = sb("pk_rest", [P, 2, NT, NKEY])
        sv = sb("pk_sv", [P, 2, NT, TOPK])
        si = sb("pk_si", [P, 2, NT, TOPK], U32)
        sif = sb("pk_sif", [P, 2, NT, TOPK], BF16)
        dif = sb("pk_dif", [P, NT, TOPK], BF16)
        cand = sb("pk_cand", [P, NT, NCAND])
        crest = sb("pk_crest", [P, NT, NCAND])
        cv = sb("pk_cv", [P, NT, TOPK])
        ci = sb("pk_ci", [P, NT, TOPK], U32)
        cf = sb("pk_cf", [P, NT, TOPK], BF16)
        small, wide = ([sb(f"pk_{name}{n}", [P, NT * TOPK, n], BF16 if name == "small" or n == 8 else F32)
                        for n in (8, 4, 2, 1)] for name in ("small", "wide"))
        hot = sb("pk_hot", [P, NT, TOPK, TOPK], BF16)
        prod = sb("pk_prod", [P, 2, NT, TOPK, TOPK], BF16)
        st = sb("pk_starts", [P, 3, TOPK])
        stb = sb("pk_starts_b", [P, 3, TOPK], BF16)
        den = sb("pk_den", [P, NT])
        acc = ps("pk_acc", [P, 2, 3 * 512])
        consts_in, w_in, keys_in = sem("pk_consts_in"), pair_of(sem, "pk_w_in"), sem("pk_keys_in")
        w_hi, w_split, summed, q_ready, scored, s_ready, s_read, exp_in, exp_out, steps, passed = (
            sem(f"pk_{n}") for n in ("w_hi", "w_split", "summed", "q", "scored", "s", "s_read", "exp_in", "exp_out",
                                     "dve", "passed"))
        hot_ready, bases_ready, seconds_ready = (sem(f"pk_{n}") for n in ("hot_ready", "bases", "seconds"))
        block = ctx.enter_context(nc.Block())

        def per_k(n):
            return stb[:, n].unsqueeze(1).to_broadcast([P, NT * TOPK, TOPK])

        def look_up_bases(eng):
            eng.tensor_tensor(prod[:, 0], hot[:], dif[:].unsqueeze(2).to_broadcast([P, NT, TOPK, TOPK]), ALU.mult
                              ).then_inc(bases_ready, 1)
            eng.tensor_tensor(prod[:, 1].rearrange("p t k a -> p (t k) a"), hot[:].rearrange("p t k a -> p (t k) a"),
                              per_k(1), ALU.mult).then_inc(bases_ready, 1)

        def look_up_seconds(eng):
            eng.tensor_tensor(prod[:, 0], hot[:], sif[:, 1].unsqueeze(2).to_broadcast([P, NT, TOPK, TOPK]), ALU.mult
                              ).then_inc(seconds_ready, 1)

        @block.sync
        def _(sp):
            sp.dma_start(st[:], rows_bcast(starts, 3 * TOPK)).then_inc(consts_in, 16)
            with sp.Fori(0, HEADS) as h:
                for z in range(2):
                    sp.wait_ge(w_split, h * 2 + (z + 1))
                    sp.dma_start(wraw[:, z], one(w_query, h * 2 + z)).then_inc(w_in[z], 16)
                sp.wait_ge(scored, h * 2 + 2)
                sp.dma_start(keys[:], keysT[bass.ds(h * 2, 2)].rearrange("z p n -> p z n")).then_inc(keys_in, 16)

        @block.tensor
        def _(pe):
            pe.sem_inc(scored, 2)
            pe.sem_inc(summed, 2)

            def project(h, z):
                pe.wait_ge(w_split, h * 2 + (z + 3))
                pe.wait_ge(s_ready, h * 2 + (z + 1))
                for k in range(KD):
                    for n, (a, b) in enumerate(PRODUCTS):
                        for t0, tn in SEGS:
                            mm = pe.matmul(acc[:, z, t0:t0 + tn], w[a][:, z, k * P:(k + 1) * P],
                                           hT[b][:, k, t0:t0 + tn], start=(k + n == 0),
                                           stop=(k == KD - 1 and n == 2))
                mm.then_inc(summed, 1)

            def score(h, z):
                pe.wait_ge(keys_in, h * 16 + 16)
                pe.wait_ge(q_ready, h * 2 + (z + 1))
                for t in range(NT):
                    mm = pe.matmul(acc[:, z, t * P:(t + 1) * P], qT[:, z, t * P:(t + 1) * P], keys[:, z],
                                   start=True, stop=True)
                mm.then_inc(scored, 1)

            for z in range(2):
                project(0, z)
                score(0, z)
            with pe.Fori(0, HEADS - 1) as h:
                for step in (project, score):
                    for z in range(2):
                        step(h + 1, z)

        @block.scalar
        def _(act):
            act.sem_inc(s_ready, 2)

            def hi(h, z):
                act.wait_ge(w_in[z], h * 16 + 16)
                act.wait_ge(summed, h * 2 + (z + 1))
                act.activation(w[0][:, z], wraw[:, z], ACT.Copy).then_inc(w_hi, 1)

            def q_out(h, z, more=True):
                act.wait_ge(summed, h * 2 + (z + 3))
                act.activation(qT[:, z], acc[:, z, 0:T], ACT.Copy).then_inc(q_ready, 1)
                if more:
                    hi(h + 1, z)

            def scores_out(h, z):
                act.wait_ge(scored, h * 2 + (z + 3))
                act.wait_ge(s_read, h + 1)
                act.activation(s[:, z].rearrange("p t n -> p (t n)"), acc[:, z, 0:T], ACT.Copy).then_inc(s_ready, 1)

            def exps(h):
                act.wait_ge(exp_in, h + 1)
                act.activation(cv[:], cv[:], ACT.Exp).then_inc(exp_out, 1)

            for z in range(2):
                hi(0, z)
            for z in range(2):
                q_out(0, z)
                scores_out(0, z)

            def head(h, more):
                for z in range(2):
                    q_out(h, z, more)
                for z in range(2):
                    scores_out(h, z)
                exps(h - 1)

            with act.Fori(0, HEADS - 2) as h:
                head(h + 1, True)
            head(HEADS - 1, False)
            exps(HEADS - 1)

        @block.gpsimd
        def _(pool):
            pool.sem_inc(w_split, 2)

            def lo(h, z):
                pool.wait_ge(w_hi, h * 2 + (z + 1))
                pool.tensor_tensor(w[1][:, z], wraw[:, z], w[0][:, z].bitcast(F32), ALU.subtract).then_inc(w_split, 1)

            def bases(h):
                pool.wait_ge(hot_ready, h * 2 + 1)
                look_up_bases(pool)

            def seconds(h):
                pool.wait_ge(hot_ready, h * 2 + 2)
                look_up_seconds(pool)

            for h in range(2):
                for z in range(2):
                    lo(h, z)
            with pool.Fori(0, HEADS - 2) as h:
                lo(h + 2, 0)
                bases(h)
                lo(h + 2, 1)
                seconds(h)
            bases(HEADS - 2)
            seconds(HEADS - 2)

        @block.vector
        def _(dve):
            own = Steps(dve, steps)
            dve.sem_inc(s_read, 1)

            def over(items):
                for ins in items:
                    own.add(ins)
                own.wait()
                dve.sem_inc(passed, 1)

            def each(f):
                over(f(z, t) for z in range(2) for t in range(NT))

            def top_of_keys(h):
                for z in range(2):
                    dve.wait_ge(s_ready, h * 2 + (z + 3))
                    dve.sem_inc(passed, 1)
                    for t in range(NT):
                        own.add(dve.max(sv[:, z, t, 0:8], s[:, z, t]))
                own.wait()
                dve.sem_inc(passed, 1)
                for z in range(2):
                    for t in range(NT):
                        own.add(dve.max_index(si[:, z, t, 0:8], sv[:, z, t, 0:8], s[:, z, t]))
                each(lambda z, t: dve.match_replace(rest[:, z, t], sv[:, z, t, 0:8], s[:, z, t], LOWEST))
                dve.sem_inc(s_read, 1)
                each(lambda z, t: dve.max(sv[:, z, t, 8:16], rest[:, z, t]))
                each(lambda z, t: dve.max_index(si[:, z, t, 8:16], sv[:, z, t, 8:16], rest[:, z, t]))

            def top_of_sums(h):
                at, made = 0, []
                for a0, na, nb in RECTS:
                    made.append(dve.tensor_tensor(
                        cand[:, :, at:at + na * nb].rearrange("p t (a b) -> p t a b", a=na),
                        sv[:, 0, :, a0:a0 + na].unsqueeze(3).to_broadcast([P, NT, na, nb]),
                        sv[:, 1, :, 0:nb].unsqueeze(2).to_broadcast([P, NT, na, nb]), ALU.add))
                    own.add(made[-1])
                    at += na * nb
                own.wait()
                dve.sem_inc(passed, 1)
                over(dve.max(cv[:, t, 0:8], cand[:, t]) for t in range(NT))
                for t in range(NT):
                    own.add(dve.max_index(ci[:, t, 0:8], cv[:, t, 0:8], cand[:, t]))
                over(dve.match_replace(crest[:, t], cv[:, t, 0:8], cand[:, t], LOWEST) for t in range(NT))
                over(dve.max(cv[:, t, 8:16], crest[:, t]) for t in range(NT))
                over(dve.max_index(ci[:, t, 8:16], cv[:, t, 8:16], crest[:, t]) for t in range(NT))

            def choose(compare, n):
                dve.tensor_tensor(hot[:].rearrange("p t k a -> p (t k) a"),
                                  cf[:].rearrange("p t k -> p (t k)").unsqueeze(2).to_broadcast([P, NT * TOPK, TOPK]),
                                  per_k(n), compare
                                  ).then_inc(hot_ready, 1)

            def places(h):
                own.add(dve.tensor_copy(sif[:], si[:]))
                own.add(dve.tensor_copy(cf[:], ci[:]))
                own.link(dve.tensor_copy(den[:], cv[:, :, 0:1].rearrange("p t o -> p (t o)")))
                own.add(dve.tensor_copy(dif[:, :, 0:1], sif[:, 0, :, 0:1]))
                own.link(dve.tensor_tensor(dif[:, :, 1:TOPK], sif[:, 0, :, 1:TOPK], sif[:, 0, :, 0:TOPK - 1], ALU.subtract))
                choose(ALU.is_ge, 0)
                dve.tensor_tensor(cv[:], cv[:], den[:].unsqueeze(2).to_broadcast([P, NT, TOPK]), ALU.subtract
                                  ).then_inc(exp_in, 1)

            def sums(n, tree):
                left = prod[:, n].rearrange("p t k a -> p (t k) a")
                for to in tree:
                    w = to.shape[2]
                    own.link(dve.tensor_tensor(to[:], left[:, :, 0:w], left[:, :, w:2 * w], ALU.add))
                    left = to
                return left[:].rearrange("p (t k) o -> p t (k o)", t=NT)

            def first_keys(h, alone=False):
                if alone:
                    dve.wait_ge(hot_ready, h * 2 + 1)
                    look_up_bases(dve)
                dve.wait_ge(bases_ready, h * 2 + 2)
                own.add(dve.tensor_copy(tabs[0][:, :, tabs_cols(h)], sums(0, wide)))
                own.link(dve.tensor_tensor(cf[:], cf[:], sums(1, small), ALU.subtract))
                choose(ALU.is_equal, 2)
                dve.wait_ge(exp_out, h + 1)
                own.link(dve.tensor_reduce(den[:], cv[:], AX.X, ALU.add))
                own.link(dve.reciprocal(den[:], den[:]))
                own.link(dve.tensor_tensor(tabs[2][:, :, tabs_cols(h)], cv[:],
                                           den[:].unsqueeze(2).to_broadcast([P, NT, TOPK]), ALU.mult))

            def second_keys(h, alone=False):
                if alone:
                    dve.wait_ge(hot_ready, h * 2 + 2)
                    look_up_seconds(dve)
                dve.wait_ge(seconds_ready, h + 1)
                own.link(dve.tensor_copy(tabs[1][:, :, tabs_cols(h)], sums(0, small)))

            def tabs_cols(h):
                return bass.ds(h * TOPK, TOPK)

            dve.wait_ge(consts_in, 16)
            own.link(dve.tensor_copy(stb[:], st[:]))
            top_of_keys(0)
            top_of_sums(0)
            places(0)
            with dve.Fori(0, HEADS - 1) as h:
                own.enter(h, 178)
                top_of_keys(h + 1)
                first_keys(h)
                top_of_sums(h + 1)
                second_keys(h)
                places(h + 1)
            own.leave(HEADS - 1)
            first_keys(HEADS - 1, True)
            second_keys(HEADS - 1, True)


def turn_tables(nc, tabs, ident, tabsT, iota, iota_t, io, io_t):
    with ExitStack() as ctx:
        sb, ps, sem = scope(nc, ctx)
        idm = sb("tt_ident", [P, P])
        io_raw = sb("tt_iota_raw", [P, io_t.shape[1]])
        tp = ps("tt_ps", [P, 2, 1024])
        loaded, turned, copied = sem("tt_in"), sem("tt_turned"), sem("tt_copied")
        iota_in, cast = sem("tt_iota_in"), sem("tt_cast")
        block = ctx.enter_context(nc.Block())
        steps = [(n, h) for n in range(3) for h in range(2)]

        @block.sync
        def _(sp):
            sp.dma_start(idm[:], ident).then_inc(loaded, 16)
            sp.dma_start(io_raw[:], iota_t).then_inc(iota_in, 16)
            sp.dma_start(io[:], iota).then_inc(iota_in, 16)

        @block.vector
        def _(dve):
            dve.wait_ge(iota_in, 32)
            dve.tensor_copy(io_t[:], io_raw[:]).then_inc(cast, 1)

        @block.tensor
        def _(pe):
            pe.wait_ge(loaded, 16)
            for m, (n, h) in enumerate(steps):
                if m > 1:
                    pe.wait_ge(copied, m - 1)
                for t in range(NT // 2):
                    mm = pe.transpose(tp[:, m % 2, t * P:(t + 1) * P], tabs[n][:, h * (NT // 2) + t], idm[:])
                mm.then_inc(turned, 1)

        @block.scalar
        def _(act):
            for m, (n, h) in enumerate(steps):
                act.wait_ge(turned, m + 1)
                act.activation(tabsT[n][:, h * HALF:(h + 1) * HALF], tp[:, m % 2, 0:HALF], ACT.Copy).then_inc(copied, 1)


def gate_table(nc, tabsT, io, io_t, gates):
    GROUP = io_t.shape[1] // P
    BY_POOL = 11
    PER = TB // GROUP
    BODY = 2 * PER
    QUADS = GROUP // 4
    with ExitStack() as ctx:
        sb, ps, sem = scope(nc, ctx)
        hot = sb("gt_hot", [P, 2, P * GROUP], BF16)
        left, right = (sb(f"gt_{n}", [P, 2, GROUP, P]) for n in ("left", "right"))
        stage = sb("gt_stage", [P, 2, P * TB])
        prod = ps("gt_prod", [P, 2 * QUADS, 512])
        hot_ready, right_ready, pool_done, act_done, quads_done, copied, passed = (
            sem(f"gt_{n}") for n in ("hot", "right", "pool", "act", "quads", "copied", "passed"))
        stored = pair_of(sem, "gt_stored")
        block = ctx.enter_context(nc.Block())
        N = T // TB

        @block.sync
        def _(sp):
            sp.sem_inc(stored[0], 16)
            sp.sem_inc(stored[1], 16)
            with sp.Fori(0, N // 2) as i:
                for u in range(2):
                    sp.wait_ge(copied, i * (BODY * QUADS) + ((u + 1) * PER * QUADS + 2 * QUADS))
                    sp.dma_start(one(gates, i * 2 + u), stage[:, u]).then_inc(stored[u], 16)
            for u in range(2):
                sp.wait_ge(stored[u], 16 * (1 + N // 2))

        def tokens(i, g):
            return bass.ds(i * (BODY * GROUP) + g * GROUP, GROUP)

        @block.vector
        def _(dve):
            with dve.Fori(0, N // 2) as i:
                for g in range(BODY):
                    n = i * BODY + (g + 1)
                    dve.wait_ge(pool_done, n)
                    dve.wait_ge(act_done, n)
                    dve.tensor_tensor(hot[:, g % 2].rearrange("p (i t) -> p i t", t=GROUP),
                                      io_t[:].rearrange("p (i t) -> p i t", t=GROUP),
                                      tabsT[0][:, tokens(i, g)].unsqueeze(1).to_broadcast([P, P, GROUP]),
                                      ALU.is_equal).then_inc(hot_ready, 1)
                    dve.wait_ge(quads_done, n * QUADS)
                    dve.tensor_tensor(right[:, g % 2], io[:].unsqueeze(1).to_broadcast([P, GROUP, P]),
                                      tabsT[1][:, tokens(i, g)].unsqueeze(2).to_broadcast([P, GROUP, P]),
                                      ALU.is_equal).then_inc(right_ready, 1)

        @block.gpsimd
        def _(pool):
            pool.sem_inc(pool_done, 2)
            with pool.Fori(0, N // 2) as i:
                for g in range(BODY):
                    n = i * BODY + (g + 1)
                    pool.wait_ge(hot_ready, n)
                    pool.wait_ge(quads_done, n * QUADS)
                    pool.sem_inc(passed, 1)
                    pool.tensor_tensor(left[:, g % 2, 0:BY_POOL],
                                       hot[:, g % 2].rearrange("p (i t) -> p t i", t=GROUP)[:, 0:BY_POOL],
                                       tabsT[2][:, bass.ds(i * (BODY * GROUP) + g * GROUP, BY_POOL)].unsqueeze(
                                           2).to_broadcast([P, BY_POOL, P]), ALU.mult).then_inc(pool_done, 1)

        @block.tensor
        def _(pe):
            pe.sem_inc(quads_done, 2 * QUADS)
            with pe.Fori(0, N // 2) as i:
                for g in range(BODY):
                    n = i * BODY + (g + 1)
                    pe.wait_ge(right_ready, n)
                    pe.wait_ge(pool_done, n + 2)
                    pe.wait_ge(act_done, n + 2)
                    for q in range(QUADS):
                        pe.wait_ge(copied, i * (BODY * QUADS) + (g * QUADS + q + 1))
                        for t in range(4 * q, 4 * q + 4):
                            mm = pe.matmul(prod[:, (g % 2) * QUADS + q, (t % 4) * P:(t % 4 + 1) * P],
                                           left[:, g % 2, t], right[:, g % 2, t], start=True, stop=True)
                        mm.then_inc(quads_done, 1)

        @block.scalar
        def _(act):
            act.sem_inc(copied, 2 * QUADS)
            act.sem_inc(act_done, 2)

            def weigh(i, g):
                act.wait_ge(hot_ready, i * BODY + (g + 1))
                act.wait_ge(quads_done, i * (BODY * QUADS) + (g + 1) * QUADS)
                by_token = hot[:, g % 2].rearrange("p (i t) -> p t i", t=GROUP)
                for t in range(BY_POOL, GROUP):
                    ins = act.activation(left[:, g % 2, t], by_token[:, t], ACT.Copy,
                                         scale=tabsT[2][:, bass.ds(i * (BODY * GROUP) + (g * GROUP + t), 1)])
                ins.then_inc(act_done, 1)

            def take(i, g):
                u = g // PER
                if g % PER == 0:
                    act.wait_ge(stored[u], i * 16 + 16)
                by_token = stage[:, u].rearrange("p (j t) -> p t j", t=TB)
                for q in range(QUADS):
                    t0 = (g % PER) * GROUP + 4 * q
                    act.wait_ge(quads_done, i * (BODY * QUADS) + ((g + 2) * QUADS + q + 1))
                    act.activation(by_token[:, t0:t0 + 4, :], prod[:, (g % 2) * QUADS + q].rearrange(
                        "p (t j) -> p t j", t=4), ACT.Copy).then_inc(copied, 1)

            weigh(0, 0)
            with act.Fori(0, N // 2 - 1) as i:
                for g in range(BODY):
                    weigh(i, g + 1)
                    take(i, g)
            for g in range(BODY):
                if g + 1 < BODY:
                    weigh(N // 2 - 1, g + 1)
                take(N // 2 - 1, g)


def experts(nc, hT, up, vp, gates, x2, w_row, out):
    GROUPS = NKEY // 2
    SEG = HALF // 2
    BANKS, OUTS = 4, 2 * NTH
    with ExitStack() as ctx:
        sb, ps, sem = scope(nc, ctx)
        acc = sb("ex_acc", [P, NTH, D])
        uraw, vraw = sb("ex_uraw", [P, 2, D]), sb("ex_vraw", [P, 2, D])
        uu = [sb(f"ex_u_{part}", [P, 2, D], F32R) for part in ("hi", "lo")]
        vv = [sb(f"ex_v_{part}", [P, 2, 2, D], F32R) for part in ("hi", "lo")]
        aa = [sb(f"ex_a_{part}", [P, 2, 2, HALF], F32R) for part in ("hi", "lo")]
        gt = sb("ex_gates", [P, 2, HALF // TB, 2 * TB])
        gl = sb("ex_gelu", [P, 2 * HALF])
        wrow = sb("ex_wrow", [P, D])
        ssq = sb("ex_ssq", [P, NTH])
        hps = ps("ex_h", [P, 2, 2, 512])
        ops_ = ps("ex_out", [P, BANKS, 512])
        u_in, v_in, g_in = pair_of(sem, "ex_u_in"), pair_of(sem, "ex_v_in"), pair_of(sem, "ex_g_in")
        acc_in, w_in, stored = sem("ex_acc_in"), sem("ex_w_in"), [sem(f"ex_stored{t}") for t in range(NTH)]
        u_hi, u_split, v_hi, v_split, h_done, gelu_done, a_ready, out_done, added, squared, var, root, normed, steps = (
            sem(f"ex_{n}") for n in ("u_hi", "u_split", "v_hi", "v_split", "h_done", "gelu", "a", "out_done", "added",
                                     "squared", "var", "root", "normed", "dve"))
        passed = sem("ex_passed")
        block = ctx.enter_context(nc.Block())
        A_CR, OUT_CR, ADD_CR = 3, 2 * OUTS, OUTS

        def sweep(eng, n_loop, first, body, last):
            for s in range(2):
                first(s)
                with eng.Fori(0, n_loop) as i:
                    for u in range(2):
                        body(s, i, u)
                last(s)

        @block.sync
        def _(sp):
            sp.dma_start(wrow[:], rows_bcast(w_row, D)).then_inc(w_in, 16)

            def load(s, i, u):
                for c in range(2):
                    sp.wait_ge(u_split, s * (2 * GROUPS) + i * 4 + (2 * u + c + 1))
                    sp.dma_start(uraw[:, c], one(up, i * 4 + (2 * u + c))).then_inc(u_in[c], 16)
                for c in range(2):
                    sp.wait_ge(v_split, s * (2 * GROUPS) + i * 4 + (2 * u + c + 1))
                    sp.dma_start(vraw[:, c], one(vp, i * 4 + (2 * u + c))).then_inc(v_in[c], 16)
                sp.wait_ge(a_ready, s * (2 * GROUPS) + i * 4 + (2 * u + 1))
                sp.dma_start(gt[:, u], gates[bass.ds(s * (HALF // TB), HALF // TB), :, bass.ds(i * (4 * TB) + u * (2 * TB), 2 * TB)]
                             .rearrange("b p n -> p b n")).then_inc(g_in[u], 16)
            sweep(sp, GROUPS // 2, lambda s: None, load, lambda s: None)

        @block.gpsimd
        def _(pool):
            for s in range(2):
                for t in range(NTH):
                    if s:
                        pool.wait_ge(stored[t], 16)
                    pool.dma_start(acc[:, t], x2[s * HALF + t * P:s * HALF + (t + 1) * P, :]).then_inc(acc_in, 16)

        @block.tensor
        def _(pe):
            pe.sem_inc(h_done, 2)
            pe.sem_inc(out_done, OUT_CR)

            def hidden(s, i, o):
                for c in range(2):
                    n = s * (2 * GROUPS) + i * 4 + (2 * o + c)
                    pe.wait_ge(u_split, n + 3)
                    pe.wait_ge(gelu_done, n + 1)
                    for k in range(KD):
                        for m, (a, b) in enumerate(PRODUCTS):
                            for h in range(2):
                                mm = pe.matmul(hps[:, c, h, 0:SEG], uu[a][:, c, k * P:(k + 1) * P],
                                               hT[b][:, k, bass.ds(s * HALF + h * SEG, SEG)],
                                               start=(k + m == 0), stop=(k == KD - 1 and m == 2))
                    mm.then_inc(h_done, 1)

            def project(s, i, o):
                gb = o % 2
                n0 = s * (GROUPS * OUTS) + i * (2 * OUTS) + o * OUTS
                pe.wait_ge(a_ready, s * (2 * GROUPS) + i * 4 + (2 * o + 2 + A_CR))
                pe.wait_ge(v_split, s * (2 * GROUPS) + i * 4 + (2 * o + 2 + 2))
                for m in range(OUTS):
                    t, h = m // 2, m % 2
                    bank = (gb * OUTS + m) % BANKS
                    pe.wait_ge(added, n0 + (m + 1 - BANKS + ADD_CR))
                    for c in range(2):
                        for x, (a, b) in enumerate(PRODUCTS):
                            mm = pe.matmul(ops_[:, bank], aa[a][:, gb, c, t * P:(t + 1) * P],
                                           vv[b][:, gb, c, h * 512:(h + 1) * 512],
                                           start=(c + x == 0), stop=(c == 1 and x == 2))
                    mm.then_inc(out_done, 1)

            def body(s, i, u):
                hidden(s, i, u + 1)
                project(s, i, u)

            def last(s):
                hidden(s, GROUPS // 2 - 1, 1)
                project(s, GROUPS // 2 - 1, 0)
                project(s, GROUPS // 2 - 1, 1)
            sweep(pe, GROUPS // 2 - 1, lambda s: hidden(s, 0, 0), body, last)

        @block.scalar
        def _(act):
            act.sem_inc(gelu_done, 2)

            def u_part(s, i, o, c):
                act.wait_ge(u_in[c], s * (16 * GROUPS) + i * 32 + (16 * o + 16))
                act.wait_ge(h_done, s * (2 * GROUPS) + i * 4 + (2 * o + c + 1))
                act.activation(uu[0][:, c], uraw[:, c], ACT.Copy).then_inc(u_hi, 1)

            def group_0(s):
                for c in range(2):
                    u_part(s, 0, 0, c)
                v_parts(s, 0, 0)

            def v_parts(s, i, o):
                act.wait_ge(out_done, s * (GROUPS * OUTS) + i * (2 * OUTS) + (o + 1) * OUTS)
                for c in range(2):
                    act.wait_ge(v_in[c], s * (16 * GROUPS) + i * 32 + (16 * o + 16))
                    act.activation(vv[0][:, o % 2, c], vraw[:, c], ACT.Copy).then_inc(v_hi, 1)

            def gelu(s, i, o, c):
                n = s * (2 * GROUPS) + i * 4 + (2 * o + c)
                act.wait_ge(h_done, n + 3)
                act.wait_ge(a_ready, n + 2)
                act.activation(gl[:, c * HALF:(c + 1) * HALF].rearrange("p (h t) -> p h t", h=2),
                               hps[:, c, :, 0:SEG], ACT.Gelu).then_inc(gelu_done, 1)

            def step(s, i, o):
                for c in range(2):
                    gelu(s, i, o, c)
                    u_part(s, i, o + 1, c)
                v_parts(s, i, o + 1)

            def last(s):
                for c in range(2):
                    gelu(s, GROUPS // 2 - 1, 1, c)
                if s == 0:
                    group_0(1)
                for t in range(NTH):
                    act.wait_ge(added, (s + 1) * GROUPS * OUTS - OUTS + 2 * (t + 1) + ADD_CR)
                    act.wait_ge(squared, s * NTH + t + 1)
                    act.activation(gl[:, 0:D], acc[:, t, :], ACT.Square, accum_out=ssq[:, t:t + 1]).then_inc(squared, 1)
                act.wait_ge(var, s + 1)
                act.activation(ssq[:], ssq[:], ACT.Sqrt).then_inc(root, 1)
                for t in range(NTH):
                    act.wait_ge(normed, s * NTH + t + 1)
                    act.dma_start(out[s * HALF + t * P:s * HALF + (t + 1) * P, :], acc[:, t, :]).then_inc(stored[t], 16)
            group_0(0)
            act.sem_inc(squared, 1)
            sweep(act, GROUPS // 2 - 1, lambda s: step(s, 0, 0), lambda s, i, u: step(s, i, u + 1), last)
            for t in range(NTH):
                act.wait_ge(stored[t], 32)

        @block.vector
        def _(dve):
            own = Steps(dve, steps)
            dve.sem_inc(u_split, 2)
            dve.sem_inc(v_split, 2)
            dve.sem_inc(a_ready, A_CR)
            dve.sem_inc(added, ADD_CR)

            def u_part(s, i, o, c):
                dve.wait_ge(u_hi, s * (2 * GROUPS) + i * 4 + (2 * o + c + 1))
                dve.tensor_tensor(uu[1][:, c], uraw[:, c], uu[0][:, c].bitcast(F32), ALU.subtract
                                  ).then_inc(u_split, 1)

            def group_0(s):
                for c in range(2):
                    u_part(s, 0, 0, c)
                v_parts(s, 0, 0)

            def v_parts(s, i, o):
                for c in range(2):
                    dve.wait_ge(v_hi, s * (2 * GROUPS) + i * 4 + (2 * o + c + 1))
                    dve.tensor_tensor(vv[1][:, o % 2, c], vraw[:, c], vv[0][:, o % 2, c].bitcast(F32), ALU.subtract
                                      ).then_inc(v_split, 1)

            def gated(s, i, o, c):
                gb = o % 2
                dve.wait_ge(g_in[gb], s * (8 * GROUPS) + i * 16 + (16 * (o // 2) + 16))
                dve.wait_ge(out_done, s * (GROUPS * OUTS) + i * (2 * OUTS) + (o + 1) * OUTS)
                dve.wait_ge(gelu_done, s * (2 * GROUPS) + i * 4 + (2 * o + c + 3))
                g = gl[:, c * HALF:(c + 1) * HALF]
                by_block = g.rearrange("p (b t) -> p b t", t=TB)
                own.link(dve.tensor_tensor(by_block, by_block, gt[:, gb, :, c * TB:(c + 1) * TB], ALU.mult))
                own.link(dve.tensor_copy(aa[0][:, gb, c], g))
                dve.tensor_tensor(aa[1][:, gb, c], g, aa[0][:, gb, c].bitcast(F32), ALU.subtract
                                  ).then_inc(a_ready, 1)

            def adds(s, i, o, which=range(OUTS)):
                n0 = s * (GROUPS * OUTS) + i * (2 * OUTS) + o * OUTS
                for m in which:
                    t, h = m // 2, m % 2
                    dve.wait_ge(out_done, n0 + (m + 1 + OUT_CR))
                    dve.wait_ge(added, n0 + (m + 1))
                    part = acc[:, t, h * 512:(h + 1) * 512]
                    dve.tensor_tensor(part, part, ops_[:, ((o % 2) * OUTS + m) % BANKS], ALU.add).then_inc(added, 1)

            def step(s, i, o):
                gated(s, i, o, 0)
                u_part(s, i, o + 1, 0)
                gated(s, i, o, 1)
                adds(s, i, o - 1, range(2))
                u_part(s, i, o + 1, 1)
                adds(s, i, o - 1, range(2, OUTS))
                v_parts(s, i, o + 1)

            group_0(0)
            for s in range(2):
                for c in range(2):
                    gated(s, 0, 0, c)
                    u_part(s, 0, 1, c)
                v_parts(s, 0, 1)
                dve.wait_ge(acc_in, (s + 1) * 16 * NTH)
                dve.sem_inc(passed, 1)
                with dve.Fori(0, GROUPS // 2 - 1) as i:
                    own.enter(i, 8)
                    step(s, i, 1)
                    step(s, i, 2)
                own.leave(GROUPS // 2 - 1)
                for c in range(2):
                    gated(s, GROUPS // 2 - 1, 1, c)
                adds(s, GROUPS // 2 - 1, 0)
                if s == 0:
                    group_0(1)
                adds(s, GROUPS // 2 - 1, 1)
                dve.wait_ge(squared, s * NTH + (NTH + 1))
                dve.tensor_scalar(ssq[:], ssq[:], 1.0 / D, EPS, ALU.mult, ALU.add).then_inc(var, 1)
                dve.wait_ge(root, s + 1)
                own.link(dve.reciprocal(ssq[:], ssq[:]))
                dve.wait_ge(w_in, 16)
                for t in range(NTH):
                    dve.scalar_tensor_tensor(acc[:, t, :], acc[:, t, :], ssq[:, t:t + 1], wrow[:],
                                             ALU.mult, ALU.mult).then_inc(normed, 1)


def encoder_layer(nc, x, norm_mix, w_in, bias_tab, conv_w, conv_b, dt_bias, a_log, d_row, ssd_norm, w_out,
                  norm_ffn, w_query, keysT, up, vp, norm_final, consts, starts, iota, iota_t,
                  ident, out):
    projT = nc.dram_tensor("projT", [NB_IN, P, T], F32).ap()
    xbcT = nc.dram_tensor("xbcT", [8, P, T], F32).ap()
    mixT = nc.dram_tensor("mixT", [KD, P, T], F32).ap()
    x2 = nc.dram_tensor("x2", [T, D], F32).ap()
    gates = nc.dram_tensor("gates", [T // TB, P, P * TB], F32).ap()

    def parts_of(ctx, name):
        return [ctx.enter_context(nc.sbuf_tensor(f"{name}_{part}", [P, KD, T], F32R)) for part in ("hi", "lo")]

    with ExitStack() as ctx:
        hT = parts_of(ctx, "hm")
        norm_inputs(nc, x, norm_mix, ident, hT)
        project_in(nc, w_in, hT, conv_w, conv_b, projT, xbcT)
    attention(nc, projT, bias_tab, ident, mixT)
    ssd(nc, projT, xbcT, dt_bias, a_log, d_row, ssd_norm, consts, mixT)
    with ExitStack() as ctx:
        hT = parts_of(ctx, "hf")
        project_out(nc, mixT, w_out, x, norm_ffn, ident, x2, hT)
        with ExitStack() as tables:
            tabsT = [tables.enter_context(nc.sbuf_tensor(f"tabsT{n}", [P, T], F32 if n else BF16)) for n in range(3)]
            io = tables.enter_context(nc.sbuf_tensor("iota", [P, P], F32))
            io_t = tables.enter_context(nc.sbuf_tensor("iota_t", [P, iota_t.shape[1]], BF16))
            with ExitStack() as c:
                tabs = [c.enter_context(nc.sbuf_tensor(f"tabs{n}", [P, NT, P], F32)) for n in range(3)]
                retrieve(nc, hT, w_query, keysT, starts, tabs)
                turn_tables(nc, tabs, ident, tabsT, iota, iota_t, io, io_t)
            gate_table(nc, tabsT, io, io_t, gates)
        experts(nc, hT, up, vp, gates, x2, norm_final, out)


def _bias_layout(np, rpb):
    q, k = np.arange(GRID_W)[:, None], np.arange(GRID_W)[None]
    first = np.clip(q - 8, 0, GRID_W - 16)
    inside = (k >= first) & (k < first + 16)
    dc = np.clip(k - q, -15, 15) + 15
    tab = np.full((HEADS, P, 25, GRID_W), -1.0e30, np.float32)
    for half in range(2):
        for e in range(25):
            dr = (e if e < 16 else e - 13) - half
            if 0 <= dr <= 14 and (e, half) not in ((16, 1), (24, 0)):
                tab[:, 64 * half:64 * half + 64, e] = np.where(inside, rpb[:, dr][:, dc], np.float32(-1.0e30))
    return tab.reshape(HEADS, P, 25 * GRID_W)


def kernel(**inputs):
    import numpy as np
    import concourse.bacc as _bacc
    from concourse.bass_utils import run_bass_kernel_spmd as _run

    a = {k: np.asarray(v) for k, v in inputs.items()}
    w_in = np.zeros((D, NB_IN * P), np.float32)
    w_in[:, :a["w_in"].shape[2]] = a["w_in"][0]
    u, l = np.arange(P)[:, None], np.arange(P)[None]
    s = np.array(row_starts(), np.float32)
    arrays = {
        "x": np.concatenate([a["x_prompt"][0], a["x_sample"][0]], 0),
        "norm_mix": a["norm_mix_w"][0],
        "w_in": w_in.reshape(KD, P, NB_IN, P).transpose(2, 1, 0, 3).reshape(NB_IN, P, KD * P),
        "bias_tab": _bias_layout(np, a["rpb"][0]),
        "conv_w": a["conv_w"][0].reshape(CONV_TAPS, 8, P).transpose(2, 1, 0).reshape(P, 8 * CONV_TAPS),
        "conv_b": a["conv_b"][0].reshape(8, P).T,
        "dt_bias": a["dt_bias"][0].reshape(2 * HEADS),
        "a_log": a["a_log"][0].reshape(2 * HEADS),
        "d_row": np.repeat(a["d_skip"][0], HD),
        "ssd_norm": a["ssd_norm_w"][0],
        "w_out": a["w_out"][0].reshape(KD, P, D),
        "norm_ffn": a["norm_ffn_w"][0],
        "w_query": a["w_query"][0].reshape(KD, P, 2 * HEADS, P).transpose(2, 1, 0, 3).reshape(2 * HEADS, P, KD * P),
        "keysT": a["sub_keys"][0].reshape(2 * HEADS, NKEY, P).transpose(0, 2, 1),
        "up": a["expert_u"][0].reshape(NKEY, NKEY, KD, P).transpose(1, 3, 2, 0).reshape(NKEY, P, D),
        "vp": a["expert_v"][0].reshape(NKEY, NKEY, D).transpose(1, 0, 2),
        "norm_final": a["norm_final_w"],
        "consts": np.stack([u == l, u <= l, u > l, u >= l, u < l, u >= 0 * l], 1).astype(np.float32),
        "starts": np.concatenate([s, np.diff(s, prepend=0), np.arange(TOPK)]).astype(np.float32),
        "iota": np.tile(np.arange(P, dtype=np.float32), (P, 1)),
        "iota_t": np.tile(np.repeat(np.arange(P, dtype=np.float32), 16), (P, 1)),
        "ident": np.eye(P, dtype=np.float32),
    }
    nc = _bacc.Bacc("TRN2", target_bir_lowering=False, num_devices=1)
    feeds, args = {}, {}
    for name, v in arrays.items():
        v = np.ascontiguousarray(v)
        feeds[f"in_{name}"] = v
        args[name] = nc.dram_tensor(f"in_{name}", v.shape, mybir.dt.from_np(v.dtype), kind="ExternalInput").ap()
    args["out"] = nc.dram_tensor("out_y", (T, D), F32, kind="ExternalOutput").ap()
    encoder_layer(nc, **args)
    y = _run(nc, [feeds], core_ids=[0]).results[0]["out_y"]
    return y[None, :SEQ_P], y[None, SEQ_P:]
```
